# Optimizing a Trainium2 kernel written in Bass

```python
import math
import jax, jax.numpy as jnp
from jax import lax
import numpy as np

D_MODEL = 1024
BATCH = 1
SEQ = 512
DEPTH = 2

N_EVEN = (DEPTH + 1) // 2
N_ODD = DEPTH // 2

RET_HEADS = 4
RET_DK = 128
RET_DV = 128
RET_CHUNK = 128
ROPE_THETA = 10000.0
DSA_HEADS = 8
DSA_DH = 64
IDX_HEADS = 8
IDX_DH = 32
DSA_TOPK_MAX = 256
Q_BLOCK = 128
REL_BUCKETS = 32
REL_MAX_DIST = 128
EVEN_COLS = (RET_HEADS * RET_DK, RET_HEADS * RET_DK, RET_HEADS * RET_DV, RET_HEADS * RET_DV,
             DSA_HEADS * DSA_DH, DSA_DH, DSA_DH, IDX_HEADS * IDX_DH, IDX_DH, IDX_HEADS)
EVEN_IN = sum(EVEN_COLS)
EVEN_SPLITS = [sum(EVEN_COLS[:i + 1]) for i in range(len(EVEN_COLS) - 1)]
MIX_OUT_EVEN = RET_HEADS * RET_DV + DSA_HEADS * DSA_DH
SSM_DINNER = 2 * D_MODEL
SSM_HEADDIM = 64
SSM_HEADS = SSM_DINNER // SSM_HEADDIM
SSM_GROUPS = 8
SSM_STATE = 128
SSM_CONV = 4
SSM_CHUNK = 128
CONV_DIM = SSM_DINNER + 2 * SSM_GROUPS * SSM_STATE
SSM_IN = SSM_DINNER + CONV_DIM + SSM_HEADS
N_EXPERTS = 64
TOPK = 8
D_EXPERT = 256
D_SHARED = 256
ROUTED_SCALE = 2.5
MOE_BLOCK = 128
EPS = 1e-6

kernel_name = 'hybrid_retention_dsa_ssd_moe'

def rmsnorm(x, g):
    x32 = x.astype(jnp.float32)
    y = x32 * lax.rsqrt(jnp.mean(x32 * x32, axis=-1, keepdims=True) + EPS)
    return (y * g.astype(jnp.float32)).astype(x.dtype)

def modulate(h, shift, scale):
    return h * (1.0 + scale[:, None, :]) + shift[:, None, :]

def rotary(x, pos):
    half = x.shape[-1] // 2
    inv = ROPE_THETA ** (-jnp.arange(half, dtype=jnp.float32) / half)
    ang = pos.astype(jnp.float32)[..., None] * inv
    cos = jnp.cos(ang)[:, :, None, :]
    sin = jnp.sin(ang)[:, :, None, :]
    x1, x2 = x[..., :half], x[..., half:]
    return jnp.concatenate([x1 * cos - x2 * sin, x1 * sin + x2 * cos], axis=-1).astype(x.dtype)

def t5_bucket(dist):
    n = jnp.maximum(dist, 0)
    max_exact = REL_BUCKETS // 2
    nf = jnp.maximum(n, 1).astype(jnp.float32)
    large = max_exact + (jnp.log(nf / max_exact) / math.log(REL_MAX_DIST / max_exact)
                         * (REL_BUCKETS - max_exact)).astype(jnp.int32)
    large = jnp.minimum(large, REL_BUCKETS - 1)
    return jnp.where(n < max_exact, n, large)

def retention(q, k, v, pos):
    B_, T, H, dk = q.shape
    dv = v.shape[-1]
    L = RET_CHUNK
    nC = T // L
    q = rotary(q, pos)
    k = rotary(k, pos) * dk ** -0.5
    log_g = jnp.log(1.0 - 2.0 ** (-5.0 - jnp.arange(H, dtype=jnp.float32)))
    idx = jnp.arange(L, dtype=jnp.float32)
    rel = idx[:, None] - idx[None, :]
    d_intra = jnp.where(rel >= 0, jnp.exp(log_g[:, None, None] * jnp.maximum(rel, 0.0)), 0.0)
    zeta = jnp.exp(log_g[:, None] * (L - 1 - idx))
    xi = jnp.exp(log_g[:, None] * (idx + 1))
    chunk_decay = jnp.exp(log_g * L)
    qc = q.reshape(B_, nC, L, H, dk)
    kc = k.reshape(B_, nC, L, H, dk)
    vc = v.reshape(B_, nC, L, H, dv)
    inner = jnp.einsum('bcnhd,bcmhd->bhcnm', qc, kc) * d_intra[:, None]
    y_intra = jnp.einsum('bhcnm,bcmhe->bcnhe', inner, vc)
    u = jnp.einsum('bcmhd,hm,bcmhe->cbhde', kc, zeta, vc)

    def step(r, u_c):
        return r * chunk_decay[:, None, None] + u_c, r

    _, r_prev = lax.scan(step, jnp.zeros_like(u[0]), u)
    y_cross = jnp.einsum('bcnhd,hn,cbhde->bcnhe', qc, xi, r_prev)
    return (y_intra + y_cross).reshape(B_, T, H, dv)

def dsa_attention(q, k, v, qi, ki, wi, pos, rel_bias, q_gain, k_gain):
    B_, T, H, dh = q.shape
    topk = min(DSA_TOPK_MAX, T // 4)
    nQ = T // Q_BLOCK
    q = rmsnorm(q, q_gain)
    k = rmsnorm(k, k_gain)
    wi = wi.astype(jnp.float32) * (IDX_HEADS ** -0.5 * IDX_DH ** -0.5)
    key_idx = jnp.arange(T, dtype=jnp.int32)

    def to_blocks(a):
        return a.reshape(B_, nQ, Q_BLOCK, *a.shape[2:]).swapaxes(0, 1)

    def gather_rows(table, sel):
        return jax.vmap(lambda tb, ib: tb[ib])(table, sel)

    def block(args):
        qb, qib, wib, posb, tb = args
        logit = jax.nn.relu(jnp.einsum('bqhd,bsd->bqhs', qib, ki).astype(jnp.float32))
        score = jnp.einsum('bqhs,bqh->bqs', logit, wib)
        causal = key_idx[None, None, :] <= tb[None, :, None]
        score = jnp.where(causal, score, -jnp.inf)
        _, sel = lax.top_k(score, topk)
        valid = sel <= tb[None, :, None]
        k_sel = gather_rows(k, sel)
        v_sel = gather_rows(v, sel)
        pos_sel = gather_rows(pos, sel)
        bias = rel_bias[t5_bucket(posb[:, :, None] - pos_sel)]
        logits = (jnp.einsum('bqhd,bqkd->bhqk', qb, k_sel).astype(jnp.float32) * dh ** -0.5
                  + jnp.moveaxis(bias, -1, 1).astype(jnp.float32))
        logits = jnp.where(valid[:, None], logits, -jnp.inf)
        p = jax.nn.softmax(logits, axis=-1).astype(v.dtype)
        return jnp.einsum('bhqk,bqkd->bqhd', p, v_sel)

    out = lax.map(block, (to_blocks(q), to_blocks(qi), to_blocks(wi), to_blocks(pos),
                          key_idx.reshape(nQ, Q_BLOCK)))
    return out.swapaxes(0, 1).reshape(B_, T, H, dh)

def even_mixer(h, pos, rel_bias, w_in, ret_norm_g, dsa_q_g, dsa_k_g, w_out):
    B_, T, _ = h.shape
    qr, kr, vr, gr, qa, ka, va, qi, ki, wi = jnp.split(h @ w_in, EVEN_SPLITS, axis=-1)
    y_ret = retention(qr.reshape(B_, T, RET_HEADS, RET_DK), kr.reshape(B_, T, RET_HEADS, RET_DK),
                      vr.reshape(B_, T, RET_HEADS, RET_DV), pos)
    y_ret = rmsnorm(y_ret, ret_norm_g).reshape(B_, T, RET_HEADS * RET_DV) * jax.nn.silu(gr)
    y_att = dsa_attention(qa.reshape(B_, T, DSA_HEADS, DSA_DH), ka, va,
                          qi.reshape(B_, T, IDX_HEADS, IDX_DH), ki, wi, pos, rel_bias, dsa_q_g, dsa_k_g)
    y = jnp.concatenate([y_ret.astype(h.dtype), y_att.reshape(B_, T, DSA_HEADS * DSA_DH).astype(h.dtype)], axis=-1)
    return y @ w_out

def ssd_scan(x, dt, A, Bm, Cm):
    B_, T, H, P = x.shape
    G, N = Bm.shape[2], Bm.shape[3]
    R = H // G
    L = SSM_CHUNK
    nC = T // L
    xc = x.reshape(B_, nC, L, G, R, P)
    dtc = dt.reshape(B_, nC, L, G, R)
    Bc = Bm.reshape(B_, nC, L, G, N)
    Cc = Cm.reshape(B_, nC, L, G, N)
    cs = jnp.cumsum(dtc * A.reshape(G, R), axis=2)
    causal = jnp.tril(jnp.ones((L, L), dtype=bool))
    seg = cs[:, :, :, None] - cs[:, :, None]
    decay = jnp.exp(jnp.where(causal[:, :, None, None], seg, -jnp.inf))
    xdt = xc * dtc[..., None]
    cb = jnp.einsum('bclgn,bcsgn->bclsg', Cc, Bc)
    y_diag = jnp.einsum('bclsg,bclsgr,bcsgrp->bclgrp', cb, decay, xdt)
    decay_to_end = jnp.exp(cs[:, :, -1:] - cs)
    states = jnp.einsum('bclgn,bclgr,bclgrp->cbgrpn', Bc, decay_to_end, xdt)
    chunk_decay = jnp.exp(cs[:, :, -1]).swapaxes(0, 1)

    def step(s, inp):
        st, dec = inp
        return s * dec[..., None, None] + st, s

    _, prev = lax.scan(step, jnp.zeros_like(states[0]), (states, chunk_decay))
    y_off = jnp.einsum('bclgn,cbgrpn,bclgr->bclgrp', Cc, prev, jnp.exp(cs))
    return (y_diag + y_off).reshape(B_, T, H, P)

def ssd_mixer(h, w_in, conv_w, conv_b, dt_bias, a_log, d_skip, norm_g, w_out):
    B_, T, _ = h.shape
    z, xbc, dt = jnp.split(h @ w_in, [SSM_DINNER, SSM_DINNER + CONV_DIM], axis=-1)
    xbc = lax.conv_general_dilated(xbc, conv_w[:, None, :], window_strides=(1,),
                                   padding=[(SSM_CONV - 1, 0)],
                                   dimension_numbers=('NWC', 'WIO', 'NWC'),
                                   feature_group_count=CONV_DIM) + conv_b
    xbc = jax.nn.silu(xbc)
    xs, Bm, Cm = jnp.split(xbc, [SSM_DINNER, SSM_DINNER + SSM_GROUPS * SSM_STATE], axis=-1)
    xs = xs.reshape(B_, T, SSM_HEADS, SSM_HEADDIM)
    Bm = Bm.reshape(B_, T, SSM_GROUPS, SSM_STATE)
    Cm = Cm.reshape(B_, T, SSM_GROUPS, SSM_STATE)
    dt = jax.nn.softplus(dt.astype(jnp.float32) + dt_bias.astype(jnp.float32))
    A = -jnp.exp(a_log.astype(jnp.float32))
    y = ssd_scan(xs, dt, A, Bm, Cm) + xs * d_skip[:, None]
    yz = (y.reshape(B_, T, SSM_DINNER) * jax.nn.silu(z)).reshape(B_, T, SSM_GROUPS, SSM_DINNER // SSM_GROUPS)
    y = rmsnorm(yz, norm_g.reshape(SSM_GROUPS, SSM_DINNER // SSM_GROUPS)).reshape(B_, T, SSM_DINNER)
    return y.astype(h.dtype) @ w_out

def moe_ffn(h, router_w, router_b, w1, w3, w2, ws1, ws3, ws2):
    B_, T, D = h.shape
    N = B_ * T
    xt = h.reshape(N, D)
    scores = jax.nn.sigmoid((xt @ router_w).astype(jnp.float32))
    _, idx = lax.top_k(scores + router_b.astype(jnp.float32), TOPK)
    sel = jnp.take_along_axis(scores, idx, axis=1)
    gates = sel / jnp.sum(sel, axis=-1, keepdims=True) * ROUTED_SCALE
    A_ = N * TOPK
    flat_e = idx.reshape(A_)
    flat_tok = jnp.arange(A_, dtype=jnp.int32) // TOPK
    flat_g = gates.reshape(A_)
    order = jnp.argsort(flat_e)
    e_sorted = flat_e[order]
    counts = jnp.zeros((N_EXPERTS,), jnp.int32).at[flat_e].add(1)
    padded = (counts + MOE_BLOCK - 1) // MOE_BLOCK * MOE_BLOCK
    start = jnp.cumsum(counts) - counts
    pend = jnp.cumsum(padded)
    pstart = pend - padded
    dest = pstart[e_sorted] + (jnp.arange(A_, dtype=jnp.int32) - start[e_sorted])
    n_blocks = (A_ + N_EXPERTS * (MOE_BLOCK - 1) + MOE_BLOCK - 1) // MOE_BLOCK
    P_ = n_blocks * MOE_BLOCK
    slot_tok = jnp.full((P_,), N, jnp.int32).at[dest].set(flat_tok[order])
    slot_gate = jnp.zeros((P_,), jnp.float32).at[dest].set(flat_g[order])
    block_exp = jnp.minimum(jnp.searchsorted(pend, jnp.arange(n_blocks, dtype=jnp.int32) * MOE_BLOCK,
                                             side='right'), N_EXPERTS - 1)
    xpad = jnp.concatenate([xt, jnp.zeros((1, D), xt.dtype)], axis=0)
    xs = xpad[slot_tok].reshape(n_blocks, MOE_BLOCK, D)

    def expert_block(args):
        xb, e = args
        return (jax.nn.silu(xb @ w1[e]) * (xb @ w3[e])) @ w2[e]

    ys = lax.map(expert_block, (xs, block_exp)).reshape(P_, D)
    routed = jnp.zeros((N + 1, D), jnp.float32).at[slot_tok].add(
        ys.astype(jnp.float32) * slot_gate[:, None])[:N]
    shared = (jax.nn.silu(xt @ ws1) * (xt @ ws3)) @ ws2
    return (routed.astype(h.dtype) + shared).reshape(B_, T, D)

def setup_inputs(seed: int = 0) -> dict:
    key = jax.random.key(seed)
    ks = jax.random.split(key, 32)
    f32 = jnp.float32
    D = D_MODEL

    def nrm(k, shape, scale):
        return jax.random.normal(k, shape, f32) * scale

    x = nrm(ks[0], (BATCH, SEQ, D), 1.0)
    c = nrm(ks[1], (BATCH, D), 1.0)
    positions = (jax.random.randint(ks[2], (BATCH, 1), 0, 1024, dtype=jnp.int32)
                 + jnp.arange(SEQ, dtype=jnp.int32)[None, :]).astype(jnp.int32)
    ada_w = nrm(ks[3], (DEPTH, D, 6 * D), 0.5 * D ** -0.5)
    ada_b = nrm(ks[4], (DEPTH, 6 * D), 0.02)
    norm_mix_g = 1.0 + nrm(ks[5], (DEPTH, D), 0.02)
    norm_ffn_g = 1.0 + nrm(ks[6], (DEPTH, D), 0.02)
    rel_bias = nrm(ks[7], (REL_BUCKETS, DSA_HEADS), 0.5)
    even_w_in = nrm(ks[8], (N_EVEN, D, EVEN_IN), D ** -0.5)
    ret_norm_g = 1.0 + nrm(ks[9], (N_EVEN, RET_HEADS, RET_DV), 0.02)
    dsa_q_g = 1.0 + nrm(ks[10], (N_EVEN, DSA_DH), 0.02)
    dsa_k_g = 1.0 + nrm(ks[11], (N_EVEN, DSA_DH), 0.02)
    even_w_out = nrm(ks[12], (N_EVEN, MIX_OUT_EVEN, D), MIX_OUT_EVEN ** -0.5)
    ssm_w_in = nrm(ks[13], (N_ODD, D, SSM_IN), D ** -0.5)
    ssm_conv_w = nrm(ks[14], (N_ODD, SSM_CONV, CONV_DIM), SSM_CONV ** -0.5)
    ssm_conv_b = nrm(ks[15], (N_ODD, CONV_DIM), 0.02)
    dt0 = jnp.exp(jax.random.uniform(ks[16], (N_ODD, SSM_HEADS), f32, math.log(1e-3), math.log(1e-1)))
    ssm_dt_bias = dt0 + jnp.log(-jnp.expm1(-dt0))
    ssm_a_log = jnp.log(jax.random.uniform(ks[17], (N_ODD, SSM_HEADS), f32, 1.0, 16.0))
    ssm_d = 1.0 + nrm(ks[18], (N_ODD, SSM_HEADS), 0.02)
    ssm_norm_g = 1.0 + nrm(ks[19], (N_ODD, SSM_DINNER), 0.02)
    ssm_w_out = nrm(ks[20], (N_ODD, SSM_DINNER, D), SSM_DINNER ** -0.5)
    router_w = nrm(ks[21], (DEPTH, D, N_EXPERTS), D ** -0.5)
    router_b = nrm(ks[22], (DEPTH, N_EXPERTS), 0.01)
    exp_w1 = nrm(ks[23], (DEPTH, N_EXPERTS, D, D_EXPERT), D ** -0.5)
    exp_w3 = nrm(ks[24], (DEPTH, N_EXPERTS, D, D_EXPERT), D ** -0.5)
    exp_w2 = nrm(ks[25], (DEPTH, N_EXPERTS, D_EXPERT, D), D_EXPERT ** -0.5)
    sh_w1 = nrm(ks[26], (DEPTH, D, D_SHARED), D ** -0.5)
    sh_w3 = nrm(ks[27], (DEPTH, D, D_SHARED), D ** -0.5)
    sh_w2 = nrm(ks[28], (DEPTH, D_SHARED, D), D_SHARED ** -0.5)
    return {'x': x, 'c': c, 'positions': positions, 'ada_w': ada_w, 'ada_b': ada_b,
            'norm_mix_g': norm_mix_g, 'norm_ffn_g': norm_ffn_g, 'rel_bias': rel_bias,
            'even_w_in': even_w_in, 'ret_norm_g': ret_norm_g, 'dsa_q_g': dsa_q_g, 'dsa_k_g': dsa_k_g,
            'even_w_out': even_w_out, 'ssm_w_in': ssm_w_in, 'ssm_conv_w': ssm_conv_w,
            'ssm_conv_b': ssm_conv_b, 'ssm_dt_bias': ssm_dt_bias, 'ssm_a_log': ssm_a_log,
            'ssm_d': ssm_d, 'ssm_norm_g': ssm_norm_g, 'ssm_w_out': ssm_w_out,
            'router_w': router_w, 'router_b': router_b, 'exp_w1': exp_w1, 'exp_w3': exp_w3,
            'exp_w2': exp_w2, 'sh_w1': sh_w1, 'sh_w3': sh_w3, 'sh_w2': sh_w2}

def reference(x, c, positions, ada_w, ada_b, norm_mix_g, norm_ffn_g, rel_bias,
              even_w_in, ret_norm_g, dsa_q_g, dsa_k_g, even_w_out,
              ssm_w_in, ssm_conv_w, ssm_conv_b, ssm_dt_bias, ssm_a_log, ssm_d, ssm_norm_g, ssm_w_out,
              router_w, router_b, exp_w1, exp_w3, exp_w2, sh_w1, sh_w3, sh_w2):
    cond = jax.nn.silu(c)
    for i in range(DEPTH):
        mod = cond @ ada_w[i] + ada_b[i]
        sh1, sc1, g1, sh2, sc2, g2 = jnp.split(mod, 6, axis=-1)
        h = modulate(rmsnorm(x, norm_mix_g[i]), sh1, sc1)
        j = i // 2
        if i % 2 == 0:
            mix = even_mixer(h, positions, rel_bias, even_w_in[j], ret_norm_g[j],
                             dsa_q_g[j], dsa_k_g[j], even_w_out[j])
        else:
            mix = ssd_mixer(h, ssm_w_in[j], ssm_conv_w[j], ssm_conv_b[j], ssm_dt_bias[j],
                            ssm_a_log[j], ssm_d[j], ssm_norm_g[j], ssm_w_out[j])
        x = x + g1[:, None, :] * mix
        h = modulate(rmsnorm(x, norm_ffn_g[i]), sh2, sc2)
        x = x + g2[:, None, :] * moe_ffn(h, router_w[i], router_b[i], exp_w1[i], exp_w3[i], exp_w2[i],
                                         sh_w1[i], sh_w3[i], sh_w2[i])
    return x


_drawn_inputs = setup_inputs


def setup_inputs(seed=0):
    import zlib

    import numpy as np

    out = dict(_drawn_inputs(seed))
    spreads = {}
    factors = {'ret_norm_g': 3.631,
     'dsa_q_g': 6.543,
     'dsa_k_g': 5.19,
     'ssm_conv_b': 3.933,
     'ssm_d': 5.075,
     'ssm_norm_g': 4.012}
    for name, (base, spread) in spreads.items():
        noise = np.random.default_rng([zlib.crc32(name.encode()), seed]).standard_normal(out[name].shape)
        drawn = base * np.exp(spread * noise) if base else spread * noise
        out[name] = __import__('jax').numpy.asarray(drawn.astype(out[name].dtype))
    for name, factor in factors.items():
        out[name] = (out[name] * factor).astype(out[name].dtype)
    return out
```

```python
import math
from collections import namedtuple
from contextlib import ExitStack

import numpy as np

import concourse.bass as bass
from concourse import mybir

F32 = mybir.dt.float32
BF16 = mybir.dt.bfloat16
I32 = mybir.dt.int32
ALU = mybir.AluOpType
ACT = mybir.ActivationFunctionType
AX = mybir.AxisListType

P = 128
D = 1024
T = 512
NT = T // P
KD = D // P
EPS = 1e-6
BANK = 512
SLOT = 2048
NSLOT = 6
NEG = -1e30

RH, RDK = 4, 128
AH, DH, IH, IDH = 8, 64, 8, 32
TOPK_KEYS = min(256, T // 4)
EVEN_IN = 2984
QA, KA, VA, QI, KI, WI = 2048, 2560, 2624, 2688, 2944, 2976
BUCKETS, MAX_DIST = 32, 128
DIN, SH, SG, SN, SP = 2048, 32, 8, 128, 64
CONV_DIM = DIN + 2 * SG * SN
SSM_IN = DIN + CONV_DIM + SH
E, TOPK, FE = 64, 8, 256
ROUTED_SCALE = 2.5
PI2_A = 6.28125
PI2_B = float(np.float32(2 * math.pi - 6.28125) // np.float32(2.0 ** -21) * 2.0 ** -21)
PI2_C = 2 * math.pi - PI2_A - PI2_B
ROUND = 1.5 * 2.0 ** 23


def bucket_thresholds():
    exact = BUCKETS // 2
    n = np.arange(1, 4 * MAX_DIST)
    large = exact + (np.log(n.astype(np.float32) / exact) / math.log(MAX_DIST / exact)
                     * (BUCKETS - exact)).astype(np.int32)
    bucket = np.where(n < exact, n, np.minimum(large, BUCKETS - 1))
    return np.array([-1e9] + [n[bucket >= b][0] for b in range(1, BUCKETS)], np.float32)


def constants():
    i = np.arange(P, dtype=np.float64)
    log_g = np.log(1.0 - 2.0 ** (-5.0 - np.arange(RH)))
    rel = i[None, :] - i[:, None]
    decay = [np.where(rel >= 0, np.exp(g * np.maximum(rel, 0)), 0) for g in log_g]
    parts = {
        "ident": np.eye(P),
        "upper": (rel >= 0) * 1.0,
        "ones": np.ones((P, P)),
        "causal": np.where(rel > 0, NEG, 0.0),
        "decayT": np.concatenate(decay, 1),
        "xi": np.tile(np.concatenate([np.exp(g * (i + 1)) for g in log_g])[None], (P, 1)),
        "zeta": np.stack([np.exp(g * (P - 1 - i)) for g in log_g], 1),
        "inv": np.tile((np.float32(10000.0) ** (-np.arange(64, dtype=np.float32) / np.float32(64)))[None], (P, 1)),
        "thr": np.tile(bucket_thresholds(), 4)[:, None],
        "quad": (np.arange(P)[:, None] // 32 == np.arange(4)[None]) * 1.0,
    }
    at, where = 0, {}
    for name, a in parts.items():
        where[name] = (at, at + a.shape[1])
        at += a.shape[1]
    return np.ascontiguousarray(np.concatenate(list(parts.values()), 1).astype(np.float32)), where


class Stage:
    pass


class Chain:

    def __init__(self, eng, sem):
        self.eng, self.sem, self.n = eng, sem, 0

    def __call__(self, ins):
        self.n += 1
        ins.then_inc(self.sem, 1)
        self.eng.wait_ge(self.sem, self.n)


Item = namedtuple("Item", "s buf free full filled")


class Ring:

    def __init__(self, slots, full):
        self.slots, self.full = slots, full
        self.n, self.fills, self.release = 0, [0] * NSLOT, [None] * NSLOT

    def take(self, release):
        s = self.n % NSLOT
        self.n += 1
        self.fills[s] += 16
        free, self.release[s] = self.release[s], release
        return Item(s, self.slots[:, s, :], free, self.full[s], self.fills[s])


def load_slot(eng, item, dst, src):
    if item.free:
        eng.wait_ge(*item.free)
    eng.dma_start(dst, src).then_inc(item.full, 16)


def bank(g, b):
    return g.ps[:, b * BANK:(b + 1) * BANK]


def const(g, name):
    a, b = g.where[name]
    return g.consts[:, a:b]


def sems(g, stage, *names):
    new = [g.nc.alloc_semaphore(f"{stage}_{n}") for n in names]
    g.live += new
    return namedtuple("Semaphores", names)(*new)


def recycle(g):
    g.nc.clear_and_free_semaphores(g.live)
    g.nc.all_engine_barrier()
    g.live = []
    g.ring.release = [None] * NSLOT


def phase_ada(g, layer):
    nc = g.nc
    s = sems(g, f"ada{layer}", "small", "cond", "condb", "mm", "evac", "cols", "colA")
    with ExitStack() as local:
        sb = lambda n, sh, dt=F32: local.enter_context(nc.sbuf_tensor(f"ada{layer}_{n}", sh, dt))
        brow = sb("brow", [1, 6 * D])
        modrow = sb("modrow", [1, 4 * D])
        ccol = sb("ccol", [P, KD])
        cond = sb("cond", [P, KD])
        condb = sb("condb", [P, KD, P])
        gcol = sb("gcol", [P, 2, KD])
        NB = 6 * D // BANK
        ps = [bank(g, b) for b in range(4)]
        colps = bank(g, 4)
        items = [g.ring.take((s.mm, n // 2 + 1)) for n in range(2 * NB)]
        w = g.dram["ada_w"][layer].rearrange("(p j) n -> p j n", j=KD)
        ones = const(g, "ones")
        rows = {0: 0, 1: 1, 2: 2, 3: 3, 6: 4, 7: 5, 8: 6, 9: 7}
        with nc.Block() as block:
            @block.sync
            def _(sp):
                if layer == 0:
                    sp.dma_start(g.consts[:, :], g.dram["consts_in"]).then_inc(s.small, 16)
                sp.dma_start(ccol[:, :], g.dram["c"][0].rearrange("(p j) -> p j", j=KD)).then_inc(s.small, 16)
                sp.dma_start(brow[:, :], g.dram["ada_b"][layer:layer + 1, :]).then_inc(s.small, 16)
                sp.dma_start(gcol[:, 0, :], g.dram["norm_mix_g"][layer].rearrange("(p j) -> p j", j=KD)).then_inc(s.small, 16)
                sp.dma_start(gcol[:, 1, :], g.dram["norm_ffn_g"][layer].rearrange("(p j) -> p j", j=KD)).then_inc(s.small, 16)
                for n, it in enumerate(items):
                    nb, half = n // 2, n % 2
                    load_slot(sp, it, it.buf.rearrange("p (j n) -> p j n", j=4),
                              w[:, 4 * half:4 * half + 4, nb * BANK:(nb + 1) * BANK])

            @block.scalar
            def _(act):
                act.wait_ge(s.small, 80 if layer == 0 else 64)
                act.activation(cond[:, :], ccol[:, :], ACT.Silu).then_inc(s.cond, 1)
                for nb in range(NB):
                    act.wait_ge(s.mm, nb + 1)
                    if nb in rows:
                        r = rows[nb]
                        act.copy(modrow[:, r * BANK:(r + 1) * BANK], ps[nb % 4][0:1, :]).then_inc(s.evac, 1)
                    else:
                        i = 0 if nb < 6 else 1
                        act.copy(g.gate_b[:, i, (nb % 2) * BANK:(nb % 2 + 1) * BANK], ps[nb % 4]).then_inc(s.evac, 1)

            @block.tensor
            def _(pe):
                pe.wait_ge(s.small, 80 if layer == 0 else 64)
                pe.wait_ge(s.condb, 1)
                for nb in range(NB):
                    if nb >= 4:
                        pe.wait_ge(s.evac, nb - 3)
                    pe.matmul(ps[nb % 4], ones[0:1, :], brow[0:1, nb * BANK:(nb + 1) * BANK], start=True, stop=False)
                    for half in range(2):
                        it = items[2 * nb + half]
                        pe.wait_ge(it.full, it.filled)
                        for j in range(4):
                            mm = pe.matmul(ps[nb % 4], condb[:, 4 * half + j, :], it.buf[:, j * BANK:(j + 1) * BANK],
                                           start=False, stop=(half == 1 and j == 3))
                    mm.then_inc(s.mm, 1)
                pe.wait_ge(s.evac, NB)
                for v in range(4):
                    for j in range(KD):
                        mm = pe.matmul(colps[:, v * KD + j:v * KD + j + 1],
                                       modrow[0:1, v * D + j:(v + 1) * D:KD], ones[0:1, 0:1], start=True, stop=True)
                mm.then_inc(s.cols, 1)

            @block.vector
            def _(dve):
                dve.wait_ge(s.cond, 1)
                dve.tensor_copy(condb[:, :, :], cond[:, :].unsqueeze(2).broadcast_to([P, KD, P])).then_inc(s.condb, 1)
                dve.wait_ge(s.cols, 1)
                for i in range(2):
                    dve.tensor_copy(g.shift[:, i, :], colps[:, (2 * i) * KD:(2 * i + 1) * KD]).then_inc(s.colA, 1)
                    dve.scalar_tensor_tensor(g.scale[:, i, :], colps[:, (2 * i + 1) * KD:(2 * i + 2) * KD], 1.0,
                                             gcol[:, i, :], ALU.add, ALU.mult).then_inc(s.colA, 1)


def phase_norm(g, tag, x_dram, which, hT):
    nc = g.nc
    s = sems(g, f"norm_{tag}", "x_even", "x_odd", "sq", "ms", "rstd", "xn", "tr", "ev_a", "ev_v", "chain")
    with ExitStack() as local:
        sb = lambda n, sh, dt=F32: local.enter_context(nc.sbuf_tensor(f"norm_{tag}_{n}", sh, dt))
        x = sb("x", [P, 2, D])
        junk = sb("junk", [P, D])
        ss = sb("ss", [P, NT])
        ms = sb("ms", [P, NT])
        rstd = sb("rstd", [P, NT])
        scale, shift = g.scale[:, which, :], g.shift[:, which, :]
        ident = const(g, "ident")
        x_loaded = [s.x_even, s.x_odd]
        with nc.Block() as block:
            @block.sync
            def _(sp):
                for t in range(NT):
                    if t >= 2:
                        sp.wait_ge(s.tr, 2 * (t - 1))
                    sp.dma_start(x[:, t % 2, :], x_dram[t * P:(t + 1) * P, :]).then_inc(x_loaded[t % 2], 16)

            @block.scalar
            def _(act):
                for t in range(NT):
                    act.wait_ge(x_loaded[t % 2], 16 * (t // 2 + 1))
                    if t:
                        act.wait_ge(s.sq, t)
                    act.activation(junk[:, :], x[:, t % 2, :], ACT.Square, accum_out=ss[:, t:t + 1]).then_inc(s.sq, 1)
                    act.wait_ge(s.ms, t + 1)
                    act.activation(rstd[:, t:t + 1], ms[:, t:t + 1], ACT.Sqrt).then_inc(s.rstd, 1)
                    act.wait_ge(s.tr, 2 * t + 2)
                    for j in range(4, KD):
                        act.activation(hT[:, j, t * P:(t + 1) * P], bank(g, 1 + 2 * (t % 2))[:, (j - 4) * P:(j - 3) * P],
                                       ACT.Identity, scale=scale[:, j:j + 1], bias=shift[:, j:j + 1]).then_inc(s.ev_a, 1)

            @block.vector
            def _(dve):
                link = Chain(dve, s.chain)
                for t in range(NT):
                    dve.wait_ge(s.sq, t + 1)
                    link(dve.tensor_scalar(ms[:, t:t + 1], ss[:, t:t + 1], 1.0 / D, EPS, ALU.mult, ALU.add))
                    dve.reciprocal(ms[:, t:t + 1], ms[:, t:t + 1]).then_inc(s.ms, 1)
                    dve.wait_ge(s.rstd, t + 1)
                    dve.tensor_scalar(x[:, t % 2, :], x[:, t % 2, :], rstd[:, t:t + 1], None, ALU.mult).then_inc(s.xn, 1)
                    dve.wait_ge(s.tr, 2 * t + 1)
                    for j in range(4):
                        dve.tensor_scalar(hT[:, j, t * P:(t + 1) * P], bank(g, 2 * (t % 2))[:, j * P:(j + 1) * P],
                                          scale[:, j:j + 1], shift[:, j:j + 1], ALU.mult, ALU.add).then_inc(s.ev_v, 1)

            @block.tensor
            def _(pe):
                for t in range(NT):
                    pe.wait_ge(s.xn, t + 1)
                    if t >= 2:
                        pe.wait_ge(s.ev_v, 4 * (t - 1))
                        pe.wait_ge(s.ev_a, 4 * (t - 1))
                    for j in range(KD):
                        tr = pe.transpose(bank(g, j // 4 + 2 * (t % 2))[:, (j % 4) * P:(j % 4 + 1) * P],
                                          x[:, t % 2, j:D:KD], ident)
                        if j % 4 == 3:
                            tr.then_inc(s.tr, 1)


def phase_even_in(g, hT, proj):
    nc = g.nc
    s = sems(g, "even_in", "half", "mm", "ev_a", "ev_v")
    w = g.dram["even_w_in"].rearrange("(p j) n -> p j n", j=KD)
    NB = -(-EVEN_IN // BANK)
    width = [min(BANK, EVEN_IN - nb * BANK) for nb in range(NB)]
    items = [g.ring.take((s.half, nb + 1) if h == 0 else (s.mm, 4 * nb + 4)) for nb in range(NB) for h in range(2)]
    with nc.Block() as block:
        @block.sync
        def _(sp):
            for n, it in enumerate(items):
                nb, half = n // 2, n % 2
                load_slot(sp, it, it.buf.rearrange("p (j n) -> p j n", j=4)[:, :, 0:width[nb]],
                          w[:, 4 * half:4 * half + 4, nb * BANK:nb * BANK + width[nb]])

        @block.tensor
        def _(pe):
            for nb in range(NB):
                for half in range(2):
                    it = items[2 * nb + half]
                    pe.wait_ge(it.full, it.filled)
                    for t in range(NT):
                        if nb and half == 0:
                            pe.wait_ge(s.ev_a if t % 2 == 0 else s.ev_v, 2 * (nb - 1) + t // 2 + 1)
                        for j in range(4):
                            k = 4 * half + j
                            mm = pe.matmul(bank(g, t)[:, 0:width[nb]], hT[:, k, t * P:(t + 1) * P],
                                           it.buf[:, j * BANK:j * BANK + width[nb]], start=(k == 0), stop=(k == 7))
                        if half == 1:
                            mm.then_inc(s.mm, 1)
                        elif t == NT - 1:
                            mm.then_inc(s.half, 1)

        def evacuate(eng, copy, odd, sem):
            for nb in range(NB):
                for t in range(odd, NT, 2):
                    eng.wait_ge(s.mm, 4 * nb + t + 1)
                    copy(proj[:, t, nb * BANK:nb * BANK + width[nb]], bank(g, t)[:, 0:width[nb]]).then_inc(sem, 1)

        @block.scalar
        def _(act):
            evacuate(act, act.copy, 0, s.ev_a)

        @block.vector
        def _(dve):
            evacuate(dve, dve.tensor_copy, 1, s.ev_v)


def phase_even_prep(g, proj, m):
    nc = g.nc
    s = sems(g, "prep", "pos", "angle", "trig", "ms", "rstd", "gate", "chain", "done", "rep", "repd")
    with ExitStack() as local:
        sb = lambda n, sh, dt=F32: local.enter_context(nc.sbuf_tensor(f"prep_{n}", sh, dt))
        pos_i = sb("pos_i", [P, NT], I32)
        pos_f = sb("pos_f", [P, NT])
        ang = sb("ang", [P, NT, 64])
        turns = sb("turns", [P, NT, 64])
        arg = sb("arg", [P, 2, NT, 64])
        trig = sb("trig", [P, 2, NT, 64])
        trig_k = sb("trig_k", [P, 2, NT, 64])
        part = sb("part", [P, 4, NT, 256])
        ss = sb("ss", [P, NT, 9])
        rs = sb("rs", [P, NT, 9])
        q_gain = sb("q_gain", [P, 1])
        with nc.Block() as block:
            @block.sync
            def _(sp):
                sp.dma_start(pos_i[:, :], g.dram["positions"].rearrange("(t p) -> p t", p=P)).then_inc(s.pos, 16)
                sp.dma_start(m.ret_gain[:, :], g.dram["ret_norm_g"].rearrange("h d -> (h d)").partition_broadcast(P)).then_inc(s.pos, 16)
                for half in range(2):
                    at = slice(64 * half, 64 * half + 64)
                    sp.dma_start(q_gain[at, :], g.dram["dsa_q_g"].rearrange("(d a) -> d a", a=1)).then_inc(s.pos, 16)
                    sp.dma_start(m.k_gain[at, :], g.dram["dsa_k_g"].rearrange("(d a) -> d a", a=1)).then_inc(s.pos, 16)
                sp.dma_start(m.pos_row_i[:, :], g.dram["positions"].partition_broadcast(P)).then_inc(s.pos, 16)
                sp.dma_start(m.pos_quad_i[:, :], g.dram["positions"].rearrange("(g q) -> q g", q=4)).then_inc(s.pos, 16)
                for r in range(4):
                    sp.dma_start(m.rel[32 * r:32 * r + 32, 0, :], g.dram["rel_bias"]).then_inc(s.rep, 16)
                sp.wait_ge(s.repd, 1)
                for r in range(4):
                    sp.dma_start(m.rel[32 * r + 1:32 * r + 32, 1, :], g.dram["rel_bias"][0:BUCKETS - 1, :]).then_inc(s.rep, 16)
                sp.wait_ge(s.rep, 128)

            @block.scalar
            def _(act):
                act.activation(proj[:, :, 1536:2048], proj[:, :, 1536:2048], ACT.Silu).then_inc(s.gate, 1)
                act.wait_ge(s.angle, 1)
                act.activation(trig[:, :, :, :], arg[:, :, :, :], ACT.Sin).then_inc(s.trig, 1)
                act.wait_ge(s.ms, 1)
                act.activation(rs[:, :, :], ss[:, :, :], ACT.Sqrt).then_inc(s.rstd, 1)

            @block.vector
            def _(dve):
                link = Chain(dve, s.chain)
                dve.memset(m.rel[:, 1, :], 0.0).then_inc(s.repd, 1)
                dve.wait_ge(s.pos, 128)
                link(dve.tensor_copy(pos_f[:, :], pos_i[:, :]))
                for t in range(NT):
                    last = dve.tensor_scalar(ang[:, t, :], const(g, "inv"), pos_f[:, t:t + 1], None, ALU.mult)
                link(last)
                link(dve.tensor_scalar(turns[:, :, :], ang[:, :, :], 0.5 / math.pi, ROUND, ALU.mult, ALU.add))
                link(dve.tensor_scalar(turns[:, :, :], turns[:, :, :], -ROUND, None, ALU.add))
                for c in (PI2_A, PI2_B, PI2_C):
                    link(dve.scalar_tensor_tensor(ang[:, :, :], turns[:, :, :], -c, ang[:, :, :], ALU.mult, ALU.add))
                link(dve.tensor_scalar(arg[:, 0, :, :], ang[:, :, :], 3.1415925, -3.1415925, ALU.min, ALU.max))
                link(dve.tensor_scalar(ang[:, :, :], ang[:, :, :], 0.5 * math.pi, None, ALU.add))
                link(dve.tensor_scalar(turns[:, :, :], ang[:, :, :], math.pi, -2.0 * math.pi, ALU.is_gt, ALU.mult))
                link(dve.tensor_tensor(ang[:, :, :], ang[:, :, :], turns[:, :, :], ALU.add))
                dve.tensor_scalar(arg[:, 1, :, :], ang[:, :, :], 3.1415925, -3.1415925, ALU.min, ALU.max).then_inc(s.angle, 1)
                sq = part[:, 0:2, :, :].rearrange("p a t c -> p (a t c)").rearrange("p (t c) -> p t c", t=NT)
                link(dve.tensor_tensor(sq, proj[:, :, QA:KA], proj[:, :, QA:KA], ALU.mult))
                sqk = part[:, 2, :, 0:64]
                link(dve.tensor_tensor(sqk, proj[:, :, KA:VA], proj[:, :, KA:VA], ALU.mult))
                link(dve.tensor_reduce(ss[:, :, 0:8], sq.rearrange("p t (h d) -> p t h d", d=DH), AX.X, ALU.add))
                link(dve.tensor_reduce(ss[:, :, 8:9], sqk.unsqueeze(2), AX.X, ALU.add))
                link(dve.tensor_scalar(ss[:, :, :], ss[:, :, :], 1.0 / DH, EPS, ALU.mult, ALU.add))
                dve.reciprocal(ss[:, :, :], ss[:, :, :]).then_inc(s.ms, 1)
                dve.tensor_scalar(m.q_gain[:, :], q_gain[:, :], DH ** -0.5, None, ALU.mult).then_inc(s.done, 1)
                dve.tensor_scalar(m.wi[:, :, :], proj[:, :, WI:EVEN_IN], IH ** -0.5 * IDH ** -0.5, None, ALU.mult).then_inc(s.done, 1)
                dve.wait_ge(s.trig, 1)
                link(dve.tensor_scalar(trig_k[:, :, :, :], trig[:, :, :, :], RDK ** -0.5, None, ALU.mult))
                for base, tr in ((0, trig), (512, trig_k)):
                    v = proj[:, :, base:base + 512].rearrange("p t (h two d) -> p t h two d", two=2, d=64)
                    x1, x2 = v[:, :, :, 0, :], v[:, :, :, 1, :]
                    sn = tr[:, 0, :, :].unsqueeze(2).broadcast_to([P, NT, RH, 64])
                    cs = tr[:, 1, :, :].unsqueeze(2).broadcast_to([P, NT, RH, 64])
                    pt = [part[:, i, :, :].rearrange("p t (h d) -> p t h d", d=64) for i in range(4)]
                    for i, (x, f) in enumerate(((x1, cs), (x2, sn), (x1, sn), (x2, cs))):
                        link(dve.tensor_tensor(pt[i], x, f, ALU.mult))
                    link(dve.tensor_tensor(x1, pt[0], pt[1], ALU.subtract))
                    link(dve.tensor_tensor(x2, pt[2], pt[3], ALU.add))
                for t in range(NT):
                    k = proj[:, t, 512:1024].rearrange("p (h d) -> p h d", d=RDK)
                    dve.tensor_tensor(m.kz[:, t, :].rearrange("p (h d) -> p h d", d=RDK), k,
                                      const(g, "zeta").unsqueeze(2).broadcast_to([P, RH, RDK]), ALU.mult).then_inc(s.done, 1)
                dve.wait_ge(s.rstd, 1)
                qa = proj[:, :, QA:KA].rearrange("p t (h d) -> p t h d", d=DH)
                dve.tensor_tensor(qa, qa, rs[:, :, 0:8].unsqueeze(3).broadcast_to([P, NT, AH, DH]), ALU.mult).then_inc(s.done, 1)
                ka = proj[:, :, KA:VA]
                dve.tensor_tensor(ka, ka, rs[:, :, 8:9].broadcast_to([P, NT, DH]), ALU.mult).then_inc(s.done, 1)


def phase_even_turn(g, proj, m):
    nc = g.nc
    s = sems(g, "turn", "ki4", "tr", "ev_a", "ev_v")
    ident = const(g, "ident")
    groups = []
    for h in range(RH):
        groups.append(("q", h, [proj[:, t, h * 128:(h + 1) * 128] for t in range(NT)], P))
    for h in range(RH):
        groups.append(("k", h, [proj[:, t, 512 + h * 128:512 + (h + 1) * 128] for t in range(NT)], P))
    for r in range(AH // 2):
        groups.append(("qa", r, [proj[:, t, QA + r * 128:QA + (r + 1) * 128] for t in range(NT)], P))
    groups.append(("ka", 0, [proj[:, t, KA:VA] for t in range(NT)], DH))
    for r in range(2):
        groups.append(("qi", r, [proj[:, t, QI + r * 128:QI + (r + 1) * 128] for t in range(NT)], P))
    groups.append(("ki", 0, [m.ki4[:, t, :] for t in range(NT)], P))
    copies_a = {"q": 1, "qa": 2}
    copies_v = {"q": 1, "k": 1, "ka": 1, "qi": 1, "ki": 1}
    done_a, done_v, na, nv = [], [], 0, 0
    for kind, *_ in groups:
        na += copies_a.get(kind, 0)
        nv += copies_v.get(kind, 0)
        done_a.append(na)
        done_v.append(nv)
    with nc.Block() as block:
        @block.gpsimd
        def _(pool):
            ki = proj[:, :, KI:WI]
            for r in range(4):
                pool.tensor_copy(m.ki4[:, :, r * IDH:(r + 1) * IDH], ki).then_inc(s.ki4, 1)

        @block.tensor
        def _(pe):
            for n, (kind, r, srcs, rows) in enumerate(groups):
                if n >= 8:
                    if done_a[n - 8]:
                        pe.wait_ge(s.ev_a, done_a[n - 8])
                    pe.wait_ge(s.ev_v, done_v[n - 8])
                if kind == "ki":
                    pe.wait_ge(s.ki4, 4)
                for t in range(NT):
                    tr = pe.transpose(bank(g, n % 8)[0:rows, t * P:(t + 1) * P], srcs[t], ident)
                tr.then_inc(s.tr, 1)

        @block.scalar
        def _(act):
            for n, (kind, r, _, rows) in enumerate(groups):
                b = bank(g, n % 8)
                if kind in copies_a:
                    act.wait_ge(s.tr, n + 1)
                if kind == "q":
                    act.copy(m.qT[:, r, :], b).then_inc(s.ev_a, 1)
                if kind == "qa":
                    for odd in range(2):
                        at = slice(64 * odd, 64 * odd + 64)
                        act.activation(m.qaT[:, :, 2 * r + odd], b[at, :], ACT.Copy,
                                       scale=m.q_gain[at, :]).then_inc(s.ev_a, 1)

        @block.vector
        def _(dve):
            for n, (kind, r, _, rows) in enumerate(groups):
                b = bank(g, n % 8)
                if kind == "q":
                    dve.wait_ge(s.ev_a, n + 1)
                    xi = const(g, "xi")[:, r * P:(r + 1) * P].unsqueeze(1).broadcast_to([P, NT, P])
                    dve.tensor_tensor(m.qxT[:, r, :].rearrange("p (t n) -> p t n", t=NT),
                                      m.qT[:, r, :].rearrange("p (t n) -> p t n", t=NT), xi, ALU.mult).then_inc(s.ev_v, 1)
                elif kind in copies_v:
                    dve.wait_ge(s.tr, n + 1)
                if kind == "k":
                    dve.tensor_copy(m.kT[:, r, :], b).then_inc(s.ev_v, 1)
                if kind == "ka":
                    dve.tensor_scalar(m.kaT[:, :], b[0:DH, :], m.k_gain[0:DH, :], None, ALU.mult).then_inc(s.ev_v, 1)
                if kind == "qi":
                    dve.tensor_copy(m.qiT[:, r, :], b).then_inc(s.ev_v, 1)
                if kind == "ki":
                    dve.tensor_copy(m.kiT[:, :], b).then_inc(s.ev_v, 1)


def phase_retention(g, proj, m, yT):
    nc = g.nc
    s = sems(g, "ret", "inner", "decayed", "y", "u", "state", "y_out", "chain", "ms", "rstd", "yn", "tr", "ev")
    log_g = np.log(1.0 - 2.0 ** (-5.0 - np.arange(RH)))
    with ExitStack() as local:
        sb = lambda n, sh, dt=F32: local.enter_context(nc.sbuf_tensor(f"ret_{n}", sh, dt))
        inner = sb("inner", [P, 2, RH * P])
        state = sb("state", [P, RH, P])
        y, sq = proj[:, :, 0:512], proj[:, :, 512:1024]
        ss = sb("ss", [P, NT, RH])
        rs = sb("rs", [P, NT, RH])
        with nc.Block() as block:
            @block.tensor
            def _(pe):
                def scores(c):
                    if c >= 2:
                        pe.wait_ge(s.decayed, c - 1)
                    for h in range(RH):
                        mm = pe.matmul(bank(g, c % 2)[:, h * P:(h + 1) * P], m.kT[:, h, c * P:(c + 1) * P],
                                       m.qT[:, h, c * P:(c + 1) * P], start=True, stop=True)
                    mm.then_inc(s.inner, 1)
                    for h in range(RH):
                        mm = pe.matmul(bank(g, 4 + c % 2)[:, h * P:(h + 1) * P], m.kz[:, c, h * P:(h + 1) * P],
                                       proj[:, c, 1024 + h * P:1024 + (h + 1) * P], start=True, stop=True)
                    mm.then_inc(s.u, 1)

                scores(0)
                for c in range(NT):
                    pe.wait_ge(s.decayed, c + 1)
                    if c >= 2:
                        pe.wait_ge(s.y_out, c - 1)
                    if c:
                        pe.wait_ge(s.state, RH * c)
                    for h in range(RH):
                        yb = bank(g, 2 + c % 2)[:, h * P:(h + 1) * P]
                        mm = pe.matmul(yb, inner[:, c % 2, h * P:(h + 1) * P],
                                       proj[:, c, 1024 + h * P:1024 + (h + 1) * P], start=True, stop=(c == 0))
                        if c:
                            mm = pe.matmul(yb, m.qxT[:, h, c * P:(c + 1) * P], state[:, h, :], start=False, stop=True)
                    mm.then_inc(s.y, 1)
                    if c + 1 < NT:
                        scores(c + 1)
                for h in range(RH):
                    pe.wait_ge(s.yn, NT)
                    for t in range(NT):
                        tr = pe.transpose(bank(g, h)[:, t * P:(t + 1) * P], y[:, t, h * P:(h + 1) * P], const(g, "ident"))
                    tr.then_inc(s.tr, 1)

            @block.scalar
            def _(act):
                for c in range(NT):
                    act.wait_ge(s.y, c + 1)
                    act.copy(y[:, c, :], bank(g, 2 + c % 2)).then_inc(s.y_out, 1)
                act.wait_ge(s.ms, 1)
                act.activation(rs[:, :, :], ss[:, :, :], ACT.Sqrt).then_inc(s.rstd, 1)
                for h in range(RH):
                    act.wait_ge(s.tr, h + 1)
                    act.copy(yT[:, h, :], bank(g, h)).then_inc(s.ev, 1)

            @block.vector
            def _(dve):
                link = Chain(dve, s.chain)
                for c in range(NT):
                    dve.wait_ge(s.inner, c + 1)
                    dve.tensor_tensor(inner[:, c % 2, :], bank(g, c % 2), const(g, "decayT"), ALU.mult).then_inc(s.decayed, 1)
                    if c == NT - 1:
                        break
                    dve.wait_ge(s.u, c + 1)
                    dve.wait_ge(s.y, c + 1)
                    if c:
                        dve.wait_ge(s.state, RH * c)
                    for h in range(RH):
                        u = bank(g, 4 + c % 2)[:, h * P:(h + 1) * P]
                        if c == 0:
                            dve.tensor_copy(state[:, h, :], u).then_inc(s.state, 1)
                        else:
                            dve.scalar_tensor_tensor(state[:, h, :], state[:, h, :], float(np.exp(log_g[h] * P)), u,
                                                     ALU.mult, ALU.add).then_inc(s.state, 1)
                dve.wait_ge(s.y_out, NT)
                link(dve.tensor_tensor(sq[:, :, :], y[:, :, :], y[:, :, :], ALU.mult))
                link(dve.tensor_reduce(ss[:, :, :], sq.rearrange("p t (h d) -> p t h d", d=P), AX.X, ALU.add))
                link(dve.tensor_scalar(ss[:, :, :], ss[:, :, :], 1.0 / P, EPS, ALU.mult, ALU.add))
                dve.reciprocal(ss[:, :, :], ss[:, :, :]).then_inc(s.ms, 1)
                link(dve.tensor_tensor(sq[:, :, :], proj[:, :, 1536:2048],
                                       m.ret_gain[:, :].unsqueeze(1).broadcast_to([P, NT, RH * P]), ALU.mult))
                dve.wait_ge(s.rstd, 1)
                yv = y.rearrange("p t (h d) -> p t h d", d=P)
                link(dve.tensor_tensor(yv, yv, rs[:, :, :].unsqueeze(3).broadcast_to([P, NT, RH, P]), ALU.mult))
                for t in range(NT):
                    dve.tensor_tensor(y[:, t, :], y[:, t, :], sq[:, t, :], ALU.mult).then_inc(s.yn, 1)


def phase_index(g, m):
    nc = g.nc
    s = sems(g, "index", "mm", "relu", "added", "chain", "quad", "quadT", "pos", "posT")
    with ExitStack() as local:
        sb = lambda n, sh, dt=F32: local.enter_context(nc.sbuf_tensor(f"index_{n}", sh, dt))
        relu = sb("relu", [P, 2, T])
        score = sb("score", [P, T])
        best = sb("best", [P, 8])
        quadT = sb("quadT", [4, P])
        pos_quad = sb("pos_quad", [4, P])
        delta = sb("delta", [P, AH])
        rest = sb("rest", [P, 4, AH])
        with nc.Block() as block:
            @block.tensor
            def _(pe):
                pe.transpose(bank(g, 7)[0:4, 0:P], const(g, "quad"), const(g, "ident")).then_inc(s.quad, 1)
                n = 0
                for qb in range(1, NT):
                    w = P * (qb + 1)
                    for h in range(IH):
                        if n >= 4:
                            pe.wait_ge(s.relu, n - 3)
                        at = slice(32 * (h % 4), 32 * (h % 4) + 32)
                        pe.matmul(bank(g, n % 4)[:, 0:w], m.qiT[at, h // 4, qb * P:(qb + 1) * P], m.kiT[at, 0:w],
                                  start=True, stop=True).then_inc(s.mm, 1)
                        n += 1
                    if qb == 1:
                        pe.wait_ge(s.quadT, 1)
                        pe.matmul(bank(g, 7)[:, P:2 * P], quadT[:, :], pos_quad[:, :], start=True, stop=True).then_inc(s.pos, 1)

            @block.scalar
            def _(act):
                for n in range(IH * (NT - 1)):
                    w = P * (n // IH + 2)
                    act.wait_ge(s.mm, n + 1)
                    if n >= 2:
                        act.wait_ge(s.added, n - 1)
                    act.activation(relu[:, n % 2, 0:w], bank(g, n % 4)[:, 0:w], ACT.Relu).then_inc(s.relu, 1)

            @block.vector
            def _(dve):
                link = Chain(dve, s.chain)
                link(dve.tensor_copy(pos_quad[:, :], m.pos_quad_i[:, :]))
                link(dve.tensor_copy(m.pos_row[:, :], m.pos_row_i[:, :]))
                dve.wait_ge(s.quad, 1)
                dve.tensor_copy(quadT[:, :], bank(g, 7)[0:4, 0:P]).then_inc(s.quadT, 1)
                link(dve.tensor_tensor(delta[:, :], m.rel[:, 0, :], m.rel[:, 1, :], ALU.subtract))
                link(dve.tensor_tensor(rest[:, :, :], delta[:, :].unsqueeze(1).broadcast_to([P, 4, AH]),
                                       const(g, "quad").unsqueeze(2).broadcast_to([P, 4, AH]), ALU.mult))
                for i in range(3):
                    d = m.delta3[:, i, :].rearrange("p (q h) -> p q h", q=4)
                    link(dve.tensor_copy(d, rest[:, :, :]))
                    if i < 2:
                        link(dve.tensor_tensor(rest[:, :, :], rest[:, :, :], d, ALU.subtract))
                link(dve.tensor_copy(m.expand[:, :].rearrange("p (q h) -> p q h", h=AH),
                                     const(g, "ident").unsqueeze(2).broadcast_to([P, P, AH])))
                link(dve.tensor_copy(m.mask[:, 0, 0:P], const(g, "causal")))
                n = 0
                for qb in range(1, NT):
                    w = P * (qb + 1)
                    sc = score[:, 0:w]
                    for h in range(IH):
                        dve.wait_ge(s.relu, n + 1)
                        if h:
                            dve.wait_ge(s.added, n)
                            dve.scalar_tensor_tensor(sc, relu[:, n % 2, 0:w], m.wi[:, qb, h:h + 1], sc,
                                                     ALU.mult, ALU.add).then_inc(s.added, 1)
                        else:
                            dve.tensor_scalar(sc, relu[:, n % 2, 0:w], m.wi[:, qb, 0:1], None, ALU.mult).then_inc(s.added, 1)
                        n += 1
                    if qb == 1:
                        dve.wait_ge(s.pos, 1)
                        link(dve.tensor_scalar(m.pos_edge[:, :], bank(g, 7)[:, P:2 * P], const(g, "thr"), None, ALU.subtract))
                    dve.wait_ge(s.added, n)
                    link(dve.tensor_tensor(score[:, w - P:w], score[:, w - P:w], const(g, "causal"), ALU.add))
                    for r in range(TOPK_KEYS // 8):
                        link(dve.max(best[:, :], sc))
                        link(dve.match_replace(sc, best[:, :], sc, -3e38))
                    link(dve.tensor_scalar(m.mask[:, qb, 0:w], sc, -2e38, NEG, ALU.is_gt, ALU.mult))


def phase_attention(g, proj, m, yT):
    nc = g.nc
    s = sems(g, "att", "steps", "logits", "max", "exp", "prob", "turn", "turned", "out", "stored", "chain")
    NTILE = T // 16
    with ExitStack() as local:
        sb = lambda n, sh, dt=F32: local.enter_context(nc.sbuf_tensor(f"att_{n}", sh, dt))
        steps = sb("steps", [P, 2, 4, T], BF16)
        prob = sb("prob", [P, 2, T])
        probT = sb("probT", [P, 2, T])
        nmax = sb("nmax", [P, 2])
        total = sb("total", [P, 2])
        inv = sb("inv", [P, 2])
        with nc.Block() as block:
            @block.tensor
            def _(pe):
                def logits(i):
                    w, b = P * (i // 8 + 1), bank(g, i % 2)
                    if i >= 2:
                        pe.wait_ge(s.exp, i - 1)
                    pe.matmul(b[:, 0:w], m.qaT[:, 16 * i:16 * i + 16, :].rearrange("p q h -> p (q h)"), m.kaT[:, 0:w],
                              start=True, stop=False)
                    pe.matmul(b[:, 0:w], m.expand[:, (i % 8) * P:(i % 8 + 1) * P], m.mask[:, i // 8, 0:w],
                              start=False, stop=False)
                    pe.wait_ge(s.steps, i + 1)
                    for j in range(4):
                        for part in range(3):
                            mm = pe.matmul(b[32 * j:32 * j + 32, 0:w], m.delta3[:, part, :], steps[:, i % 2, j, 0:w],
                                           start=False, stop=(part == 2))
                    mm.then_inc(s.logits, 1)

                def turn(i):
                    w, b = P * (i // 8 + 1), bank(g, 2 + i % 2)
                    pe.wait_ge(s.prob, i + 1)
                    if i >= 2:
                        pe.wait_ge(s.turned, i - 1)
                    for k in range(w // P):
                        tr = pe.transpose(b[:, k * P:(k + 1) * P], prob[:, i % 2, k * P:(k + 1) * P], const(g, "ident"))
                    tr.then_inc(s.turn, 1)

                def values(i):
                    nk, b = i // 8 + 1, bank(g, 4 + i % 2)
                    pe.wait_ge(s.turned, i + 1)
                    if i >= 2:
                        pe.wait_ge(s.stored, 2 * (i - 1))
                    for k in range(nk):
                        mm = pe.matmul(b[0:DH, 0:P], proj[:, k, VA:QI], probT[:, i % 2, k * P:(k + 1) * P],
                                       start=(k == 0), stop=(k == nk - 1))
                    mm.then_inc(s.out, 1)

                for i in range(NTILE + 2):
                    if i < NTILE:
                        logits(i)
                    if 1 <= i <= NTILE:
                        turn(i - 1)
                    if i >= 2:
                        values(i - 2)

            @block.scalar
            def _(act):
                def exp(i):
                    w = P * (i // 8 + 1)
                    act.wait_ge(s.max, i + 1)
                    if i >= 2:
                        act.wait_ge(s.turn, i - 1)
                    act.activation(prob[:, i % 2, 0:w], bank(g, i % 2)[:, 0:w], ACT.Exp, bias=nmax[:, i % 2:i % 2 + 1],
                                   accum_out=total[:, i % 2:i % 2 + 1]).then_inc(s.exp, 1)

                def turned(i):
                    w = P * (i // 8 + 1)
                    act.wait_ge(s.turn, i + 1)
                    if i >= 2:
                        act.wait_ge(s.out, i - 1)
                    act.copy(probT[:, i % 2, 0:w], bank(g, 2 + i % 2)[:, 0:w]).then_inc(s.turned, 1)

                def store(i):
                    act.wait_ge(s.out, i + 1)
                    o = bank(g, 4 + i % 2)[0:DH, 0:P].rearrange("p (q h two) -> p h two q", h=4, two=2)
                    for odd in range(2):
                        act.copy(yT[64 * odd:64 * odd + 64, 4:8, 16 * i:16 * i + 16], o[:, :, odd, :]).then_inc(s.stored, 1)

                for i in range(NTILE + 3):
                    if i < NTILE:
                        exp(i)
                    if 1 <= i <= NTILE:
                        turned(i - 1)
                    if 3 <= i:
                        store(i - 3)

            @block.vector
            def _(dve):
                link = Chain(dve, s.chain)

                def make_steps(i):
                    w = P * (i // 8 + 1)
                    if i >= 2:
                        dve.wait_ge(s.logits, i - 1)
                    for j in range(4):
                        last = dve.tensor_scalar(steps[:, i % 2, j, 0:w], m.pos_row[:, 0:w],
                                                 m.pos_edge[:, 4 * i + j:4 * i + j + 1], None, ALU.is_le)
                    last.then_inc(s.steps, 1)

                make_steps(0)
                for i in range(NTILE):
                    w = P * (i // 8 + 1)
                    if i + 1 < NTILE:
                        make_steps(i + 1)
                    dve.wait_ge(s.logits, i + 1)
                    link(dve.reduce_max(nmax[:, i % 2:i % 2 + 1], bank(g, i % 2)[:, 0:w], AX.X))
                    dve.tensor_scalar(nmax[:, i % 2:i % 2 + 1], nmax[:, i % 2:i % 2 + 1], -1.0, None, ALU.mult).then_inc(s.max, 1)
                    dve.wait_ge(s.exp, i + 1)
                    link(dve.reciprocal(inv[:, i % 2:i % 2 + 1], total[:, i % 2:i % 2 + 1]))
                    dve.tensor_scalar(prob[:, i % 2, 0:w], prob[:, i % 2, 0:w], inv[:, i % 2:i % 2 + 1], None,
                                      ALU.mult).then_inc(s.prob, 1)


def phase_out(g, tag, yT, w_view, kc, x_dram, out_dram):
    nc = g.nc
    s = sems(g, f"out_{tag}", "x", "half", "mm", "gated", "added", "store")
    nslots = kc // 4
    last_of = lambda nb: (s.mm, 4 * nb + 4)
    items = [g.ring.take((s.half, nb * (nslots - 1) + q + 1) if q < nslots - 1 else last_of(nb))
             for nb in range(2) for q in range(nslots)]
    with ExitStack() as local:
        x = local.enter_context(nc.sbuf_tensor(f"out_{tag}_x", [P, NT, D], F32))
        with nc.Block() as block:
            @block.sync
            def _(sp):
                for n, it in enumerate(items):
                    nb, q = n // nslots, n % nslots
                    load_slot(sp, it, it.buf.rearrange("p (j n) -> p j n", j=4),
                              w_view[:, 4 * q:4 * q + 4, nb * BANK:(nb + 1) * BANK])
                    if n == 0:
                        sp.dma_start(x[:, :, :], x_dram.rearrange("(t p) n -> p t n", p=P)).then_inc(s.x, 16)
                for t in range(NT):
                    sp.wait_ge(s.added, NT + t + 1)
                    sp.dma_start(out_dram[t * P:(t + 1) * P, :], x[:, t, :]).then_inc(s.store, 16)
                sp.wait_ge(s.store, 16 * NT)

            @block.tensor
            def _(pe):
                for nb in range(2):
                    for q in range(nslots):
                        it = items[nb * nslots + q]
                        pe.wait_ge(it.full, it.filled)
                        for t in range(NT):
                            for j in range(4):
                                k = 4 * q + j
                                mm = pe.matmul(bank(g, 4 * nb + t), yT[:, k, t * P:(t + 1) * P],
                                               it.buf[:, j * BANK:(j + 1) * BANK], start=(k == 0), stop=(k == kc - 1))
                            if q == nslots - 1:
                                mm.then_inc(s.mm, 1)
                            elif t == NT - 1:
                                mm.then_inc(s.half, 1)

            @block.vector
            def _(dve):
                dve.wait_ge(s.x, 16)
                for nb in range(2):
                    at = slice(nb * BANK, (nb + 1) * BANK)
                    for t in range(NT):
                        n = 4 * nb + t
                        dve.wait_ge(s.mm, n + 1)
                        dve.tensor_tensor(bank(g, n), bank(g, n), g.gate_b[:, 0, at], ALU.mult).then_inc(s.gated, 1)
                        dve.wait_ge(s.gated, n + 1)
                        dve.tensor_tensor(x[:, t, at], bank(g, n), x[:, t, at], ALU.add).then_inc(s.added, 1)


def phase_router(g, tag, layer, hT, r):
    nc = g.nc
    s = sems(g, f"router_{tag}", "w", "logits", "exp", "chain")
    with ExitStack() as local:
        sb = lambda n, sh, dt=F32: local.enter_context(nc.sbuf_tensor(f"router_{tag}_{n}", sh, dt))
        w = sb("w", [P, KD, E])
        bias = sb("bias", [P, E])
        score = sb("score", [P, NT, E])
        biased = sb("biased", [P, NT, E])
        left = sb("left", [P, NT, E])
        best = sb("best", [P, NT, 8])
        total = sb("total", [P, NT])
        with nc.Block() as block:
            @block.sync
            def _(sp):
                sp.dma_start(w[:, :, :], g.dram["router_w"][layer].rearrange("(p j) n -> p j n", j=KD)).then_inc(s.w, 16)
                sp.dma_start(bias[:, :], g.dram["router_b"][layer].partition_broadcast(P)).then_inc(s.w, 16)

            @block.tensor
            def _(pe):
                pe.wait_ge(s.w, 32)
                for t in range(NT):
                    for j in range(KD):
                        mm = pe.matmul(bank(g, 0)[:, t * E:(t + 1) * E], hT[:, j, t * P:(t + 1) * P], w[:, j, :],
                                       start=(j == 0), stop=(j == KD - 1))
                mm.then_inc(s.logits, 1)

            @block.scalar
            def _(act):
                act.wait_ge(s.logits, 1)
                act.activation(score[:, :, :].rearrange("p t e -> p (t e)"), bank(g, 0)[:, 0:NT * E], ACT.Exp,
                               scale=-1.0).then_inc(s.exp, 1)

            @block.vector
            def _(dve):
                link = Chain(dve, s.chain)
                dve.wait_ge(s.w, 32)
                dve.wait_ge(s.exp, 1)
                link(dve.tensor_scalar(score[:, :, :], score[:, :, :], 1.0, None, ALU.add))
                link(dve.reciprocal(score[:, :, :], score[:, :, :]))
                link(dve.tensor_tensor(biased[:, :, :], score[:, :, :], bias[:, :].unsqueeze(1).broadcast_to([P, NT, E]), ALU.add))
                for t in range(NT):
                    last = dve.max(best[:, t, :], biased[:, t, :])
                link(last)
                for t in range(NT):
                    last = dve.match_replace(left[:, t, :], best[:, t, :], biased[:, t, :], NEG)
                link(last)
                link(dve.tensor_scalar(r.sel[:, :, :], left[:, :, :], NEG / 2, None, ALU.is_lt))
                link(dve.tensor_tensor(r.gates[:, :, :], r.sel[:, :, :], score[:, :, :], ALU.mult))
                link(dve.tensor_reduce(total[:, :], r.gates[:, :, :], AX.X, ALU.add))
                link(dve.reciprocal(total[:, :], total[:, :]))
                link(dve.tensor_scalar(total[:, :], total[:, :], ROUTED_SCALE, None, ALU.mult))
                link(dve.tensor_tensor(r.gates[:, :, :], r.gates[:, :, :], total[:, :].unsqueeze(2).broadcast_to([P, NT, E]), ALU.mult))


def phase_dense_experts(g, tag, layer, hT, r, x_dram, out_dram):
    nc = g.nc
    s = sems(g, f"dense_{tag}", "up", "silu", "hidden", "down", "acc", "x", "gated", "store")
    with ExitStack() as local:
        sb = lambda n, sh, dt=F32: local.enter_context(nc.sbuf_tensor(f"dense_{tag}_{n}", sh, dt))
        acc = sb("acc", [P, NT, D])
        silu = sb("silu", [P, 2, 2, T])
        hidden = sb("hidden", [P, 2, 2, T])
        x = sb("x", [P, 2, D])
        items = [g.ring.take(None) for _ in range(3 * (E + 1))]

        def slot(n, par, which):
            it = items[3 * par + which]
            return it, it.filled + ((n - par) // 2 * 16 if isinstance(n, int) else (n - par) * 8)

        def steps(eng, body):
            body(0, 0)
            body(1, 1)
            with eng.Fori(0, (E - 2) // 2) as i:
                body(2 * i + 2, 0)
                body(2 * i + 3, 1)
            body(E, 0)

        with nc.Block() as block:
            @block.sync
            def _(sp):
                def loads(n, par):
                    w1, w3, w2 = [slot(n, par, k)[0] for k in range(3)]
                    first = isinstance(n, int) and n < 2
                    if isinstance(n, int) and n == 0:
                        srcs = g.dram["sh_w1"][layer:layer + 1], g.dram["sh_w3"][layer:layer + 1], g.dram["sh_w2"][layer:layer + 1]
                    else:
                        srcs = [w[layer, bass.ds(n - 1, 1)] for w in (g.dram["exp_w1"], g.dram["exp_w3"], g.dram["exp_w2"])]
                    if not first:
                        sp.wait_ge(s.up, 4 * (n - 2) + 2)
                    sp.dma_start(w1.buf.rearrange("p (e j n) -> p e j n", e=1, j=KD),
                                 srcs[0].rearrange("e (p j) n -> p e j n", j=KD)).then_inc(w1.full, 16)
                    if not first:
                        sp.wait_ge(s.up, 4 * (n - 2) + 4)
                    sp.dma_start(w3.buf.rearrange("p (e j n) -> p e j n", e=1, j=KD),
                                 srcs[1].rearrange("e (p j) n -> p e j n", j=KD)).then_inc(w3.full, 16)
                    if not first:
                        sp.wait_ge(s.down, 8 * (n - 2) + 8)
                    sp.dma_start(w2.buf.rearrange("p (e j n) -> p e j n", e=1, j=2),
                                 srcs[2].rearrange("e (j p) n -> p e j n", p=P)).then_inc(w2.full, 16)

                steps(sp, loads)
                for t in range(NT):
                    if t >= 2:
                        sp.wait_ge(s.store, 16 * (t - 1))
                    sp.dma_start(x[:, t % 2, :], x_dram[t * P:(t + 1) * P, :]).then_inc(s.x, 16)
                    sp.wait_ge(s.gated, 2 * (t + 1))
                    sp.dma_start(out_dram[t * P:(t + 1) * P, :], x[:, t % 2, :]).then_inc(s.store, 16)
                sp.wait_ge(s.store, 16 * NT)

            @block.tensor
            def _(pe):
                def up(n, par):
                    for m in range(4):
                        it, filled = slot(n, par, m // 2)
                        if m % 2 == 0:
                            pe.wait_ge(it.full, filled)
                        if m == 0 and not (isinstance(n, int) and n == 0):
                            pe.wait_ge(s.hidden, 2 * n)
                        for j in range(KD):
                            mm = pe.matmul(bank(g, m), it.buf[:, j * FE + (m % 2) * P:j * FE + (m % 2 + 1) * P],
                                           hT[:, j, :], start=(j == 0), stop=(j == KD - 1))
                        mm.then_inc(s.up, 1)

                def down(n, par):
                    it, filled = slot(n, par, 2)
                    pe.wait_ge(it.full, filled)
                    pe.wait_ge(s.hidden, 2 * n + 2)
                    for q in range(8):
                        if not (isinstance(n, int) and n == 0 and q < 4):
                            pe.wait_ge(s.acc, 8 * n + q - 3)
                        for k in range(2):
                            mm = pe.matmul(bank(g, 4 + q % 4), hidden[:, par, k, (q // 2) * P:(q // 2 + 1) * P],
                                           it.buf[:, k * D + (q % 2) * BANK:k * D + (q % 2 + 1) * BANK],
                                           start=(k == 0), stop=(k == 1))
                        mm.then_inc(s.down, 1)

                def step(n, par):
                    up(n, par)
                    if not (isinstance(n, int) and n == 0):
                        down(n - 1, 1 - par)

                steps(pe, step)
                down(E, 0)

            @block.scalar
            def _(act):
                def step(n, par):
                    for c in range(2):
                        act.wait_ge(s.up, 4 * n + 1 + c)
                        if not (isinstance(n, int) and n < 2):
                            act.wait_ge(s.hidden, 2 * (n - 2) + c + 1)
                        act.activation(silu[:, par, c, :], bank(g, c), ACT.Silu).then_inc(s.silu, 1)

                steps(act, step)

            @block.vector
            def _(dve):
                def make_hidden(n, par):
                    for c in range(2):
                        dve.wait_ge(s.silu, 2 * n + c + 1)
                        dve.wait_ge(s.up, 4 * n + 3 + c)
                        if not (isinstance(n, int) and n < 2):
                            dve.wait_ge(s.down, 8 * (n - 1))
                        dve.tensor_tensor(hidden[:, par, c, :], silu[:, par, c, :], bank(g, 2 + c), ALU.mult).then_inc(s.hidden, 1)

                def accumulate(n, par):
                    for q in range(8):
                        t, at = q // 2, slice((q % 2) * BANK, (q % 2 + 1) * BANK)
                        dve.wait_ge(s.down, 8 * n + q + 1)
                        if isinstance(n, int) and n == 0:
                            dve.tensor_copy(acc[:, t, at], bank(g, 4 + q % 4)).then_inc(s.acc, 1)
                        else:
                            dve.wait_ge(s.acc, 8 * n + q - 7)
                            dve.scalar_tensor_tensor(acc[:, t, at], bank(g, 4 + q % 4), r.gates[:, t, bass.ds(n - 1, 1)],
                                                     acc[:, t, at], ALU.mult, ALU.add).then_inc(s.acc, 1)

                def step(n, par):
                    make_hidden(n, par)
                    if not (isinstance(n, int) and n == 0):
                        accumulate(n - 1, 1 - par)

                steps(dve, step)
                accumulate(E, 0)
                for t in range(NT):
                    dve.wait_ge(s.acc, 8 * E + 2 * t + 2)
                    dve.tensor_tensor(acc[:, t, :], acc[:, t, :], g.gate_b[:, 1, :], ALU.mult).then_inc(s.gated, 1)
                    dve.wait_ge(s.gated, 2 * t + 1)
                    dve.wait_ge(s.x, 16 * (t + 1))
                    dve.tensor_tensor(x[:, t % 2, :], x[:, t % 2, :], acc[:, t, :], ALU.add).then_inc(s.gated, 1)


def phase_ssd_in(g, hT, d):
    nc = g.nc
    s = sems(g, "ssd_in", "small", "dt_half", "dt_mm", "dt_out", "turned", "turn_out", "half", "mm", "ev_a", "ev_v",
             "scaled", "conv", "act", "tr", "x_out", "chain")
    NZ = DIN // BANK
    NC = CONV_DIM // BANK
    w = g.dram["ssm_w_in"].rearrange("(p j) n -> p j n", j=KD)
    with ExitStack() as local:
        sb = lambda n, sh, dt=F32: local.enter_context(nc.sbuf_tensor(f"ssd_in_{n}", sh, dt))
        taps = sb("taps", [32, 5, P])
        tapsT = sb("tapsT", [P, 5, 32])
        conv = sb("conv", [P, 2, T])
        silu = sb("silu", [P, 2, T])
        NB = NZ + NC
        items = [g.ring.take((s.half, nb + 1) if h == 0 else (s.mm, 4 * nb + 4)) for nb in range(NB) for h in range(2)]
        items.append(g.ring.take(None))
        with nc.Block() as block:
            @block.sync
            def _(sp):
                for k in range(4):
                    sp.dma_start(taps[:, k, :], g.dram["ssm_conv_w"][k].rearrange("(c p) -> c p", p=P)).then_inc(s.small, 16)
                sp.dma_start(taps[:, 4, :], g.dram["ssm_conv_b"].rearrange("(c p) -> c p", p=P)).then_inc(s.small, 16)
                sp.dma_start(d.dt_bias[:, :], g.dram["ssm_dt_bias"].partition_broadcast(P)).then_inc(s.small, 16)
                sp.dma_start(d.a[:, :], g.dram["ssm_a_log"].partition_broadcast(P)).then_inc(s.small, 16)
                sp.dma_start(d.skip[:, :], g.dram["ssm_d"].partition_broadcast(P)).then_inc(s.small, 16)
                for n, it in enumerate(items[:-1]):
                    nb, half = n // 2, n % 2
                    load_slot(sp, it, it.buf.rearrange("p (j n) -> p j n", j=4),
                              w[:, 4 * half:4 * half + 4, nb * BANK:(nb + 1) * BANK])
                it = items[-1]
                load_slot(sp, it, it.buf[:, 0:KD * SH].rearrange("p (j n) -> p j n", j=KD), w[:, :, NB * BANK:SSM_IN])

            @block.tensor
            def _(pe):
                pe.wait_ge(s.small, 128)
                for k in range(5):
                    tr = pe.transpose(bank(g, 7)[:, k * 32:(k + 1) * 32], taps[:, k, :], const(g, "ident")[0:32, 0:32])
                tr.then_inc(s.turned, 1)

                def turn_x(c):
                    pe.wait_ge(s.act, c + 1)
                    if c >= 2:
                        pe.wait_ge(s.x_out, c - 1)
                    for t in range(NT):
                        tr = pe.transpose(bank(g, 4 + c % 2)[:, t * P:(t + 1) * P], silu[:, c % 2, t * P:(t + 1) * P],
                                          const(g, "ident"))
                    tr.then_inc(s.tr, 1)

                for nb in range(NB):
                    for half in range(2):
                        it = items[2 * nb + half]
                        pe.wait_ge(it.full, it.filled)
                        for t in range(4):
                            if nb and half == 0:
                                if nb <= NZ:
                                    pe.wait_ge(s.ev_a, 4 * (nb - 1) + t + 1)
                                else:
                                    pe.wait_ge(s.conv, 3 * (4 * (nb - 1 - NZ) + t + 1))
                            for j in range(4):
                                k = 4 * half + j
                                if nb < NZ:
                                    lhsT, rhs = hT[:, k, t * P:(t + 1) * P], it.buf[:, j * BANK:(j + 1) * BANK]
                                else:
                                    lhsT, rhs = it.buf[:, j * BANK + t * P:j * BANK + (t + 1) * P], hT[:, k, :]
                                mm = pe.matmul(bank(g, t), lhsT, rhs, start=(k == 0), stop=(k == 7))
                            if half == 1:
                                mm.then_inc(s.mm, 1)
                            elif t == 3:
                                mm.then_inc(s.half, 1)
                            c = 4 * (nb - NZ) + t - 2
                            if half == 1 and 0 <= c < DIN // P:
                                turn_x(c)
                it = items[-1]
                pe.wait_ge(it.full, it.filled)
                for t in range(NT):
                    for k in range(KD):
                        mm = pe.matmul(bank(g, 6)[:, t * SH:(t + 1) * SH], hT[:, k, t * P:(t + 1) * P],
                                       it.buf[:, k * SH:(k + 1) * SH], start=(k == 0), stop=(k == KD - 1))
                mm.then_inc(s.dt_mm, 1)

            def place(c):
                if c < DIN // P:
                    return silu[:, c % 2, :]
                c -= DIN // P
                return d.BT[:, c, :] if c < SG else d.CT[:, c - SG, :]

            @block.scalar
            def _(act):
                act.wait_ge(s.small, 128)
                act.activation(d.a[:, :], d.a[:, :], ACT.Exp).then_inc(s.dt_half, 1)
                for n in range(4 * NZ):
                    act.wait_ge(s.mm, n + 1)
                    act.activation(d.z[:, n % 4, (n // 4) * BANK:(n // 4 + 1) * BANK], bank(g, n % 4), ACT.Silu).then_inc(s.ev_a, 1)
                act.wait_ge(s.turn_out, 1)

                def scaled(c):
                    act.wait_ge(s.mm, 4 * NZ + c + 1)
                    if c >= 2:
                        act.wait_ge(s.act, c - 1)
                    act.activation(conv[:, c % 2, :], bank(g, c % 4), ACT.Identity, scale=tapsT[:, 3, c:c + 1],
                                   bias=tapsT[:, 4, c:c + 1]).then_inc(s.scaled, 1)

                def activate(c):
                    act.wait_ge(s.conv, 3 * (c + 1))
                    if c < DIN // P and c >= 2:
                        act.wait_ge(s.tr, c - 1)
                    act.activation(place(c), conv[:, c % 2, :], ACT.Silu).then_inc(s.act, 1)

                def copy_x(c):
                    act.wait_ge(s.tr, c + 1)
                    act.copy(d.x[:, :, c * P:(c + 1) * P], bank(g, 4 + c % 2).rearrange("p (t n) -> p t n", t=NT)).then_inc(s.x_out, 1)

                N = CONV_DIM // P
                for c in range(N + 1):
                    if c < N:
                        scaled(c)
                    if 3 <= c < DIN // P + 3:
                        copy_x(c - 3)
                    if c >= 1:
                        activate(c - 1)

            @block.vector
            def _(dve):
                link = Chain(dve, s.chain)
                dve.wait_ge(s.turned, 1)
                dve.tensor_copy(tapsT[:, :, :].rearrange("p k c -> p (k c)"), bank(g, 7)[:, 0:160]).then_inc(s.turn_out, 1)
                dve.wait_ge(s.turn_out, 1)
                n = 0
                for c in range(CONV_DIM // P):
                    dve.wait_ge(s.scaled, c + 1)
                    for back in range(1, 4):
                        if back > 1:
                            dve.wait_ge(s.conv, n)
                        dve.scalar_tensor_tensor(conv[:, c % 2, back:T], bank(g, c % 4)[:, 0:T - back],
                                                 tapsT[:, 3 - back, c:c + 1], conv[:, c % 2, back:T],
                                                 ALU.mult, ALU.add).then_inc(s.conv, 1)
                        n += 1
                dve.wait_ge(s.dt_half, 1)
                link(dve.tensor_scalar(d.a[:, :], d.a[:, :], -1.0, None, ALU.mult))
                dve.wait_ge(s.dt_mm, 1)
                dve.wait_ge(s.small, 128)
                dve.tensor_tensor(d.dt[:, :, :], bank(g, 6)[:, 0:NT * SH].rearrange("p (t h) -> p t h", t=NT),
                                  d.dt_bias[:, :].unsqueeze(1).broadcast_to([P, NT, SH]), ALU.add).then_inc(s.dt_out, 1)


def phase_ssd_scan(g, d):
    nc = g.nc
    s = sems(g, "scan", "gain", "abs", "ln", "da", "cum", "cums", "ecs", "rows", "y", "seg", "exp", "mix", "state",
             "xdt", "ydone", "sq", "ms", "rstd", "chain", "skip")
    R = SH // SG
    W = R * SP
    with ExitStack() as local:
        sb = lambda n, sh, dt=F32: local.enter_context(nc.sbuf_tensor(f"scan_{n}", sh, dt))
        gain = sb("gain", [P, DIN])
        tmp = sb("tmp", [P, NT, SH])
        dA = sb("dA", [P, NT, SH])
        cs = sb("cs", [P, NT, SH])
        ecs = sb("ecs", [P, NT, SH])
        dte = sb("dte", [P, NT, SH])
        cdec = sb("cdec", [P, NT, SH])
        xdt = sb("xdt", [P, 2, W])
        xdte = sb("xdte", [P, 2, W])
        cbm = sb("cbm", [P, 2, P])
        seg = sb("seg", [P, 2, R * P])
        btok = sb("btok", [P, 2, P])
        state = sb("state", [P, SG, W])
        skip = sb("skip", [P, 2, W])
        yt = sb("yt", [P, 2, W])
        ss = sb("ss", [P, NT, SG])
        rs = sb("rs", [P, NT, SG])
        junk = sb("junk", [P, W])
        NCG = NT * SG
        heads = lambda ap: ap.rearrange("p (r c) -> p r c", r=R)
        spread = lambda ap, n: ap.unsqueeze(2).broadcast_to([P, R, n])
        with nc.Block() as block:
            @block.sync
            def _(sp):
                sp.dma_start(gain[:, :], g.dram["ssm_norm_g"].partition_broadcast(P)).then_inc(s.gain, 16)

            @block.tensor
            def _(pe):
                pe.wait_ge(s.da, 1)
                for c in range(NT):
                    pe.matmul(bank(g, 0)[:, c * SH:(c + 1) * SH], const(g, "upper"), dA[:, c, :], start=True, stop=True)
                    mm = pe.matmul(bank(g, 0)[:, 128 + c * SH:128 + (c + 1) * SH], const(g, "ones"), dA[:, c, :],
                                   start=True, stop=True)
                mm.then_inc(s.cum, 1)

                def decays(n):
                    c, q, b = n // SG, n % SG, n % 2
                    at = slice(c * P, (c + 1) * P)
                    if n == 0:
                        pe.wait_ge(s.cums, 1)
                    if n >= 2:
                        pe.wait_ge(s.mix, n - 1)
                    pe.matmul(bank(g, b)[:, 0:P], d.BT[:, q, at], d.CT[:, q, at], start=True, stop=True)
                    pe.transpose(bank(g, b)[:, P:2 * P], d.BT[:, q, at], const(g, "ident"))
                    for r in range(R):
                        mm = pe.matmul(bank(g, 2 + b)[:, r * P:(r + 1) * P],
                                       dA[:, c, q * R + r:q * R + r + 1].broadcast_to([P, P]), const(g, "upper"),
                                       start=True, stop=True)
                    mm.then_inc(s.rows, 1)

                decays(0)
                for n in range(NCG):
                    c, q, b = n // SG, n % SG, n % 2
                    at = slice(c * P, (c + 1) * P)
                    if n + 1 < NCG:
                        decays(n + 1)
                    pe.wait_ge(s.mix, n + 1)
                    pe.wait_ge(s.xdt, 2 * n + 2)
                    if n >= 2:
                        pe.wait_ge(s.ydone, n - 1)
                    if c:
                        pe.wait_ge(s.state, n - SG + 1)
                    for r in range(R):
                        pe.matmul(bank(g, 4 + b)[:, r * SP:(r + 1) * SP], seg[:, b, r * P:(r + 1) * P],
                                  xdt[:, b, r * SP:(r + 1) * SP], start=True, stop=True)
                    if c:
                        pe.matmul(bank(g, 4 + b)[:, W:2 * W], d.CT[:, q, at], state[:, q, :], start=True, stop=True)
                    if c < NT - 1:
                        mm = pe.matmul(bank(g, 6 + b)[:, 0:W], btok[:, b, :], xdte[:, b, :], start=True, stop=True)
                    else:
                        mm = pe.matmul(bank(g, 6 + b)[:, 0:1], const(g, "ident"), const(g, "ones")[:, 0:1], start=True, stop=True)
                    mm.then_inc(s.y, 1)

            @block.gpsimd
            def _(pool):
                for n in range(NCG):
                    c, q, b = n // SG, n % SG, n % 2
                    if n >= 2:
                        pool.wait_ge(s.ydone, n - 1)
                    xg = heads(d.x[:, c, q * W:(q + 1) * W])
                    pool.tensor_tensor(heads(skip[:, b, :]), xg, spread(d.skip[:, q * R:(q + 1) * R], SP), ALU.mult).then_inc(s.skip, 1)

            @block.scalar
            def _(act):
                act.activation(tmp[:, :, :], d.dt[:, :, :], ACT.Abs).then_inc(s.abs, 1)
                act.wait_ge(s.abs, 1)
                act.activation(tmp[:, :, :], tmp[:, :, :], ACT.Exp, scale=-1.0).then_inc(s.abs, 1)
                act.wait_ge(s.abs, 2)
                act.activation(tmp[:, :, :], tmp[:, :, :], ACT.Ln, bias=1.0).then_inc(s.ln, 1)
                act.wait_ge(s.ecs, 1)
                act.activation(ecs[:, :, :], cs[:, :, :], ACT.Exp).then_inc(s.cums, 1)
                act.activation(dte[:, :, :], dte[:, :, :], ACT.Exp).then_inc(s.cums, 1)
                act.activation(cdec[:, :, :], cdec[:, :, :], ACT.Exp).then_inc(s.cums, 1)
                for n in range(NCG):
                    b = n % 2
                    act.wait_ge(s.seg, n + 1)
                    act.activation(seg[:, b, :], seg[:, b, :], ACT.Exp).then_inc(s.exp, 1)
                for n in range(NCG):
                    c, q = n // SG, n % SG
                    act.wait_ge(s.ydone, NCG)
                    if n:
                        act.wait_ge(s.sq, n)
                    act.activation(junk[:, :], d.z[:, c, q * W:(q + 1) * W], ACT.Square, accum_out=ss[:, c, q:q + 1]).then_inc(s.sq, 1)
                act.wait_ge(s.ms, 1)
                act.activation(rs[:, :, :], ss[:, :, :], ACT.Sqrt).then_inc(s.rstd, 1)

            @block.vector
            def _(dve):
                link = Chain(dve, s.chain)
                dve.wait_ge(s.ln, 1)
                link(dve.scalar_tensor_tensor(d.dt[:, :, :], d.dt[:, :, :], 0.0, tmp[:, :, :], ALU.max, ALU.add))
                dve.tensor_tensor(dA[:, :, :], d.dt[:, :, :], d.a[:, :].unsqueeze(1).broadcast_to([P, NT, SH]), ALU.mult).then_inc(s.da, 1)
                dve.wait_ge(s.cum, 1)
                v = lambda a: a[:, :, :].rearrange("p c h -> p (c h)")
                link(dve.tensor_copy(v(cs), bank(g, 0)[:, 0:128]))
                link(dve.tensor_copy(v(cdec), bank(g, 0)[:, 128:256]))
                dve.tensor_tensor(v(dte), v(cdec), v(cs), ALU.subtract).then_inc(s.ecs, 1)
                dve.wait_ge(s.cums, 3)
                for n in range(NCG + 1):
                    if n < NCG:
                        c, q, b = n // SG, n % SG, n % 2
                        hs = slice(q * R, (q + 1) * R)
                        if n >= 2:
                            dve.wait_ge(s.y, n - 1)
                        dve.tensor_tensor(heads(xdt[:, b, :]), heads(d.x[:, c, q * W:(q + 1) * W]),
                                          spread(d.dt[:, c, hs], SP), ALU.mult).then_inc(s.xdt, 1)
                        dve.wait_ge(s.xdt, 2 * n + 1)
                        dve.tensor_tensor(heads(xdte[:, b, :]), heads(xdt[:, b, :]), spread(dte[:, c, hs], SP),
                                          ALU.mult).then_inc(s.xdt, 1)
                        dve.wait_ge(s.rows, n + 1)
                        link(dve.tensor_tensor(heads(seg[:, b, :]), heads(bank(g, 2 + b)), spread(cs[:, c, hs], P), ALU.subtract))
                        dve.tensor_scalar(seg[:, b, :], seg[:, b, :], 0.0, None, ALU.min).then_inc(s.seg, 1)
                        link(dve.tensor_copy(btok[:, b, :], bank(g, b)[:, P:2 * P]))
                        link(dve.tensor_tensor(cbm[:, b, :], bank(g, b)[:, 0:P], const(g, "upper"), ALU.mult))
                        dve.wait_ge(s.exp, n + 1)
                        dve.tensor_tensor(heads(seg[:, b, :]), heads(seg[:, b, :]),
                                          cbm[:, b, :].unsqueeze(1).broadcast_to([P, R, P]), ALU.mult).then_inc(s.mix, 1)
                    if n >= 1:
                        k = n - 1
                        c, q, b = k // SG, k % SG, k % 2
                        hs = slice(q * R, (q + 1) * R)
                        dve.wait_ge(s.y, k + 1)
                        if c < NT - 1:
                            if c:
                                dve.wait_ge(s.state, k - SG + 1)
                                link(dve.tensor_tensor(heads(state[:, q, :]), heads(state[:, q, :]), spread(cdec[:, c, hs], SP), ALU.mult))
                                dve.tensor_tensor(state[:, q, :], state[:, q, :], bank(g, 6 + b)[:, 0:W], ALU.add).then_inc(s.state, 1)
                            else:
                                dve.tensor_copy(state[:, q, :], bank(g, 6 + b)[:, 0:W]).then_inc(s.state, 1)
                        y, yb = yt[:, b, :], bank(g, 4 + b)
                        dve.wait_ge(s.skip, k + 1)
                        link(dve.tensor_tensor(y, skip[:, b, :], yb[:, 0:W], ALU.add))
                        if c:
                            link(dve.tensor_tensor(heads(skip[:, b, :]), heads(yb[:, W:2 * W]), spread(ecs[:, c, hs], SP), ALU.mult))
                            link(dve.tensor_tensor(y, y, skip[:, b, :], ALU.add))
                        z = d.z[:, c, q * W:(q + 1) * W]
                        dve.tensor_tensor(z, z, y, ALU.mult).then_inc(s.ydone, 1)
                dve.wait_ge(s.sq, NCG)
                link(dve.tensor_scalar(ss[:, :, :], ss[:, :, :], 1.0 / W, EPS, ALU.mult, ALU.add))
                dve.reciprocal(ss[:, :, :], ss[:, :, :]).then_inc(s.ms, 1)
                dve.wait_ge(s.rstd, 1)
                dve.wait_ge(s.gain, 16)
                for c in range(NT):
                    zg = d.z[:, c, :].rearrange("p (q w) -> p q w", q=SG)
                    link(dve.tensor_tensor(zg, zg, rs[:, c, :].unsqueeze(2).broadcast_to([P, SG, W]), ALU.mult))
                    link(dve.tensor_tensor(d.z[:, c, :], d.z[:, c, :], gain[:, :], ALU.mult))


def phase_ssd_turn(g, d, yT):
    nc = g.nc
    s = sems(g, "ssd_turn", "tr", "ev_a", "ev_v")
    with nc.Block() as block:
        @block.tensor
        def _(pe):
            for k in range(DIN // P):
                if k >= 8:
                    pe.wait_ge(s.ev_a if k % 2 == 0 else s.ev_v, (k - 8) // 2 + 1)
                for t in range(NT):
                    tr = pe.transpose(bank(g, k % 8)[:, t * P:(t + 1) * P], d.z[:, t, k * P:(k + 1) * P], const(g, "ident"))
                tr.then_inc(s.tr, 1)

        def evacuate(eng, copy, odd, sem):
            for k in range(odd, DIN // P, 2):
                eng.wait_ge(s.tr, k + 1)
                copy(yT[:, k, :], bank(g, k % 8)).then_inc(sem, 1)

        @block.scalar
        def _(act):
            evacuate(act, act.copy, 0, s.ev_a)

        @block.vector
        def _(dve):
            evacuate(dve, dve.tensor_copy, 1, s.ev_v)


def ssd_layer(g):
    nc = g.nc
    with ExitStack() as mixer:
        mb = lambda n, sh, dt=F32: mixer.enter_context(nc.sbuf_tensor(n, sh, dt))
        d = Stage()
        d.z = mb("z", [P, NT, DIN])
        d.dt_bias = mb("dt_bias", [P, SH])
        d.a = mb("a", [P, SH])
        d.skip = mb("skip_w", [P, SH])
        d.dt = mb("dt", [P, NT, SH])
        with ExitStack() as scan:
            cb = lambda n, sh: scan.enter_context(nc.sbuf_tensor(n, sh, F32))
            d.x, d.BT, d.CT = cb("xs", [P, NT, DIN]), cb("BT", [P, SG, T]), cb("CT", [P, SG, T])
            with ExitStack() as inp:
                hT = inp.enter_context(nc.sbuf_tensor("hT1", [P, KD, T], F32))
                phase_norm(g, "mix1", g.dram["x2"], 0, hT)
                phase_ssd_in(g, hT, d)
            phase_ssd_scan(g, d)
        yT = mb("yT1", [P, DIN // P, T])
        phase_ssd_turn(g, d, yT)
        phase_out(g, "mix1", yT, g.dram["ssm_w_out"].rearrange("(j p) n -> p j n", p=P), DIN // P, g.dram["x2"], g.dram["x3"])


def ffn(g, tag, layer, x_dram, out_dram):
    nc = g.nc
    with ExitStack() as local:
        fb = lambda n, sh, dt=F32: local.enter_context(nc.sbuf_tensor(f"{n}_{tag}", sh, dt))
        hT = fb("hT_ffn", [P, KD, T])
        r = Stage()
        r.gates = fb("gates", [P, NT, E])
        r.sel = fb("sel", [P, NT, E])
        phase_norm(g, tag, x_dram, 1, hT)
        phase_router(g, tag, layer, hT, r)
        phase_dense_experts(g, tag, layer, hT, r, x_dram, out_dram)


def build(nc, a, where):
    with ExitStack() as ctx:
        g = Stage()
        g.nc, g.ctx, g.where, g.live, g.dram = nc, ctx, where, [], a
        sb = lambda n, sh, dt=F32: ctx.enter_context(nc.sbuf_tensor(n, sh, dt))
        g.ps = ctx.enter_context(nc.psum_tensor("ps", [P, 8 * BANK], F32))
        NC_ = max(b for _, b in where.values())
        g.consts = sb("consts", [P, NC_])
        ring = sb("ring", [P, NSLOT, SLOT])
        g.ring = Ring(ring, [ctx.enter_context(nc.semaphore(f"slot{i}_full")) for i in range(NSLOT)])
        g.gate_b = sb("gate_b", [P, 2, D])
        g.scale = sb("scale", [P, 2, KD])
        g.shift = sb("shift", [P, 2, KD])
        phase_ada(g, 0)
        with ExitStack() as mixer:
            mb = lambda n, sh, dt=F32: mixer.enter_context(nc.sbuf_tensor(n, sh, dt))
            yT = mb("yT0", [P, KD, T])
            proj = mb("proj", [P, NT, EVEN_IN])
            with ExitStack() as inp:
                hT = inp.enter_context(nc.sbuf_tensor("hT0", [P, KD, T], F32))
                phase_norm(g, "mix0", g.dram["x"], 0, hT)
                phase_even_in(g, hT, proj)
            m = Stage()
            m.ret_gain = mb("ret_gain", [P, RH * P])
            m.q_gain = mb("q_gain", [P, 1])
            m.k_gain = mb("k_gain", [P, 1])
            m.pos_row_i = mb("pos_row_i", [P, T], I32)
            m.pos_row = mb("pos_row", [P, T])
            m.pos_quad_i = mb("pos_quad_i", [4, P], I32)
            m.pos_edge = mb("pos_edge", [P, P])
            m.rel = mb("rel", [P, 2, AH])
            m.delta3 = mb("delta3", [P, 3, 4 * AH], BF16)
            m.expand = mb("expand", [P, P * AH], BF16)
            m.mask = mb("mask", [P, NT, T], BF16)
            m.wi = mb("wi", [P, NT, IH])
            m.kaT = mb("kaT", [DH, T])
            m.qaT = mb("qaT", [DH, T, AH])
            with ExitStack() as head:
                hb = lambda n, sh, dt=F32: head.enter_context(nc.sbuf_tensor(n, sh, dt))
                m.qiT, m.kiT, m.ki4 = hb("qiT", [P, 2, T]), hb("kiT", [P, T]), hb("ki4", [P, NT, P])
                m.kz = hb("kz", [P, NT, RH * P])
                phase_even_prep(g, proj, m)
                m.qT, m.kT, m.qxT = hb("qT", [P, RH, T]), hb("kT", [P, RH, T]), hb("qxT", [P, RH, T])
                phase_even_turn(g, proj, m)
                phase_retention(g, proj, m, yT)
                phase_index(g, m)
            phase_attention(g, proj, m, yT)
            phase_out(g, "mix0", yT, g.dram["even_w_out"].rearrange("(j p) n -> p j n", p=P), KD, g.dram["x"], g.dram["x1"])
        recycle(g)
        ffn(g, "ffn0", 0, g.dram["x1"], g.dram["x2"])
        recycle(g)
        phase_ada(g, 1)
        ssd_layer(g)
        recycle(g)
        ffn(g, "ffn1", 1, g.dram["x3"], g.dram["out"])


_INS = ["x", "c", "positions", "ada_w", "ada_b", "norm_mix_g", "norm_ffn_g", "rel_bias", "even_w_in", "ret_norm_g",
        "dsa_q_g", "dsa_k_g", "even_w_out", "ssm_w_in", "ssm_conv_w", "ssm_conv_b", "ssm_dt_bias", "ssm_a_log",
        "ssm_d", "ssm_norm_g", "ssm_w_out", "router_w", "router_b", "exp_w1", "exp_w3", "exp_w2", "sh_w1", "sh_w3",
        "sh_w2"]
_FLAT = {"x", "positions", "even_w_in", "ret_norm_g", "dsa_q_g", "dsa_k_g", "even_w_out", "ssm_w_in", "ssm_conv_w",
         "ssm_conv_b", "ssm_dt_bias", "ssm_a_log", "ssm_d", "ssm_norm_g", "ssm_w_out"}


def kernel(**inputs):
    import concourse.bacc as bacc
    from concourse.bass_utils import run_bass_kernel_spmd

    nc = bacc.Bacc("TRN2", target_bir_lowering=False, num_devices=1)
    table, where = constants()
    arrays, aps = {"consts_dram": table}, {}
    for name in _INS:
        v = np.ascontiguousarray(inputs[name])
        arrays[f"{name}_dram"] = v.reshape(v.shape[1:]) if name in _FLAT else v
    for name, v in arrays.items():
        ap = nc.dram_tensor(name, v.shape, mybir.dt.from_np(v.dtype), kind="ExternalInput").ap()
        aps["consts_in" if name == "consts_dram" else name[:-5]] = ap
    aps["out"] = nc.dram_tensor("out_dram", (T, D), F32, kind="ExternalOutput").ap()
    for name in ("x1", "x2", "x3"):
        aps[name] = nc.dram_tensor(f"{name}_scratch", (T, D), F32).ap()
    with nc.allow_non_contiguous_dma(reason="positions and gains, a few KiB, turned while they are loaded"):
        build(nc, aps, where)
    r = run_bass_kernel_spmd(nc, [arrays], core_ids=[0])
    return r.results[0]["out_dram"].reshape(1, T, D)
```

```python
import math
from collections import namedtuple
from contextlib import ExitStack

import numpy as np

import concourse.bass as bass
from concourse import mybir

F32 = mybir.dt.float32
BF16 = mybir.dt.bfloat16
I32 = mybir.dt.int32
U32 = mybir.dt.uint32
ALU = mybir.AluOpType
ACT = mybir.ActivationFunctionType
AX = mybir.AxisListType

P = 128
D = 1024
T = 512
NT = T // P
KD = D // P
EPS = 1e-6
BANK = 512
SLOT = 2048
NSLOT = 6
NEG = -1e30

RH, RDK = 4, 128
AH, DH, IH, IDH = 8, 64, 8, 32
TOPK_KEYS = min(256, T // 4)
EVEN_IN = 2984
QA, KA, VA, QI, KI, WI = 2048, 2560, 2624, 2688, 2944, 2976
BUCKETS, MAX_DIST = 32, 128
DIN, SH, SG, SN, SP = 2048, 32, 8, 128, 64
CONV_DIM = DIN + 2 * SG * SN
SSM_IN = DIN + CONV_DIM + SH
E, TOPK, FE = 64, 8, 256
ROUTED_SCALE = 2.5
PI2_A = 6.28125
PI2_B = float(np.float32(2 * math.pi - 6.28125) // np.float32(2.0 ** -21) * 2.0 ** -21)
PI2_C = 2 * math.pi - PI2_A - PI2_B
ROUND = 1.5 * 2.0 ** 23


def bucket_thresholds():
    exact = BUCKETS // 2
    n = np.arange(1, 4 * MAX_DIST)
    large = exact + (np.log(n.astype(np.float32) / exact) / math.log(MAX_DIST / exact)
                     * (BUCKETS - exact)).astype(np.int32)
    bucket = np.where(n < exact, n, np.minimum(large, BUCKETS - 1))
    return np.array([-1e9] + [n[bucket >= b][0] for b in range(1, BUCKETS)], np.float32)


def constants():
    i = np.arange(P, dtype=np.float64)
    log_g = np.log(1.0 - 2.0 ** (-5.0 - np.arange(RH)))
    rel = i[None, :] - i[:, None]
    decay = [np.where(rel >= 0, np.exp(g * np.maximum(rel, 0)), 0) for g in log_g]
    parts = {
        "ident": np.eye(P),
        "upper": (rel >= 0) * 1.0,
        "ones": np.ones((P, P)),
        "causal": np.where(rel > 0, NEG, 0.0),
        "decayT": np.concatenate(decay, 1),
        "xi": np.tile(np.concatenate([np.exp(g * (i + 1)) for g in log_g])[None], (P, 1)),
        "zeta": np.stack([np.exp(g * (P - 1 - i)) for g in log_g], 1),
        "inv": np.tile((np.float32(10000.0) ** (-np.arange(64, dtype=np.float32) / np.float32(64)))[None], (P, 1)),
        "thr": np.tile(bucket_thresholds(), 4)[:, None],
        "count": np.tile(i[None] + 1, (P, 1)),
        "row": i[:, None],
        "count_col": i[:, None] + 1,
        "minus_row": -i[:, None],
        "spare_row": T + i[:, None],
        "block_expert": np.tile(np.arange(3 * E) % E, (P, 1)),
        "block_base": np.tile(P * (1 + np.arange(3 * E) // E), (P, 1)),
        "quad": (np.arange(P)[:, None] // 32 == np.arange(4)[None]) * 1.0,
    }
    at, where = 0, {}
    for name, a in parts.items():
        where[name] = (at, at + a.shape[1])
        at += a.shape[1]
    return np.ascontiguousarray(np.concatenate(list(parts.values()), 1).astype(np.float32)), where


class Stage:
    pass


class Chain:

    def __init__(self, eng, sem, base=0):
        self.eng, self.sem, self.n = eng, sem, base

    def __call__(self, ins):
        self.n = self.n + 1
        ins.then_inc(self.sem, 1)
        self.eng.wait_ge(self.sem, self.n)


Item = namedtuple("Item", "s buf free full filled")


class Ring:

    def __init__(self, slots, full):
        self.slots, self.full = slots, full
        self.n, self.fills, self.release = 0, [0] * NSLOT, [None] * NSLOT

    def take(self, release):
        s = self.n % NSLOT
        self.n += 1
        self.fills[s] += 16
        free, self.release[s] = self.release[s], release
        return Item(s, self.slots[:, s, :], free, self.full[s], self.fills[s])


def load_slot(eng, item, dst, src):
    if item.free:
        eng.wait_ge(*item.free)
    eng.dma_start(dst, src).then_inc(item.full, 16)


def bank(g, b):
    return g.ps[:, b * BANK:(b + 1) * BANK]


def const(g, name):
    a, b = g.where[name]
    return g.consts[:, a:b]


def sems(g, stage, *names):
    new = [g.nc.alloc_semaphore(f"{stage}_{n}") for n in names]
    g.live += new
    return namedtuple("Semaphores", names)(*new)


def recycle(g):
    g.nc.clear_and_free_semaphores(g.live)
    g.nc.all_engine_barrier()
    g.live = []
    g.ring.release = [None] * NSLOT


def phase_ada_head(g):
    nc = g.nc
    s = sems(g, "ada", "table", "c", "bias", "cond", "mm", "added", "stored")
    with ExitStack() as local:
        sb = lambda n, sh, dt=F32: local.enter_context(nc.sbuf_tensor(f"ada_{n}", sh, dt))
        brow = sb("brow", [1, 2 * D])
        modrow = sb("modrow", [1, 2 * D])
        ccol = sb("ccol", [P, KD])
        NB = 2 * D // BANK
        items = [g.ring.take((s.mm, n // 2 + 1)) for n in range(2 * NB)]
        w = g.dram["ada_w"][0].rearrange("(p j) n -> p j n", j=KD)
        with nc.Block() as block:
            @block.sync
            def _(sp):
                sp.dma_start(ccol[:, :], g.dram["c"][0].rearrange("(p j) -> p j", j=KD)).then_inc(s.c, 16)
                for n, it in enumerate(items):
                    nb, half = n // 2, n % 2
                    load_slot(sp, it, it.buf.rearrange("p (j n) -> p j n", j=4),
                              w[:, 4 * half:4 * half + 4, nb * BANK:(nb + 1) * BANK])
                    if n == 1:
                        sp.dma_start(brow[:, :], g.dram["ada_b"][0:1, 0:2 * D]).then_inc(s.bias, 16)
                        sp.dma_start(g.consts[:, :], g.dram["consts_in"]).then_inc(s.table, 16)
                sp.wait_ge(s.added, NB)
                sp.dma_start(g.dram["mod"][0:1, 0:2 * D], modrow[:, :]).then_inc(s.stored, 16)
                sp.wait_ge(s.table, 16)
                sp.wait_ge(s.stored, 16)

            @block.scalar
            def _(act):
                act.wait_ge(s.c, 16)
                act.activation(g.cond[:, :], ccol[:, :], ACT.Silu).then_inc(s.cond, 1)

            @block.tensor
            def _(pe):
                pe.wait_ge(s.cond, 1)
                for nb in range(NB):
                    for half in range(2):
                        it = items[2 * nb + half]
                        pe.wait_ge(it.full, it.filled)
                        for j in range(4):
                            mm = pe.matmul(bank(g, nb)[0:1, :], g.cond[:, 4 * half + j:4 * half + j + 1],
                                           it.buf[:, j * BANK:(j + 1) * BANK], start=(half == 0 and j == 0),
                                           stop=(half == 1 and j == 3))
                    mm.then_inc(s.mm, 1)

            @block.vector
            def _(dve):
                dve.wait_ge(s.bias, 16)
                for nb in range(NB):
                    dve.wait_ge(s.mm, nb + 1)
                    at = slice(nb * BANK, (nb + 1) * BANK)
                    dve.tensor_tensor(modrow[:, at], bank(g, nb)[0:1, :], brow[:, at], ALU.add).then_inc(s.added, 1)


def phase_norm(g, tag, layer, x_dram, which, hT, rows_dram=None):
    nc = g.nc
    s = sems(g, f"norm_{tag}", "x0", "x1", "x2", "x3", "mod", "gate", "sq", "ms", "rstd", "xn", "tr", "scaled", "ev_a",
             "ev_v", "chain", "stored")
    with ExitStack() as local:
        sb = lambda n, sh, dt=F32: local.enter_context(nc.sbuf_tensor(f"norm_{tag}_{n}", sh, dt))
        x = sb("x", [P, NT, D])
        junk = sb("junk", [P, D])
        ss = sb("ss", [P, NT])
        ms = sb("ms", [P, NT])
        rstd = sb("rstd", [P, NT])
        gain = sb("gain", [P, KD])
        one_more = sb("one_more", [P, KD])
        scale, shift = g.scale[:, which, :], g.shift[:, which, :]
        ident = const(g, "ident")
        x_loaded = [s.x0, s.x1, s.x2, s.x3]
        with nc.Block() as block:
            @block.sync
            def _(sp):
                for t in range(NT):
                    sp.dma_start(x[:, t, :], x_dram[t * P:(t + 1) * P, :]).then_inc(x_loaded[t], 16)
                mod = lambda k: g.dram["mod"][layer, (3 * which + k) * D:(3 * which + k + 1) * D]
                norm_gain = g.dram["norm_ffn_g" if which else "norm_mix_g"][layer]
                for dst, src in ((shift, mod(0)), (one_more[:, :], mod(1)), (gain[:, :], norm_gain)):
                    sp.dma_start(dst, src.rearrange("(p j) -> p j", j=KD)).then_inc(s.mod, 16)
                if tag != "mix0":
                    sp.dma_start(g.gate_b[:, which, :], mod(2).partition_broadcast(P)).then_inc(s.gate, 16)
                if rows_dram is not None:
                    for t in range(NT):
                        sp.wait_ge(s.xn, t + 1)
                        sp.dma_start(rows_dram[t * P:(t + 1) * P, :], x[:, t, :]).then_inc(s.stored, 16)
                    sp.wait_ge(s.stored, 16 * NT)
                if tag != "mix0":
                    sp.wait_ge(s.gate, 16)

            @block.scalar
            def _(act):
                for t in range(NT):
                    act.wait_ge(x_loaded[t], 16)
                    if t:
                        act.wait_ge(s.sq, t)
                    act.activation(junk[:, :], x[:, t, :], ACT.Square, accum_out=ss[:, t:t + 1]).then_inc(s.sq, 1)
                act.wait_ge(s.ms, 1)
                act.activation(rstd[:, :], ms[:, :], ACT.Sqrt).then_inc(s.rstd, 1)
                act.wait_ge(s.scaled, 1)
                for t in range(NT):
                    act.wait_ge(s.tr, 2 * t + 2)
                    for j in range(4, KD):
                        act.activation(hT[:, j, t * P:(t + 1) * P], bank(g, 1 + 2 * (t % 2))[:, (j - 4) * P:(j - 3) * P],
                                       ACT.Identity, scale=scale[:, j:j + 1], bias=shift[:, j:j + 1]).then_inc(s.ev_a, 1)

            @block.vector
            def _(dve):
                link = Chain(dve, s.chain)
                dve.wait_ge(s.mod, 48)
                dve.scalar_tensor_tensor(scale, one_more[:, :], 1.0, gain[:, :], ALU.add, ALU.mult).then_inc(s.scaled, 1)
                dve.wait_ge(s.scaled, 1)
                dve.wait_ge(s.sq, NT)
                link(dve.tensor_scalar(ms[:, :], ss[:, :], 1.0 / D, EPS, ALU.mult, ALU.add))
                dve.reciprocal(ms[:, :], ms[:, :]).then_inc(s.ms, 1)
                dve.wait_ge(s.rstd, 1)

                def normalise(t):
                    dve.tensor_scalar(x[:, t, :], x[:, t, :], rstd[:, t:t + 1], None, ALU.mult).then_inc(s.xn, 1)

                normalise(0)
                normalise(1)
                for t in range(NT):
                    if t + 2 < NT:
                        normalise(t + 2)
                    dve.wait_ge(s.tr, 2 * t + 1)
                    for j in range(4):
                        dve.tensor_scalar(hT[:, j, t * P:(t + 1) * P], bank(g, 2 * (t % 2))[:, j * P:(j + 1) * P],
                                          scale[:, j:j + 1], shift[:, j:j + 1], ALU.mult, ALU.add).then_inc(s.ev_v, 1)

            @block.tensor
            def _(pe):
                for t in range(NT):
                    pe.wait_ge(s.xn, t + 1)
                    if t >= 2:
                        pe.wait_ge(s.ev_v, 4 * (t - 1))
                        pe.wait_ge(s.ev_a, 4 * (t - 1))
                    for j in range(KD):
                        tr = pe.transpose(bank(g, j // 4 + 2 * (t % 2))[:, (j % 4) * P:(j % 4 + 1) * P],
                                          x[:, t, j:D:KD], ident)
                        if j % 4 == 3:
                            tr.then_inc(s.tr, 1)


def phase_even_in(g, hT, proj):
    nc = g.nc
    s = sems(g, "even_in", "half", "mm", "ev_a", "ev_v", "sum", "total", "added", "bias_even", "bias_odd", "mod_even",
             "mod_odd", "ada0", "ada1", "ada2", "gate")
    w = g.dram["even_w_in"].rearrange("(p j) n -> p j n", j=KD)
    NB = -(-EVEN_IN // BANK)
    width = [min(BANK, EVEN_IN - nb * BANK) for nb in range(NB)]
    items = [g.ring.take((s.half, nb + 1) if h == 0 else (s.mm, 4 * nb + 4)) for nb in range(NB) for h in range(2)]
    blocks = [(0, k) for k in range(2, 6)] + [(1, k) for k in range(6)]
    PIECES, HELD = 4 * len(blocks), 3
    s_piece = (s.ada0, s.ada1, s.ada2)
    s_bias, s_mod = (s.bias_even, s.bias_odd), (s.mod_even, s.mod_odd)
    ADDS = KD * len(blocks)
    share = [ADDS * (nb + 1) // NB for nb in range(NB)]
    piece_at = lambda n: HELD + (2 * n - 1) * share[0] // 4

    def total_step(b):
        last = KD * b + KD - 1
        nb = min(i for i in range(NB) if share[i] > last)
        return 8 * nb + 2 + (last - (share[nb - 1] if nb else 0)) * 4 // share[0]

    total_at = [total_step(b) for b in range(len(blocks))]
    with ExitStack() as local:
        sb = lambda n, sh: local.enter_context(nc.sbuf_tensor(f"ada_{n}", sh, F32))
        piece = sb("piece", [P, HELD, 2 * D])
        acc = sb("acc", [P, 2, D])
        brow = sb("brow2", [1, 2, D])
        modrow = sb("modrow2", [1, 2, D])
        with nc.Block() as block:
            @block.sync
            def _(sp):
                def load_w(n):
                    it, nb, half = items[n], n // 2, n % 2
                    load_slot(sp, it, it.buf.rearrange("p (j n) -> p j n", j=4)[:, :, 0:width[nb]],
                              w[:, 4 * half:4 * half + 4, nb * BANK:nb * BANK + width[nb]])

                def load_ada(n):
                    b, q = n // 4, n % 4
                    layer, k = blocks[b]
                    if q == 3:
                        if b >= 2:
                            store(b - 2)
                        sp.dma_start(brow[:, b % 2, :], g.dram["ada_b"][layer:layer + 1, k * D:(k + 1) * D]).then_inc(s_bias[b % 2], 16)
                    if n >= HELD:
                        sp.wait_ge(s.sum, 2 * (n - HELD) + 2)
                    src = g.dram["ada_w"][layer].rearrange("(p j) n -> p j n", j=KD)
                    sp.dma_start(piece[:, n % HELD, :].rearrange("p (j n) -> p j n", j=2),
                                 src[:, 2 * q:2 * q + 2, k * D:(k + 1) * D]).then_inc(s_piece[n % HELD], 16)

                def store(b):
                    layer, k = blocks[b]
                    sp.wait_ge(s.added, b + 1)
                    sp.dma_start(g.dram["mod"][layer:layer + 1, k * D:(k + 1) * D], modrow[:, b % 2, :]).then_inc(s_mod[b % 2], 16)

                for n in range(2):
                    load_w(n)
                for n in range(HELD):
                    load_ada(n)
                for n in range(2, NSLOT):
                    load_w(n)
                late = NSLOT
                for n in range(HELD, PIECES):
                    load_ada(n)
                    while late < len(items) and n >= piece_at(late - NSLOT + 1):
                        load_w(late)
                        late += 1
                store(len(blocks) - 2)
                store(len(blocks) - 1)
                for par in range(2):
                    sp.wait_ge(s_mod[par], 16 * (len(blocks) // 2))
                sp.dma_start(g.gate_b[:, 0, :], g.dram["mod"][0, 2 * D:3 * D].partition_broadcast(P)).then_inc(s.gate, 16)
                sp.wait_ge(s.gate, 16)

            @block.tensor
            def _(pe):
                def total(b):
                    pe.wait_ge(s.sum, 8 * b + 8)
                    if b >= 2:
                        pe.wait_ge(s.added, b - 1)
                    for half in range(2):
                        mm = pe.matmul(bank(g, 4 + 2 * (b % 2) + half)[0:1, :], const(g, "ones")[:, 0:1],
                                       acc[:, b % 2, half * BANK:(half + 1) * BANK], start=True, stop=True)
                    mm.then_inc(s.total, 1)

                for nb in range(NB):
                    for half in range(2):
                        it = items[2 * nb + half]
                        pe.wait_ge(it.full, it.filled)
                        for t in range(NT):
                            if nb and half == 0:
                                pe.wait_ge(s.ev_a if t % 2 == 0 else s.ev_v, 2 * (nb - 1) + t // 2 + 1)
                            for j in range(4):
                                k = 4 * half + j
                                mm = pe.matmul(bank(g, t)[:, 0:width[nb]], hT[:, k, t * P:(t + 1) * P],
                                               it.buf[:, j * BANK:j * BANK + width[nb]], start=(k == 0), stop=(k == 7))
                            if half == 1:
                                mm.then_inc(s.mm, 1)
                            elif t == NT - 1:
                                mm.then_inc(s.half, 1)
                            for b in range(len(blocks)):
                                if total_at[b] == 8 * nb + 4 * half + t:
                                    total(b)

            @block.scalar
            def _(act):
                for nb in range(NB):
                    for t in range(0, NT, 2):
                        act.wait_ge(s.mm, 4 * nb + t + 1)
                        act.copy(proj[:, t, nb * BANK:nb * BANK + width[nb]], bank(g, t)[:, 0:width[nb]]).then_inc(s.ev_a, 1)

            @block.vector
            def _(dve):
                def accumulate(b, j):
                    n = 4 * b + j // 2
                    if j == 0 and b >= 2:
                        add_bias(b - 2)
                    if j % 2 == 0:
                        dve.wait_ge(s_piece[n % HELD], 16 * (n // HELD + 1))
                    w_j, c_j, a = piece[:, n % HELD, (j % 2) * D:(j % 2 + 1) * D], g.cond[:, j:j + 1], acc[:, b % 2, :]
                    if j == 0:
                        dve.tensor_scalar(a, w_j, c_j, None, ALU.mult).then_inc(s.sum, 1)
                    else:
                        dve.wait_ge(s.sum, KD * b + j)
                        dve.scalar_tensor_tensor(a, w_j, c_j, a, ALU.mult, ALU.add).then_inc(s.sum, 1)

                def add_bias(b):
                    dve.wait_ge(s_bias[b % 2], 16 * (b // 2 + 1))
                    dve.wait_ge(s.total, b + 1)
                    if b >= 2:
                        dve.wait_ge(s_mod[b % 2], 16 * (b // 2))
                    totals = g.ps[0:1, (4 + 2 * (b % 2)) * BANK:(6 + 2 * (b % 2)) * BANK]
                    dve.tensor_tensor(modrow[:, b % 2, :], totals, brow[:, b % 2, :], ALU.add).then_inc(s.added, 1)

                for nb in range(NB):
                    for q in range(share[nb - 1] if nb else 0, share[nb]):
                        accumulate(q // KD, q % KD)
                    for t in range(1, NT, 2):
                        dve.wait_ge(s.mm, 4 * nb + t + 1)
                        dve.tensor_copy(proj[:, t, nb * BANK:nb * BANK + width[nb]], bank(g, t)[:, 0:width[nb]]).then_inc(s.ev_v, 1)
                add_bias(len(blocks) - 2)
                add_bias(len(blocks) - 1)


def phase_even_prep(g, proj, m):
    nc = g.nc
    s = sems(g, "prep", "pos", "angle", "trig", "ms", "rstd", "gate", "chain", "done", "rep", "repd")
    with ExitStack() as local:
        sb = lambda n, sh, dt=F32: local.enter_context(nc.sbuf_tensor(f"prep_{n}", sh, dt))
        pos_i = sb("pos_i", [P, NT], I32)
        pos_f = sb("pos_f", [P, NT])
        ang = sb("ang", [P, NT, 64])
        turns = sb("turns", [P, NT, 64])
        arg = sb("arg", [P, 2, NT, 64])
        trig = sb("trig", [P, 2, NT, 64])
        trig_k = sb("trig_k", [P, 2, NT, 64])
        part = sb("part", [P, 4, NT, 256])
        ss = sb("ss", [P, NT, 9])
        rs = sb("rs", [P, NT, 9])
        q_gain = sb("q_gain", [P, 1])
        with nc.Block() as block:
            @block.sync
            def _(sp):
                sp.dma_start(pos_i[:, :], g.dram["positions"].rearrange("(t p) -> p t", p=P)).then_inc(s.pos, 16)
                sp.dma_start(m.ret_gain[:, :], g.dram["ret_norm_g"].rearrange("h d -> (h d)").partition_broadcast(P)).then_inc(s.pos, 16)
                for half in range(2):
                    at = slice(64 * half, 64 * half + 64)
                    sp.dma_start(q_gain[at, :], g.dram["dsa_q_g"].rearrange("(d a) -> d a", a=1)).then_inc(s.pos, 16)
                    sp.dma_start(m.k_gain[at, :], g.dram["dsa_k_g"].rearrange("(d a) -> d a", a=1)).then_inc(s.pos, 16)
                sp.dma_start(m.pos_row_i[:, :], g.dram["positions"].partition_broadcast(P)).then_inc(s.pos, 16)
                sp.dma_start(m.pos_quad_i[:, :], g.dram["positions"].rearrange("(g q) -> q g", q=4)).then_inc(s.pos, 16)
                for r in range(4):
                    sp.dma_start(m.rel[32 * r:32 * r + 32, 0, :], g.dram["rel_bias"]).then_inc(s.rep, 16)
                sp.wait_ge(s.repd, 1)
                for r in range(4):
                    sp.dma_start(m.rel[32 * r + 1:32 * r + 32, 1, :], g.dram["rel_bias"][0:BUCKETS - 1, :]).then_inc(s.rep, 16)
                sp.wait_ge(s.rep, 128)

            @block.scalar
            def _(act):
                act.activation(proj[:, :, 1536:2048], proj[:, :, 1536:2048], ACT.Silu).then_inc(s.gate, 1)
                act.wait_ge(s.angle, 1)
                act.activation(trig[:, :, :, :], arg[:, :, :, :], ACT.Sin).then_inc(s.trig, 1)
                act.wait_ge(s.ms, 1)
                act.activation(rs[:, :, :], ss[:, :, :], ACT.Sqrt).then_inc(s.rstd, 1)

            @block.vector
            def _(dve):
                link = Chain(dve, s.chain)
                dve.memset(m.rel[:, 1, :], 0.0).then_inc(s.repd, 1)
                dve.wait_ge(s.pos, 128)
                link(dve.tensor_copy(pos_f[:, :], pos_i[:, :]))
                for t in range(NT):
                    last = dve.tensor_scalar(ang[:, t, :], const(g, "inv"), pos_f[:, t:t + 1], None, ALU.mult)
                link(last)
                link(dve.tensor_scalar(turns[:, :, :], ang[:, :, :], 0.5 / math.pi, ROUND, ALU.mult, ALU.add))
                link(dve.tensor_scalar(turns[:, :, :], turns[:, :, :], -ROUND, None, ALU.add))
                for c in (PI2_A, PI2_B, PI2_C):
                    link(dve.scalar_tensor_tensor(ang[:, :, :], turns[:, :, :], -c, ang[:, :, :], ALU.mult, ALU.add))
                link(dve.tensor_scalar(arg[:, 0, :, :], ang[:, :, :], 3.1415925, -3.1415925, ALU.min, ALU.max))
                link(dve.tensor_scalar(ang[:, :, :], ang[:, :, :], 0.5 * math.pi, None, ALU.add))
                link(dve.tensor_scalar(turns[:, :, :], ang[:, :, :], math.pi, -2.0 * math.pi, ALU.is_gt, ALU.mult))
                link(dve.tensor_tensor(ang[:, :, :], ang[:, :, :], turns[:, :, :], ALU.add))
                dve.tensor_scalar(arg[:, 1, :, :], ang[:, :, :], 3.1415925, -3.1415925, ALU.min, ALU.max).then_inc(s.angle, 1)
                sq = part[:, 0:2, :, :].rearrange("p a t c -> p (a t c)").rearrange("p (t c) -> p t c", t=NT)
                link(dve.tensor_tensor(sq, proj[:, :, QA:KA], proj[:, :, QA:KA], ALU.mult))
                sqk = part[:, 2, :, 0:64]
                link(dve.tensor_tensor(sqk, proj[:, :, KA:VA], proj[:, :, KA:VA], ALU.mult))
                link(dve.tensor_reduce(ss[:, :, 0:8], sq.rearrange("p t (h d) -> p t h d", d=DH), AX.X, ALU.add))
                link(dve.tensor_reduce(ss[:, :, 8:9], sqk.unsqueeze(2), AX.X, ALU.add))
                link(dve.tensor_scalar(ss[:, :, :], ss[:, :, :], 1.0 / DH, EPS, ALU.mult, ALU.add))
                dve.reciprocal(ss[:, :, :], ss[:, :, :]).then_inc(s.ms, 1)
                dve.tensor_scalar(m.q_gain[:, :], q_gain[:, :], DH ** -0.5, None, ALU.mult).then_inc(s.done, 1)
                dve.tensor_scalar(m.wi[:, :, :], proj[:, :, WI:EVEN_IN], IH ** -0.5 * IDH ** -0.5, None, ALU.mult).then_inc(s.done, 1)
                dve.wait_ge(s.trig, 1)
                link(dve.tensor_scalar(trig_k[:, :, :, :], trig[:, :, :, :], RDK ** -0.5, None, ALU.mult))
                for base, tr in ((0, trig), (512, trig_k)):
                    v = proj[:, :, base:base + 512].rearrange("p t (h two d) -> p t h two d", two=2, d=64)
                    x1, x2 = v[:, :, :, 0, :], v[:, :, :, 1, :]
                    sn = tr[:, 0, :, :].unsqueeze(2).broadcast_to([P, NT, RH, 64])
                    cs = tr[:, 1, :, :].unsqueeze(2).broadcast_to([P, NT, RH, 64])
                    pt = [part[:, i, :, :].rearrange("p t (h d) -> p t h d", d=64) for i in range(4)]
                    for i, (x, f) in enumerate(((x1, cs), (x2, sn), (x1, sn), (x2, cs))):
                        link(dve.tensor_tensor(pt[i], x, f, ALU.mult))
                    link(dve.tensor_tensor(x1, pt[0], pt[1], ALU.subtract))
                    link(dve.tensor_tensor(x2, pt[2], pt[3], ALU.add))
                for t in range(NT):
                    k = proj[:, t, 512:1024].rearrange("p (h d) -> p h d", d=RDK)
                    dve.tensor_tensor(m.kz[:, t, :].rearrange("p (h d) -> p h d", d=RDK), k,
                                      const(g, "zeta").unsqueeze(2).broadcast_to([P, RH, RDK]), ALU.mult).then_inc(s.done, 1)
                dve.wait_ge(s.rstd, 1)
                qa = proj[:, :, QA:KA].rearrange("p t (h d) -> p t h d", d=DH)
                dve.tensor_tensor(qa, qa, rs[:, :, 0:8].unsqueeze(3).broadcast_to([P, NT, AH, DH]), ALU.mult).then_inc(s.done, 1)
                ka = proj[:, :, KA:VA]
                dve.tensor_tensor(ka, ka, rs[:, :, 8:9].broadcast_to([P, NT, DH]), ALU.mult).then_inc(s.done, 1)


def phase_even_turn(g, proj, m):
    nc = g.nc
    s = sems(g, "turn", "ki4", "tr", "ev_a", "ev_v")
    ident = const(g, "ident")
    groups = []
    for h in range(RH):
        groups.append(("q", h, [proj[:, t, h * 128:(h + 1) * 128] for t in range(NT)], P))
    for h in range(RH):
        groups.append(("k", h, [proj[:, t, 512 + h * 128:512 + (h + 1) * 128] for t in range(NT)], P))
    for r in range(AH // 2):
        groups.append(("qa", r, [proj[:, t, QA + r * 128:QA + (r + 1) * 128] for t in range(NT)], P))
    groups.append(("ka", 0, [proj[:, t, KA:VA] for t in range(NT)], DH))
    for r in range(2):
        groups.append(("qi", r, [proj[:, t, QI + r * 128:QI + (r + 1) * 128] for t in range(NT)], P))
    groups.append(("ki", 0, [m.ki4[:, t, :] for t in range(NT)], P))
    copies_a = {"q": 1, "qa": 2}
    copies_v = {"q": 1, "k": 1, "ka": 1, "qi": 1, "ki": 1}
    done_a, done_v, na, nv = [], [], 0, 0
    for kind, *_ in groups:
        na += copies_a.get(kind, 0)
        nv += copies_v.get(kind, 0)
        done_a.append(na)
        done_v.append(nv)
    with nc.Block() as block:
        @block.gpsimd
        def _(pool):
            ki = proj[:, :, KI:WI]
            for r in range(4):
                pool.tensor_copy(m.ki4[:, :, r * IDH:(r + 1) * IDH], ki).then_inc(s.ki4, 1)

        @block.tensor
        def _(pe):
            for n, (kind, r, srcs, rows) in enumerate(groups):
                if n >= 8:
                    if done_a[n - 8]:
                        pe.wait_ge(s.ev_a, done_a[n - 8])
                    pe.wait_ge(s.ev_v, done_v[n - 8])
                if kind == "ki":
                    pe.wait_ge(s.ki4, 4)
                for t in range(NT):
                    tr = pe.transpose(bank(g, n % 8)[0:rows, t * P:(t + 1) * P], srcs[t], ident)
                tr.then_inc(s.tr, 1)

        @block.scalar
        def _(act):
            for n, (kind, r, _, rows) in enumerate(groups):
                b = bank(g, n % 8)
                if kind in copies_a:
                    act.wait_ge(s.tr, n + 1)
                if kind == "q":
                    act.copy(m.qT[:, r, :], b).then_inc(s.ev_a, 1)
                if kind == "qa":
                    for odd in range(2):
                        at = slice(64 * odd, 64 * odd + 64)
                        act.activation(m.qaT[:, :, 2 * r + odd], b[at, :], ACT.Copy,
                                       scale=m.q_gain[at, :]).then_inc(s.ev_a, 1)

        @block.vector
        def _(dve):
            for n, (kind, r, _, rows) in enumerate(groups):
                b = bank(g, n % 8)
                if kind == "q":
                    dve.wait_ge(s.ev_a, n + 1)
                    xi = const(g, "xi")[:, r * P:(r + 1) * P].unsqueeze(1).broadcast_to([P, NT, P])
                    dve.tensor_tensor(m.qxT[:, r, :].rearrange("p (t n) -> p t n", t=NT),
                                      m.qT[:, r, :].rearrange("p (t n) -> p t n", t=NT), xi, ALU.mult).then_inc(s.ev_v, 1)
                elif kind in copies_v:
                    dve.wait_ge(s.tr, n + 1)
                if kind == "k":
                    dve.tensor_copy(m.kT[:, r, :], b).then_inc(s.ev_v, 1)
                if kind == "ka":
                    dve.tensor_scalar(m.kaT[:, :], b[0:DH, :], m.k_gain[0:DH, :], None, ALU.mult).then_inc(s.ev_v, 1)
                if kind == "qi":
                    dve.tensor_copy(m.qiT[:, r, :], b).then_inc(s.ev_v, 1)
                if kind == "ki":
                    dve.tensor_copy(m.kiT[:, :], b).then_inc(s.ev_v, 1)


def phase_retention(g, proj, m, yT):
    nc = g.nc
    s = sems(g, "ret", "inner", "decayed", "y", "u", "state", "y_out", "chain", "ms", "rstd", "yn", "tr", "ev")
    log_g = np.log(1.0 - 2.0 ** (-5.0 - np.arange(RH)))
    with ExitStack() as local:
        sb = lambda n, sh, dt=F32: local.enter_context(nc.sbuf_tensor(f"ret_{n}", sh, dt))
        inner = sb("inner", [P, 2, RH * P])
        state = sb("state", [P, RH, P])
        y, sq = proj[:, :, 0:512], proj[:, :, 512:1024]
        ss = sb("ss", [P, NT, RH])
        rs = sb("rs", [P, NT, RH])
        with nc.Block() as block:
            @block.tensor
            def _(pe):
                def scores(c):
                    if c >= 2:
                        pe.wait_ge(s.decayed, c - 1)
                    for h in range(RH):
                        mm = pe.matmul(bank(g, c % 2)[:, h * P:(h + 1) * P], m.kT[:, h, c * P:(c + 1) * P],
                                       m.qT[:, h, c * P:(c + 1) * P], start=True, stop=True)
                    mm.then_inc(s.inner, 1)
                    for h in range(RH):
                        mm = pe.matmul(bank(g, 4 + c % 2)[:, h * P:(h + 1) * P], m.kz[:, c, h * P:(h + 1) * P],
                                       proj[:, c, 1024 + h * P:1024 + (h + 1) * P], start=True, stop=True)
                    mm.then_inc(s.u, 1)

                scores(0)
                for c in range(NT):
                    pe.wait_ge(s.decayed, c + 1)
                    if c >= 2:
                        pe.wait_ge(s.y_out, c - 1)
                    if c:
                        pe.wait_ge(s.state, RH * c)
                    for h in range(RH):
                        yb = bank(g, 2 + c % 2)[:, h * P:(h + 1) * P]
                        mm = pe.matmul(yb, inner[:, c % 2, h * P:(h + 1) * P],
                                       proj[:, c, 1024 + h * P:1024 + (h + 1) * P], start=True, stop=(c == 0))
                        if c:
                            mm = pe.matmul(yb, m.qxT[:, h, c * P:(c + 1) * P], state[:, h, :], start=False, stop=True)
                    mm.then_inc(s.y, 1)
                    if c + 1 < NT:
                        scores(c + 1)
                for h in range(RH):
                    pe.wait_ge(s.yn, NT)
                    for t in range(NT):
                        tr = pe.transpose(bank(g, h)[:, t * P:(t + 1) * P], y[:, t, h * P:(h + 1) * P], const(g, "ident"))
                    tr.then_inc(s.tr, 1)

            @block.scalar
            def _(act):
                for c in range(NT):
                    act.wait_ge(s.y, c + 1)
                    act.copy(y[:, c, :], bank(g, 2 + c % 2)).then_inc(s.y_out, 1)
                act.wait_ge(s.ms, 1)
                act.activation(rs[:, :, :], ss[:, :, :], ACT.Sqrt).then_inc(s.rstd, 1)
                for h in range(RH):
                    act.wait_ge(s.tr, h + 1)
                    act.copy(yT[:, h, :], bank(g, h)).then_inc(s.ev, 1)

            @block.vector
            def _(dve):
                link = Chain(dve, s.chain)
                for c in range(NT):
                    dve.wait_ge(s.inner, c + 1)
                    dve.tensor_tensor(inner[:, c % 2, :], bank(g, c % 2), const(g, "decayT"), ALU.mult).then_inc(s.decayed, 1)
                    if c == NT - 1:
                        break
                    dve.wait_ge(s.u, c + 1)
                    dve.wait_ge(s.y, c + 1)
                    if c:
                        dve.wait_ge(s.state, RH * c)
                    for h in range(RH):
                        u = bank(g, 4 + c % 2)[:, h * P:(h + 1) * P]
                        if c == 0:
                            dve.tensor_copy(state[:, h, :], u).then_inc(s.state, 1)
                        else:
                            dve.scalar_tensor_tensor(state[:, h, :], state[:, h, :], float(np.exp(log_g[h] * P)), u,
                                                     ALU.mult, ALU.add).then_inc(s.state, 1)
                dve.wait_ge(s.y_out, NT)
                link(dve.tensor_tensor(sq[:, :, :], y[:, :, :], y[:, :, :], ALU.mult))
                link(dve.tensor_reduce(ss[:, :, :], sq.rearrange("p t (h d) -> p t h d", d=P), AX.X, ALU.add))
                link(dve.tensor_scalar(ss[:, :, :], ss[:, :, :], 1.0 / P, EPS, ALU.mult, ALU.add))
                dve.reciprocal(ss[:, :, :], ss[:, :, :]).then_inc(s.ms, 1)
                link(dve.tensor_tensor(sq[:, :, :], proj[:, :, 1536:2048],
                                       m.ret_gain[:, :].unsqueeze(1).broadcast_to([P, NT, RH * P]), ALU.mult))
                dve.wait_ge(s.rstd, 1)
                yv = y.rearrange("p t (h d) -> p t h d", d=P)
                link(dve.tensor_tensor(yv, yv, rs[:, :, :].unsqueeze(3).broadcast_to([P, NT, RH, P]), ALU.mult))
                for t in range(NT):
                    dve.tensor_tensor(y[:, t, :], y[:, t, :], sq[:, t, :], ALU.mult).then_inc(s.yn, 1)


def phase_index(g, m):
    nc = g.nc
    s = sems(g, "index", "mm", "relu", "added", "chain", "quad", "quadT", "pos", "posT")
    with ExitStack() as local:
        sb = lambda n, sh, dt=F32: local.enter_context(nc.sbuf_tensor(f"index_{n}", sh, dt))
        relu = sb("relu", [P, 2, T])
        score = sb("score", [P, T])
        best = sb("best", [P, 8])
        quadT = sb("quadT", [4, P])
        pos_quad = sb("pos_quad", [4, P])
        delta = sb("delta", [P, AH])
        rest = sb("rest", [P, 4, AH])
        with nc.Block() as block:
            @block.tensor
            def _(pe):
                pe.transpose(bank(g, 7)[0:4, 0:P], const(g, "quad"), const(g, "ident")).then_inc(s.quad, 1)
                n = 0
                for qb in range(1, NT):
                    w = P * (qb + 1)
                    for h in range(IH):
                        if n >= 4:
                            pe.wait_ge(s.relu, n - 3)
                        at = slice(32 * (h % 4), 32 * (h % 4) + 32)
                        pe.matmul(bank(g, n % 4)[:, 0:w], m.qiT[at, h // 4, qb * P:(qb + 1) * P], m.kiT[at, 0:w],
                                  start=True, stop=True).then_inc(s.mm, 1)
                        n += 1
                    if qb == 1:
                        pe.wait_ge(s.quadT, 1)
                        pe.matmul(bank(g, 7)[:, P:2 * P], quadT[:, :], pos_quad[:, :], start=True, stop=True).then_inc(s.pos, 1)

            @block.scalar
            def _(act):
                for n in range(IH * (NT - 1)):
                    w = P * (n // IH + 2)
                    act.wait_ge(s.mm, n + 1)
                    if n >= 2:
                        act.wait_ge(s.added, n - 1)
                    act.activation(relu[:, n % 2, 0:w], bank(g, n % 4)[:, 0:w], ACT.Relu).then_inc(s.relu, 1)

            @block.vector
            def _(dve):
                link = Chain(dve, s.chain)
                link(dve.tensor_copy(pos_quad[:, :], m.pos_quad_i[:, :]))
                link(dve.tensor_copy(m.pos_row[:, :], m.pos_row_i[:, :]))
                dve.wait_ge(s.quad, 1)
                dve.tensor_copy(quadT[:, :], bank(g, 7)[0:4, 0:P]).then_inc(s.quadT, 1)
                link(dve.tensor_tensor(delta[:, :], m.rel[:, 0, :], m.rel[:, 1, :], ALU.subtract))
                link(dve.tensor_tensor(rest[:, :, :], delta[:, :].unsqueeze(1).broadcast_to([P, 4, AH]),
                                       const(g, "quad").unsqueeze(2).broadcast_to([P, 4, AH]), ALU.mult))
                for i in range(3):
                    d = m.delta3[:, i, :].rearrange("p (q h) -> p q h", q=4)
                    link(dve.tensor_copy(d, rest[:, :, :]))
                    if i < 2:
                        link(dve.tensor_tensor(rest[:, :, :], rest[:, :, :], d, ALU.subtract))
                link(dve.tensor_copy(m.expand[:, :].rearrange("p (q h) -> p q h", h=AH),
                                     const(g, "ident").unsqueeze(2).broadcast_to([P, P, AH])))
                link(dve.tensor_copy(m.mask[:, 0, 0:P], const(g, "causal")))
                n = 0
                for qb in range(1, NT):
                    w = P * (qb + 1)
                    sc = score[:, 0:w]
                    for h in range(IH):
                        dve.wait_ge(s.relu, n + 1)
                        if h:
                            dve.wait_ge(s.added, n)
                            dve.scalar_tensor_tensor(sc, relu[:, n % 2, 0:w], m.wi[:, qb, h:h + 1], sc,
                                                     ALU.mult, ALU.add).then_inc(s.added, 1)
                        else:
                            dve.tensor_scalar(sc, relu[:, n % 2, 0:w], m.wi[:, qb, 0:1], None, ALU.mult).then_inc(s.added, 1)
                        n += 1
                    if qb == 1:
                        dve.wait_ge(s.pos, 1)
                        link(dve.tensor_scalar(m.pos_edge[:, :], bank(g, 7)[:, P:2 * P], const(g, "thr"), None, ALU.subtract))
                    dve.wait_ge(s.added, n)
                    link(dve.tensor_tensor(score[:, w - P:w], score[:, w - P:w], const(g, "causal"), ALU.add))
                    for r in range(TOPK_KEYS // 8):
                        link(dve.max(best[:, :], sc))
                        link(dve.match_replace(sc, best[:, :], sc, -3e38))
                    link(dve.tensor_scalar(m.mask[:, qb, 0:w], sc, -2e38, NEG, ALU.is_gt, ALU.mult))


def phase_attention(g, proj, m, yT):
    nc = g.nc
    s = sems(g, "att", "steps", "logits", "max", "exp", "prob", "turn", "turned", "out", "stored", "chain")
    NTILE = T // 16
    with ExitStack() as local:
        sb = lambda n, sh, dt=F32: local.enter_context(nc.sbuf_tensor(f"att_{n}", sh, dt))
        steps = sb("steps", [P, 2, 4, T], BF16)
        prob = sb("prob", [P, 2, T])
        probT = sb("probT", [P, 2, T])
        nmax = sb("nmax", [P, 2])
        total = sb("total", [P, 2])
        inv = sb("inv", [P, 2])
        with nc.Block() as block:
            @block.tensor
            def _(pe):
                def logits(i):
                    w, b = P * (i // 8 + 1), bank(g, i % 2)
                    if i >= 2:
                        pe.wait_ge(s.exp, i - 1)
                    pe.matmul(b[:, 0:w], m.qaT[:, 16 * i:16 * i + 16, :].rearrange("p q h -> p (q h)"), m.kaT[:, 0:w],
                              start=True, stop=False)
                    pe.matmul(b[:, 0:w], m.expand[:, (i % 8) * P:(i % 8 + 1) * P], m.mask[:, i // 8, 0:w],
                              start=False, stop=False)
                    pe.wait_ge(s.steps, i + 1)
                    for j in range(4):
                        for part in range(3):
                            mm = pe.matmul(b[32 * j:32 * j + 32, 0:w], m.delta3[:, part, :], steps[:, i % 2, j, 0:w],
                                           start=False, stop=(part == 2))
                    mm.then_inc(s.logits, 1)

                def turn(i):
                    w, b = P * (i // 8 + 1), bank(g, 2 + i % 2)
                    pe.wait_ge(s.prob, i + 1)
                    if i >= 2:
                        pe.wait_ge(s.turned, i - 1)
                    for k in range(w // P):
                        tr = pe.transpose(b[:, k * P:(k + 1) * P], prob[:, i % 2, k * P:(k + 1) * P], const(g, "ident"))
                    tr.then_inc(s.turn, 1)

                def values(i):
                    nk, b = i // 8 + 1, bank(g, 4 + i % 2)
                    pe.wait_ge(s.turned, i + 1)
                    if i >= 2:
                        pe.wait_ge(s.stored, 2 * (i - 1))
                    for k in range(nk):
                        mm = pe.matmul(b[0:DH, 0:P], proj[:, k, VA:QI], probT[:, i % 2, k * P:(k + 1) * P],
                                       start=(k == 0), stop=(k == nk - 1))
                    mm.then_inc(s.out, 1)

                for i in range(NTILE + 2):
                    if i < NTILE:
                        logits(i)
                    if 1 <= i <= NTILE:
                        turn(i - 1)
                    if i >= 2:
                        values(i - 2)

            @block.scalar
            def _(act):
                def exp(i):
                    w = P * (i // 8 + 1)
                    act.wait_ge(s.max, i + 1)
                    if i >= 2:
                        act.wait_ge(s.turn, i - 1)
                    act.activation(prob[:, i % 2, 0:w], bank(g, i % 2)[:, 0:w], ACT.Exp, bias=nmax[:, i % 2:i % 2 + 1],
                                   accum_out=total[:, i % 2:i % 2 + 1]).then_inc(s.exp, 1)

                def turned(i):
                    w = P * (i // 8 + 1)
                    act.wait_ge(s.turn, i + 1)
                    if i >= 2:
                        act.wait_ge(s.out, i - 1)
                    act.copy(probT[:, i % 2, 0:w], bank(g, 2 + i % 2)[:, 0:w]).then_inc(s.turned, 1)

                def store(i):
                    act.wait_ge(s.out, i + 1)
                    o = bank(g, 4 + i % 2)[0:DH, 0:P].rearrange("p (q h two) -> p h two q", h=4, two=2)
                    for odd in range(2):
                        act.copy(yT[64 * odd:64 * odd + 64, 4:8, 16 * i:16 * i + 16], o[:, :, odd, :]).then_inc(s.stored, 1)

                for i in range(NTILE + 3):
                    if i < NTILE:
                        exp(i)
                    if 1 <= i <= NTILE:
                        turned(i - 1)
                    if 3 <= i:
                        store(i - 3)

            @block.vector
            def _(dve):
                link = Chain(dve, s.chain)

                def make_steps(i):
                    w = P * (i // 8 + 1)
                    if i >= 2:
                        dve.wait_ge(s.logits, i - 1)
                    for j in range(4):
                        last = dve.tensor_scalar(steps[:, i % 2, j, 0:w], m.pos_row[:, 0:w],
                                                 m.pos_edge[:, 4 * i + j:4 * i + j + 1], None, ALU.is_le)
                    last.then_inc(s.steps, 1)

                make_steps(0)
                for i in range(NTILE):
                    w = P * (i // 8 + 1)
                    if i + 1 < NTILE:
                        make_steps(i + 1)
                    dve.wait_ge(s.logits, i + 1)
                    link(dve.reduce_max(nmax[:, i % 2:i % 2 + 1], bank(g, i % 2)[:, 0:w], AX.X))
                    dve.tensor_scalar(nmax[:, i % 2:i % 2 + 1], nmax[:, i % 2:i % 2 + 1], -1.0, None, ALU.mult).then_inc(s.max, 1)
                    dve.wait_ge(s.exp, i + 1)
                    link(dve.reciprocal(inv[:, i % 2:i % 2 + 1], total[:, i % 2:i % 2 + 1]))
                    dve.tensor_scalar(prob[:, i % 2, 0:w], prob[:, i % 2, 0:w], inv[:, i % 2:i % 2 + 1], None,
                                      ALU.mult).then_inc(s.prob, 1)


def phase_out(g, tag, yT, w_view, kc, x_dram, out_dram):
    nc = g.nc
    s = sems(g, f"out_{tag}", "x", "half", "mm", "gated", "added", "store")
    nslots = kc // 4
    last_of = lambda nb: (s.mm, 4 * nb + 4)
    items = [g.ring.take((s.half, nb * (nslots - 1) + q + 1) if q < nslots - 1 else last_of(nb))
             for nb in range(2) for q in range(nslots)]
    with ExitStack() as local:
        x = local.enter_context(nc.sbuf_tensor(f"out_{tag}_x", [P, NT, D], F32))
        with nc.Block() as block:
            @block.sync
            def _(sp):
                for n, it in enumerate(items):
                    nb, q = n // nslots, n % nslots
                    load_slot(sp, it, it.buf.rearrange("p (j n) -> p j n", j=4),
                              w_view[:, 4 * q:4 * q + 4, nb * BANK:(nb + 1) * BANK])
                    if n == 0:
                        sp.dma_start(x[:, :, :], x_dram[0:T, :].rearrange("(t p) n -> p t n", p=P)).then_inc(s.x, 16)
                for t in range(NT):
                    sp.wait_ge(s.added, NT + t + 1)
                    sp.dma_start(out_dram[t * P:(t + 1) * P, :], x[:, t, :]).then_inc(s.store, 16)
                sp.wait_ge(s.store, 16 * NT)

            @block.tensor
            def _(pe):
                for nb in range(2):
                    for q in range(nslots):
                        it = items[nb * nslots + q]
                        pe.wait_ge(it.full, it.filled)
                        for t in range(NT):
                            for j in range(4):
                                k = 4 * q + j
                                mm = pe.matmul(bank(g, 4 * nb + t), yT[:, k, t * P:(t + 1) * P],
                                               it.buf[:, j * BANK:(j + 1) * BANK], start=(k == 0), stop=(k == kc - 1))
                            if q == nslots - 1:
                                mm.then_inc(s.mm, 1)
                            elif t == NT - 1:
                                mm.then_inc(s.half, 1)

            @block.vector
            def _(dve):
                dve.wait_ge(s.x, 16)
                for nb in range(2):
                    at = slice(nb * BANK, (nb + 1) * BANK)
                    for t in range(NT):
                        n = 4 * nb + t
                        dve.wait_ge(s.mm, n + 1)
                        dve.tensor_tensor(bank(g, n), bank(g, n), g.gate_b[:, 0, at], ALU.mult).then_inc(s.gated, 1)
                        dve.wait_ge(s.gated, n + 1)
                        dve.tensor_tensor(x[:, t, at], bank(g, n), x[:, t, at], ALU.add).then_inc(s.added, 1)


def phase_router(g, tag, layer, hT, r):
    nc = g.nc
    s = sems(g, f"router_{tag}", "w", "logits", "exp", "chain", "sel", "counted", "listed", "spread")
    with ExitStack() as local:
        sb = lambda n, sh, dt=F32: local.enter_context(nc.sbuf_tensor(f"router_{tag}_{n}", sh, dt))
        w = sb("w", [P, KD, E])
        bias = sb("bias", [P, E])
        score = sb("score", [P, NT, E])
        biased = sb("biased", [P, NT, E])
        left = sb("left", [P, NT, E])
        best = sb("best", [P, NT, 8])
        total = sb("total", [P, NT])
        rest = sb("rest", [P, NT, E])
        more = sb("more", [P, 3 * E])
        rank = sb("rank", [P, 3 * E])
        nothing = sb("nothing", [P, 3 * E])
        junk = sb("junk", [P, 3 * E])
        which = sb("which", [P, 2])
        spreadx = sb("spreadx", [P, 2, 32])
        with nc.Block() as block:
            @block.sync
            def _(sp):
                sp.dma_start(w[:, :, :], g.dram["router_w"][layer].rearrange("(p j) n -> p j n", j=KD)).then_inc(s.w, 16)
                sp.dma_start(bias[:, :], g.dram["router_b"][layer].partition_broadcast(P)).then_inc(s.w, 16)

            @block.tensor
            def _(pe):
                pe.wait_ge(s.w, 32)
                for t in range(NT):
                    for j in range(KD):
                        mm = pe.matmul(bank(g, 0)[:, t * E:(t + 1) * E], hT[:, j, t * P:(t + 1) * P], w[:, j, :],
                                       start=(j == 0), stop=(j == KD - 1))
                mm.then_inc(s.logits, 1)
                pe.wait_ge(s.sel, 1)
                for t in range(NT):
                    for u in range(t + 1):
                        pe.matmul(bank(g, 1)[:, t * E:(t + 1) * E], const(g, "ones" if u < t else "upper"), r.sel[:, u, :],
                                  start=(u == 0), stop=(u == t))
                for u in range(NT):
                    mm = pe.matmul(bank(g, 1)[:, NT * E:(NT + 1) * E], const(g, "ones"), r.sel[:, u, :],
                                   start=(u == 0), stop=(u == NT - 1))
                mm.then_inc(s.counted, 1)
                pe.wait_ge(s.listed, 1)
                pe.matmul(bank(g, 2)[:, 0:64], const(g, "ones"), spreadx[:, :, :].rearrange("p w x -> p (w x)"),
                          start=True, stop=True).then_inc(s.spread, 1)

            @block.scalar
            def _(act):
                act.wait_ge(s.logits, 1)
                act.activation(score[:, :, :].rearrange("p t e -> p (t e)"), bank(g, 0)[:, 0:NT * E], ACT.Exp,
                               scale=-1.0).then_inc(s.exp, 1)

            @block.vector
            def _(dve):
                link = Chain(dve, s.chain)
                dve.wait_ge(s.w, 32)
                dve.wait_ge(s.exp, 1)
                link(dve.tensor_scalar(score[:, :, :], score[:, :, :], 1.0, None, ALU.add))
                link(dve.reciprocal(score[:, :, :], score[:, :, :]))
                link(dve.tensor_tensor(biased[:, :, :], score[:, :, :], bias[:, :].unsqueeze(1).broadcast_to([P, NT, E]), ALU.add))
                for t in range(NT):
                    last = dve.max(best[:, t, :], biased[:, t, :])
                link(last)
                for t in range(NT):
                    last = dve.match_replace(left[:, t, :], best[:, t, :], biased[:, t, :], NEG)
                link(last)
                dve.tensor_scalar(r.sel[:, :, :], left[:, :, :], NEG / 2, None, ALU.is_lt).then_inc(s.sel, 1)
                dve.wait_ge(s.sel, 1)
                link(dve.tensor_tensor(r.gates[:, :, :], r.sel[:, :, :], score[:, :, :], ALU.mult))
                link(dve.tensor_reduce(total[:, :], r.gates[:, :, :], AX.X, ALU.add))
                link(dve.reciprocal(total[:, :], total[:, :]))
                link(dve.tensor_scalar(total[:, :], total[:, :], ROUTED_SCALE, None, ALU.mult))
                link(dve.tensor_tensor(r.gates[:, :, :], r.gates[:, :, :], total[:, :].unsqueeze(2).broadcast_to([P, NT, E]), ALU.mult))
                dve.wait_ge(s.counted, 1)
                link(dve.tensor_tensor(r.pos[:, :, :], bank(g, 1)[:, 0:NT * E].rearrange("p (t e) -> p t e", t=NT),
                                       r.sel[:, :, :], ALU.mult))
                view = lambda a: a.rearrange("p (k e) -> p k e", k=3)
                link(dve.memset(nothing[:, :], 0.0))
                link(dve.tensor_tensor(view(more[:, :]), bank(g, 1)[:, NT * E:(NT + 1) * E].unsqueeze(1).broadcast_to([P, 3, E]),
                                       view(const(g, "block_base")), ALU.is_gt))
                link(dve.tensor_tensor_scan(rank[:, :], more[:, :], nothing[:, :], 0.0, ALU.add, ALU.add))
                link(dve.tensor_copy(r.extra_blocks[:, :], rank[:, 3 * E - 1:3 * E]))
                link(dve.tensor_tensor(rank[:, :], rank[:, :], more[:, :], ALU.mult))
                link(dve.tensor_scalar(rank[:, :], rank[:, :], const(g, "count_col"), None, ALU.is_equal))
                for i, name in enumerate(("block_expert", "block_base")):
                    link(dve.tensor_tensor(junk[:, :], rank[:, :], const(g, name), ALU.mult))
                    link(dve.reduce_sum(which[:, i:i + 1], junk[:, :], AX.X))
                link(dve.tensor_scalar(spreadx[:, 0, :], const(g, "ident")[:, 0:32], which[:, 0:1], None, ALU.mult))
                dve.tensor_scalar(spreadx[:, 1, :], const(g, "ident")[:, 0:32], which[:, 1:2], None, ALU.mult).then_inc(s.listed, 1)
                dve.wait_ge(s.spread, 1)
                link(dve.tensor_copy(r.extra_expert[:, :], bank(g, 2)[:, 0:32]))
                link(dve.tensor_copy(r.extra_base[:, :], bank(g, 2)[:, 32:64]))
                tab = r.table
                link(dve.tensor_copy(tab[:, :, :, 0], const(g, "row").unsqueeze(2).broadcast_to([P, NT, E])))
                for t in range(NT):
                    dve.memset(tab[:, t, :, 1], float(P * t - T))
                dve.memset(tab[:, :, :, 2], 1.0)
                link(dve.tensor_copy(rest[:, :, :], r.gates[:, :, :]))
                for i in range(3):
                    link(dve.tensor_copy(tab[:, :, :, 3 + i], rest[:, :, :]))
                    if i < 2:
                        link(dve.tensor_tensor(rest[:, :, :], rest[:, :, :], tab[:, :, :, 3 + i], ALU.subtract))


def phase_shared(g, tag, layer, hT, r, x_dram, out_dram):
    nc = g.nc
    s = sems(g, f"shared_{tag}", "up", "silu", "hidden", "down", "x", "gated", "added", "store", "zero", "onehot", "known",
             "chain")
    with ExitStack() as local:
        sb = lambda n, sh, dt=F32: local.enter_context(nc.sbuf_tensor(f"shared_{tag}_{n}", sh, dt))
        silu = sb("silu", [P, 2, T])
        hidden = sb("hidden", [P, 2, T])
        x = sb("x", [P, NT, D])
        zeros = sb("zeros", [P, D])
        onehot = sb("onehot", [P, 2, NT, P], BF16)
        facts = sb("facts", [P, E, 6])
        part = sb("part", [P, E])
        w1, w3, w2 = g.ring.take((s.up, 2)), g.ring.take((s.up, 4)), g.ring.take((s.down, 8))
        with nc.Block() as block:
            @block.sync
            def _(sp):
                load_slot(sp, w1, w1.buf.rearrange("p (j n) -> p j n", j=KD), g.dram["sh_w1"][layer].rearrange("(p j) n -> p j n", j=KD))
                load_slot(sp, w3, w3.buf.rearrange("p (j n) -> p j n", j=KD), g.dram["sh_w3"][layer].rearrange("(p j) n -> p j n", j=KD))
                load_slot(sp, w2, w2.buf.rearrange("p (j n) -> p j n", j=2), g.dram["sh_w2"][layer].rearrange("(j p) n -> p j n", p=P))
                sp.dma_start(x[:, :, :], x_dram[0:T, :].rearrange("(t p) n -> p t n", p=P)).then_inc(s.x, 16)
                sp.wait_ge(s.zero, 1)
                sp.dma_start(out_dram[T:T + P, :], zeros[:, :]).then_inc(s.store, 16)
                sp.dma_start(g.dram["rows"][T:T + P, :], zeros[:, :]).then_inc(s.store, 16)
                for t in range(NT):
                    sp.wait_ge(s.added, 2 * t + 2)
                    sp.dma_start(out_dram[t * P:(t + 1) * P, :], x[:, t, :]).then_inc(s.store, 16)
                sp.wait_ge(s.store, 16 * (NT + 2))

            @block.gpsimd
            def _(pool):
                pool.memset(zeros[:, :], 0.0).then_inc(s.zero, 1)

            @block.tensor
            def _(pe):
                for m in range(4):
                    it = w1 if m < 2 else w3
                    if m % 2 == 0:
                        pe.wait_ge(it.full, it.filled)
                    for j in range(KD):
                        mm = pe.matmul(bank(g, m), it.buf[:, j * FE + (m % 2) * P:j * FE + (m % 2 + 1) * P],
                                       hT[:, j, :], start=(j == 0), stop=(j == KD - 1))
                    mm.then_inc(s.up, 1)
                pe.wait_ge(w2.full, w2.filled)
                pe.wait_ge(s.hidden, 2)
                for q in range(8):
                    b = bank(g, 4 + q % 3)
                    if q >= 3:
                        pe.wait_ge(s.added, q - 2)
                    for k in range(2):
                        mm = pe.matmul(b, hidden[:, k, (q // 2) * P:(q // 2 + 1) * P],
                                       w2.buf[:, k * D + (q % 2) * BANK:k * D + (q % 2 + 1) * BANK],
                                       start=(k == 0), stop=(k == 1))
                    mm.then_inc(s.down, 1)
                with pe.Fori(0, E // 2) as i:
                    for half in range(2):
                        e = 2 * i + half
                        pe.wait_ge(s.onehot, e + 1)
                        for t in range(NT):
                            mm = pe.matmul(bank(g, 7)[:, bass.ds(6 * e, 6)], onehot[:, half, t, :],
                                           r.table[:, t, bass.ds(e, 1), :].rearrange("p e n -> p (e n)"),
                                           start=(t == 0), stop=(t == NT - 1))
                        mm.then_inc(s.known, 1)

            @block.scalar
            def _(act):
                for c in range(2):
                    act.wait_ge(s.up, 1 + c)
                    act.activation(silu[:, c, :], bank(g, c), ACT.Silu).then_inc(s.silu, 1)

            @block.vector
            def _(dve):
                link = Chain(dve, s.chain)
                for c in range(2):
                    dve.wait_ge(s.silu, c + 1)
                    dve.wait_ge(s.up, 3 + c)
                    dve.tensor_tensor(hidden[:, c, :], silu[:, c, :], bank(g, 2 + c), ALU.mult).then_inc(s.hidden, 1)
                dve.wait_ge(s.x, 16)
                for q in range(8):
                    t, at, b = q // 2, slice((q % 2) * BANK, (q % 2 + 1) * BANK), bank(g, 4 + q % 3)
                    dve.wait_ge(s.down, q + 1)
                    dve.tensor_tensor(b, b, g.gate_b[:, 1, at], ALU.mult).then_inc(s.gated, 1)
                    dve.wait_ge(s.gated, q + 1)
                    dve.tensor_tensor(x[:, t, at], b, x[:, t, at], ALU.add).then_inc(s.added, 1)

                def mark(e, half):
                    for t in range(NT):
                        last = dve.tensor_scalar(onehot[:, half, t, :], const(g, "count"), r.pos[:, t, bass.ds(e, 1)],
                                                 None, ALU.is_equal)
                    last.then_inc(s.onehot, 1)

                mark(0, 0)
                mark(1, 1)
                with dve.Fori(0, E // 2 - 1) as i:
                    for half in range(2):
                        dve.wait_ge(s.known, 2 * i + half + 1)
                        mark(2 * i + half + 2, half)
                dve.wait_ge(s.known, E)
                link(dve.tensor_copy(facts[:, :, :].rearrange("p e n -> p (e n)"), bank(g, 7)[:, 0:6 * E]))
                link(dve.scalar_tensor_tensor(part[:, :], facts[:, :, 2], const(g, "minus_row"), facts[:, :, 0], ALU.mult, ALU.add))
                link(dve.tensor_tensor(part[:, :], part[:, :], facts[:, :, 1], ALU.add))
                link(dve.tensor_scalar(r.index[:, :], part[:, :], const(g, "spare_row"), None, ALU.add))
                link(dve.tensor_tensor(part[:, :], facts[:, :, 3], facts[:, :, 4], ALU.add))
                link(dve.tensor_tensor(r.slot_gate[:, :], part[:, :], facts[:, :, 5], ALU.add))


def phase_routed_experts(g, tag, layer, r, out_dram):
    nc = g.nc
    s = sems(g, f"routed_{tag}", "copied", "gathered_even", "gathered_odd", "turned", "ev_a", "ev_v", "up", "silu", "hidden",
             "hturn", "hturned", "down", "weighted", "added_even", "added_odd", "passed")
    s_gathered = (s.gathered_even, s.gathered_odd)
    with ExitStack() as local:
        sb = lambda n, sh, dt=F32: local.enter_context(nc.sbuf_tensor(f"routed_{tag}_{n}", sh, dt))
        idx = sb("idx", [P, 4], U32)
        rows = sb("rows", [P, 2, D])
        rowsT = sb("rowsT", [P, 2, KD, P])
        silu = sb("silu", [P, 2, FE])
        hidden = sb("hidden", [P, 2, FE])
        hiddenT = sb("hiddenT", [P, 2, FE])
        y = sb("y", [P, 2, D])
        scale, shift = g.scale[:, 1, :], g.shift[:, 1, :]
        while g.ring.n % 3:
            g.ring.n += 1
        items = [g.ring.take(None) for _ in range(3 * E)]
        flip = items[0].s // 3
        both = [g.ring.slots[:, 3 * (par ^ flip):3 * (par ^ flip) + 2, :].rearrange("p w (j n) -> p w j n", j=KD) for par in range(2)]

        def slot(n, par, which):
            it = items[3 * par + which]
            return it, it.filled + (n - par) * 8

        def steps(eng, body):
            for n in range(3):
                body(n, n % 2)
            with eng.Fori(0, (E - 6) // 2) as i:
                body(2 * i + 3, 1)
                body(2 * i + 4, 0)
            for n in range(E - 3, E):
                body(n, n % 2)

        early = lambda n: isinstance(n, int) and n < 2
        first = lambda n: isinstance(n, int) and n == 0
        before_last = lambda n, k: not (isinstance(n, int) and n + k >= E)
        with nc.Block() as block:
            @block.sync
            def _(sp):
                def loads(n, par):
                    for which, (w, j) in enumerate(((g.dram["exp_w1"], KD), (g.dram["exp_w3"], KD), (g.dram["exp_w2"], 2))):
                        it = slot(n, par, which)[0]
                        if not early(n) and which == 0:
                            sp.wait_ge(s.up, n - 1)
                        if not early(n) and which == 2:
                            sp.wait_ge(s.down, 2 * (n - 1))
                        src = w[layer, bass.ds(n, 1)]
                        view = src.rearrange("e (p j) n -> p e j n", j=j) if j == KD else src.rearrange("e (j p) n -> p e j n", p=P)
                        sp.dma_start(it.buf.rearrange("p (e j n) -> p e j n", e=1, j=j), view).then_inc(it.full, 16)

                steps(sp, loads)

            @block.gpsimd
            def _(pool):
                def add(n, par):
                    done, before = (s.added_even, s.added_odd) if par == 0 else (s.added_odd, s.added_even)
                    if not first(n):
                        pool.wait_ge(before, (n + par) * 8)
                    pool.wait_ge(s.weighted, 2 * n + 2)
                    pool.sem_inc(s.passed)
                    pool.indirect_dma_start(out_dram, bass.IndirectOffsetOnAxis(idx[:, 2 + par:3 + par], 0), y[:, par, :],
                                            None, compute_op=ALU.add).then_inc(done, 16)

                def gather(n, par):
                    pool.wait_ge(s.copied, n + 1)
                    if not early(n):
                        pool.wait_ge(s.turned, 2 * (n - 1))
                    pool.sem_inc(s.passed)
                    pool.indirect_dma_start(rows[:, par, :], None, g.dram["rows"],
                                            bass.IndirectOffsetOnAxis(idx[:, par:par + 1], 0)).then_inc(s_gathered[par], 16)

                def step(n, par):
                    if before_last(n, 2):
                        gather(n + 2, par)
                    if not first(n):
                        add(n - 1, 1 - par)

                gather(0, 0)
                gather(1, 1)
                steps(pool, step)
                add(E - 1, 1)
                pool.wait_ge(s.added_even, 8 * E)
                pool.wait_ge(s.added_odd, 8 * E)

            @block.tensor
            def _(pe):
                def turn(n, par):
                    pe.wait_ge(s_gathered[par], (n - par) * 8 + 16)
                    if not first(n):
                        pe.wait_ge(s.ev_v, 4 * n)
                        pe.wait_ge(s.ev_a, 4 * n)
                    for j in range(KD):
                        tr = pe.transpose(bank(g, j // 4)[:, (j % 4) * P:(j % 4 + 1) * P], rows[:, par, j:D:KD], const(g, "ident"))
                        if j % 4 == 3:
                            tr.then_inc(s.turned, 1)

                def up(n, par):
                    for which in range(2):
                        it, filled = slot(n, par, which)
                        pe.wait_ge(it.full, filled)
                    pe.wait_ge(s.ev_v, 4 * n + 4)
                    pe.wait_ge(s.ev_a, 4 * n + 4)
                    if not early(n):
                        pe.wait_ge(s.hidden, n - 1)
                    for j in range(KD):
                        mm = pe.matmul(bank(g, 2 + par).rearrange("p (w n) -> p w n", w=2), rowsT[:, par, j, :],
                                       both[par][:, :, j, :], start=(j == 0), stop=(j == KD - 1))
                    mm.then_inc(s.up, 1)

                def hidden_turn(n, par):
                    pe.wait_ge(s.hidden, n + 1)
                    if not first(n):
                        pe.wait_ge(s.hturned, n)
                    for k in range(2):
                        tr = pe.transpose(bank(g, 4)[:, k * P:(k + 1) * P], hidden[:, par, k * P:(k + 1) * P], const(g, "ident"))
                    tr.then_inc(s.hturn, 1)

                def down(n, par):
                    it, filled = slot(n, par, 2)
                    pe.wait_ge(it.full, filled)
                    pe.wait_ge(s.hturned, n + 1)
                    for half in range(2):
                        if not first(n):
                            pe.wait_ge(s.weighted, 2 * n - 1 + half)
                        for k in range(2):
                            mm = pe.matmul(bank(g, 5 + half), hiddenT[:, par, k * P:(k + 1) * P],
                                           it.buf[:, k * D + half * BANK:k * D + (half + 1) * BANK], start=(k == 0), stop=(k == 1))
                        mm.then_inc(s.down, 1)

                def step(n, par):
                    if not first(n):
                        hidden_turn(n - 1, 1 - par)
                    up(n, par)
                    if before_last(n, 1):
                        turn(n + 1, 1 - par)
                    if not first(n):
                        down(n - 1, 1 - par)

                turn(0, 0)
                steps(pe, step)
                hidden_turn(E - 1, 1)
                down(E - 1, 1)

            @block.scalar
            def _(act):
                def turned(n, par):
                    act.wait_ge(s.turned, 2 * n + 2)
                    if not early(n):
                        act.wait_ge(s.up, n - 1)
                    for j in range(4, KD):
                        act.activation(rowsT[:, par, j, :], bank(g, 1)[:, (j - 4) * P:(j - 3) * P], ACT.Identity,
                                       scale=scale[:, j:j + 1], bias=shift[:, j:j + 1]).then_inc(s.ev_a, 1)

                def gate(n, par):
                    act.wait_ge(s.up, n + 1)
                    if not early(n):
                        act.wait_ge(s.hidden, n - 1)
                    act.activation(silu[:, par, :], bank(g, 2 + par)[:, 0:FE], ACT.Silu).then_inc(s.silu, 1)

                def step(n, par):
                    gate(n, par)
                    if before_last(n, 1):
                        turned(n + 1, 1 - par)

                turned(0, 0)
                steps(act, step)

            @block.vector
            def _(dve):
                def copy_index(n, par):
                    if not early(n):
                        dve.wait_ge(s_gathered[par], (n - par) * 8)
                    dve.tensor_copy(idx[:, par:par + 1], r.index[:, bass.ds(n, 1)]).then_inc(s.copied, 1)

                def turned(n, par):
                    dve.wait_ge(s.turned, 2 * n + 1)
                    if not early(n):
                        dve.wait_ge(s.up, n - 1)
                    for j in range(4):
                        dve.tensor_scalar(rowsT[:, par, j, :], bank(g, 0)[:, j * P:(j + 1) * P], scale[:, j:j + 1],
                                          shift[:, j:j + 1], ALU.mult, ALU.add).then_inc(s.ev_v, 1)

                def multiply(n, par):
                    dve.wait_ge(s.silu, n + 1)
                    if not early(n):
                        dve.wait_ge(s.hturn, n - 1)
                    dve.tensor_tensor(hidden[:, par, :], silu[:, par, :], bank(g, 2 + par)[:, FE:2 * FE], ALU.mult).then_inc(s.hidden, 1)

                def hidden_turned(n, par):
                    dve.wait_ge(s.hturn, n + 1)
                    if not early(n):
                        dve.wait_ge(s.down, 2 * (n - 1))
                    dve.tensor_copy(hiddenT[:, par, :], bank(g, 4)[:, 0:FE]).then_inc(s.hturned, 1)

                def weigh(n, par):
                    if not early(n):
                        dve.wait_ge(s.added_odd if par else s.added_even, (n - par) * 8)
                    dve.tensor_copy(idx[:, 2 + par:3 + par], r.index[:, bass.ds(n, 1)])
                    for half in range(2):
                        dve.wait_ge(s.down, 2 * n + half + 1)
                        at = slice(half * BANK, (half + 1) * BANK)
                        dve.scalar_tensor_tensor(y[:, par, at], bank(g, 5 + half), r.slot_gate[:, bass.ds(n, 1)],
                                                 g.gate_b[:, 1, at], ALU.mult, ALU.mult).then_inc(s.weighted, 1)

                def step(n, par):
                    if before_last(n, 2):
                        copy_index(n + 2, par)
                    if not first(n):
                        hidden_turned(n - 1, 1 - par)
                    multiply(n, par)
                    if before_last(n, 1):
                        turned(n + 1, 1 - par)
                    if not first(n):
                        weigh(n - 1, 1 - par)

                copy_index(0, 0)
                copy_index(1, 1)
                turned(0, 0)
                steps(dve, step)
                hidden_turned(E - 1, 1)
                weigh(E - 1, 1)


def phase_extra_blocks(g, tag, layer, r, out_dram, blocks):
    nc = g.nc
    s = sems(g, f"extra_{tag}", "weights", "onehot", "known", "index", "passed", "gathered", "turned", "ev_a", "ev_v", "up",
             "silu", "hidden", "hturn", "hturned", "down", "weighted", "added", "freed", "chain")
    with ExitStack() as local:
        sb = lambda n, sh, dt=F32: local.enter_context(nc.sbuf_tensor(f"extra_{tag}_{n}", sh, dt))
        onehot = sb("onehot", [P, NT, P], BF16)
        facts = sb("facts", [P, 6])
        part = sb("part", [P, 2])
        idx = sb("idx", [P, 1], U32)
        gate = sb("gate", [P, 1])
        rows = sb("rows", [P, D])
        rowsT = sb("rowsT", [P, KD, P])
        silu = sb("silu", [P, FE])
        hidden = sb("hidden", [P, FE])
        hiddenT = sb("hiddenT", [P, FE])
        y = sb("y", [P, D])
        scale, shift = g.scale[:, 1, :], g.shift[:, 1, :]
        both = g.ring.slots[:, 0:2, :].rearrange("p w (j n) -> p w j n", j=KD)
        w2 = g.ring.slots[:, 2, :]

        def expert(eng, i):
            return eng.value_load(r.extra_expert[0:1, bass.ds(i, 1)], min_val=0, max_val=E - 1)

        with nc.Block() as block:
            @block.sync
            def _(sp):
                with sp.Fori(0, blocks) as i:
                    e = expert(sp, i)
                    for k, name in enumerate(("exp_w1", "exp_w3")):
                        sp.dma_start(both[:, k:k + 1, :, :], g.dram[name][layer, bass.ds(e, 1)].rearrange("e (p j) n -> p e j n", j=KD))\
                          .then_inc(s.weights, 16)
                    sp.dma_start(w2.rearrange("p (e j n) -> p e j n", e=1, j=2),
                                 g.dram["exp_w2"][layer, bass.ds(e, 1)].rearrange("e (j p) n -> p e j n", p=P)).then_inc(s.weights, 16)
                    sp.wait_ge(s.added, 16 * i + 16)
                    sp.sem_inc(s.freed)

            @block.gpsimd
            def _(pool):
                with pool.Fori(0, blocks) as i:
                    pool.wait_ge(s.index, i + 1)
                    pool.sem_inc(s.passed)
                    pool.indirect_dma_start(rows[:, :], None, g.dram["rows"],
                                            bass.IndirectOffsetOnAxis(idx[:, :], 0)).then_inc(s.gathered, 16)
                    pool.wait_ge(s.weighted, 2 * i + 2)
                    pool.sem_inc(s.passed)
                    pool.indirect_dma_start(out_dram, bass.IndirectOffsetOnAxis(idx[:, :], 0), y[:, :],
                                            None, compute_op=ALU.add).then_inc(s.added, 16)
                    pool.wait_ge(s.added, 16 * i + 16)

            @block.tensor
            def _(pe):
                with pe.Fori(0, blocks) as i:
                    e = expert(pe, i)
                    pe.wait_ge(s.onehot, i + 1)
                    for t in range(NT):
                        mm = pe.matmul(bank(g, 7)[:, 0:6], onehot[:, t, :],
                                       r.table[:, t, bass.ds(e, 1), :].rearrange("p e n -> p (e n)"),
                                       start=(t == 0), stop=(t == NT - 1))
                    mm.then_inc(s.known, 1)
                    pe.wait_ge(s.gathered, 16 * i + 16)
                    for j in range(KD):
                        tr = pe.transpose(bank(g, j // 4)[:, (j % 4) * P:(j % 4 + 1) * P], rows[:, j:D:KD], const(g, "ident"))
                    tr.then_inc(s.turned, 1)
                    pe.wait_ge(s.weights, 48 * i + 48)
                    pe.wait_ge(s.ev_v, 4 * i + 4)
                    pe.wait_ge(s.ev_a, 4 * i + 4)
                    for j in range(KD):
                        mm = pe.matmul(bank(g, 2).rearrange("p (w n) -> p w n", w=2), rowsT[:, j, :], both[:, :, j, :],
                                       start=(j == 0), stop=(j == KD - 1))
                    mm.then_inc(s.up, 1)
                    pe.wait_ge(s.hidden, i + 1)
                    for k in range(2):
                        tr = pe.transpose(bank(g, 4)[:, k * P:(k + 1) * P], hidden[:, k * P:(k + 1) * P], const(g, "ident"))
                    tr.then_inc(s.hturn, 1)
                    pe.wait_ge(s.hturned, i + 1)
                    for half in range(2):
                        for k in range(2):
                            mm = pe.matmul(bank(g, 5 + half), hiddenT[:, k * P:(k + 1) * P],
                                           w2[:, k * D + half * BANK:k * D + (half + 1) * BANK], start=(k == 0), stop=(k == 1))
                        mm.then_inc(s.down, 1)
                    pe.wait_ge(s.added, 16 * i + 16)

            @block.scalar
            def _(act):
                with act.Fori(0, blocks) as i:
                    act.wait_ge(s.turned, i + 1)
                    for j in range(4, KD):
                        act.activation(rowsT[:, j, :], bank(g, 1)[:, (j - 4) * P:(j - 3) * P], ACT.Identity,
                                       scale=scale[:, j:j + 1], bias=shift[:, j:j + 1]).then_inc(s.ev_a, 1)
                    act.wait_ge(s.up, i + 1)
                    act.activation(silu[:, :], bank(g, 2)[:, 0:FE], ACT.Silu).then_inc(s.silu, 1)
                    act.wait_ge(s.added, 16 * i + 16)

            @block.vector
            def _(dve):
                with dve.Fori(0, blocks) as i:
                    e = expert(dve, i)
                    for t in range(NT):
                        last = dve.tensor_scalar(onehot[:, t, :], const(g, "count"), r.extra_base[:, bass.ds(i, 1)],
                                                 r.pos[:, t, bass.ds(e, 1)], ALU.add, ALU.is_equal)
                    last.then_inc(s.onehot, 1)
                    dve.wait_ge(s.known, i + 1)
                    link = Chain(dve, s.chain, 4 * i)
                    link(dve.tensor_copy(facts[:, :], bank(g, 7)[:, 0:6]))
                    link(dve.scalar_tensor_tensor(part[:, 0:1], facts[:, 2:3], const(g, "minus_row"), facts[:, 0:1], ALU.mult, ALU.add))
                    link(dve.tensor_tensor(part[:, 0:1], part[:, 0:1], facts[:, 1:2], ALU.add))
                    dve.tensor_scalar(idx[:, :], part[:, 0:1], const(g, "spare_row"), None, ALU.add).then_inc(s.index, 1)
                    link(dve.tensor_tensor(part[:, 1:2], facts[:, 3:4], facts[:, 4:5], ALU.add))
                    dve.tensor_tensor(gate[:, :], part[:, 1:2], facts[:, 5:6], ALU.add)
                    dve.wait_ge(s.turned, i + 1)
                    for j in range(4):
                        dve.tensor_scalar(rowsT[:, j, :], bank(g, 0)[:, j * P:(j + 1) * P], scale[:, j:j + 1],
                                          shift[:, j:j + 1], ALU.mult, ALU.add).then_inc(s.ev_v, 1)
                    dve.wait_ge(s.silu, i + 1)
                    dve.tensor_tensor(hidden[:, :], silu[:, :], bank(g, 2)[:, FE:2 * FE], ALU.mult).then_inc(s.hidden, 1)
                    dve.wait_ge(s.hturn, i + 1)
                    dve.tensor_copy(hiddenT[:, :], bank(g, 4)[:, 0:FE]).then_inc(s.hturned, 1)
                    for half in range(2):
                        dve.wait_ge(s.down, 2 * i + half + 1)
                        at = slice(half * BANK, (half + 1) * BANK)
                        dve.scalar_tensor_tensor(y[:, at], bank(g, 5 + half), gate[:, :], g.gate_b[:, 1, at],
                                                 ALU.mult, ALU.mult).then_inc(s.weighted, 1)
                    dve.wait_ge(s.added, 16 * i + 16)


def phase_ssd_in(g, hT, d):
    nc = g.nc
    s = sems(g, "ssd_in", "small", "dt_half", "dt_mm", "dt_out", "turned", "turn_out", "half", "mm", "ev_a", "ev_v",
             "scaled", "conv", "act", "tr", "x_out", "chain")
    NZ = DIN // BANK
    NC = CONV_DIM // BANK
    w = g.dram["ssm_w_in"].rearrange("(p j) n -> p j n", j=KD)
    with ExitStack() as local:
        sb = lambda n, sh, dt=F32: local.enter_context(nc.sbuf_tensor(f"ssd_in_{n}", sh, dt))
        taps = sb("taps", [32, 5, P])
        tapsT = sb("tapsT", [P, 5, 32])
        conv = sb("conv", [P, 2, T])
        silu = sb("silu", [P, 2, T])
        NB = NZ + NC
        items = [g.ring.take((s.half, nb + 1) if h == 0 else (s.mm, 4 * nb + 4)) for nb in range(NB) for h in range(2)]
        items.append(g.ring.take(None))
        with nc.Block() as block:
            @block.sync
            def _(sp):
                for k in range(4):
                    sp.dma_start(taps[:, k, :], g.dram["ssm_conv_w"][k].rearrange("(c p) -> c p", p=P)).then_inc(s.small, 16)
                sp.dma_start(taps[:, 4, :], g.dram["ssm_conv_b"].rearrange("(c p) -> c p", p=P)).then_inc(s.small, 16)
                sp.dma_start(d.dt_bias[:, :], g.dram["ssm_dt_bias"].partition_broadcast(P)).then_inc(s.small, 16)
                sp.dma_start(d.a[:, :], g.dram["ssm_a_log"].partition_broadcast(P)).then_inc(s.small, 16)
                sp.dma_start(d.skip[:, :], g.dram["ssm_d"].partition_broadcast(P)).then_inc(s.small, 16)
                for n, it in enumerate(items[:-1]):
                    nb, half = n // 2, n % 2
                    load_slot(sp, it, it.buf.rearrange("p (j n) -> p j n", j=4),
                              w[:, 4 * half:4 * half + 4, nb * BANK:(nb + 1) * BANK])
                it = items[-1]
                load_slot(sp, it, it.buf[:, 0:KD * SH].rearrange("p (j n) -> p j n", j=KD), w[:, :, NB * BANK:SSM_IN])

            @block.tensor
            def _(pe):
                pe.wait_ge(s.small, 128)
                for k in range(5):
                    tr = pe.transpose(bank(g, 7)[:, k * 32:(k + 1) * 32], taps[:, k, :], const(g, "ident")[0:32, 0:32])
                tr.then_inc(s.turned, 1)

                def turn_x(c):
                    pe.wait_ge(s.act, c + 1)
                    if c >= 2:
                        pe.wait_ge(s.x_out, c - 1)
                    for t in range(NT):
                        tr = pe.transpose(bank(g, 4 + c % 2)[:, t * P:(t + 1) * P], silu[:, c % 2, t * P:(t + 1) * P],
                                          const(g, "ident"))
                    tr.then_inc(s.tr, 1)

                for nb in range(NB):
                    for half in range(2):
                        it = items[2 * nb + half]
                        pe.wait_ge(it.full, it.filled)
                        for t in range(4):
                            if nb and half == 0:
                                if nb <= NZ:
                                    pe.wait_ge(s.ev_a, 4 * (nb - 1) + t + 1)
                                else:
                                    pe.wait_ge(s.conv, 3 * (4 * (nb - 1 - NZ) + t + 1))
                            for j in range(4):
                                k = 4 * half + j
                                if nb < NZ:
                                    lhsT, rhs = hT[:, k, t * P:(t + 1) * P], it.buf[:, j * BANK:(j + 1) * BANK]
                                else:
                                    lhsT, rhs = it.buf[:, j * BANK + t * P:j * BANK + (t + 1) * P], hT[:, k, :]
                                mm = pe.matmul(bank(g, t), lhsT, rhs, start=(k == 0), stop=(k == 7))
                            if half == 1:
                                mm.then_inc(s.mm, 1)
                            elif t == 3:
                                mm.then_inc(s.half, 1)
                            c = 4 * (nb - NZ) + t - 2
                            if half == 1 and 0 <= c < DIN // P:
                                turn_x(c)
                it = items[-1]
                pe.wait_ge(it.full, it.filled)
                for t in range(NT):
                    for k in range(KD):
                        mm = pe.matmul(bank(g, 6)[:, t * SH:(t + 1) * SH], hT[:, k, t * P:(t + 1) * P],
                                       it.buf[:, k * SH:(k + 1) * SH], start=(k == 0), stop=(k == KD - 1))
                mm.then_inc(s.dt_mm, 1)

            def place(c):
                if c < DIN // P:
                    return silu[:, c % 2, :]
                c -= DIN // P
                return d.BT[:, c, :] if c < SG else d.CT[:, c - SG, :]

            @block.scalar
            def _(act):
                act.wait_ge(s.small, 128)
                act.activation(d.a[:, :], d.a[:, :], ACT.Exp).then_inc(s.dt_half, 1)
                for n in range(4 * NZ):
                    act.wait_ge(s.mm, n + 1)
                    act.activation(d.z[:, n % 4, (n // 4) * BANK:(n // 4 + 1) * BANK], bank(g, n % 4), ACT.Silu).then_inc(s.ev_a, 1)
                act.wait_ge(s.turn_out, 1)

                def scaled(c):
                    act.wait_ge(s.mm, 4 * NZ + c + 1)
                    if c >= 2:
                        act.wait_ge(s.act, c - 1)
                    act.activation(conv[:, c % 2, :], bank(g, c % 4), ACT.Identity, scale=tapsT[:, 3, c:c + 1],
                                   bias=tapsT[:, 4, c:c + 1]).then_inc(s.scaled, 1)

                def activate(c):
                    act.wait_ge(s.conv, 3 * (c + 1))
                    if c < DIN // P and c >= 2:
                        act.wait_ge(s.tr, c - 1)
                    act.activation(place(c), conv[:, c % 2, :], ACT.Silu).then_inc(s.act, 1)

                def copy_x(c):
                    act.wait_ge(s.tr, c + 1)
                    act.copy(d.x[:, :, c * P:(c + 1) * P], bank(g, 4 + c % 2).rearrange("p (t n) -> p t n", t=NT)).then_inc(s.x_out, 1)

                N = CONV_DIM // P
                for c in range(N + 1):
                    if c < N:
                        scaled(c)
                    if 3 <= c < DIN // P + 3:
                        copy_x(c - 3)
                    if c >= 1:
                        activate(c - 1)

            @block.vector
            def _(dve):
                link = Chain(dve, s.chain)
                dve.wait_ge(s.turned, 1)
                dve.tensor_copy(tapsT[:, :, :].rearrange("p k c -> p (k c)"), bank(g, 7)[:, 0:160]).then_inc(s.turn_out, 1)
                dve.wait_ge(s.turn_out, 1)
                n = 0
                for c in range(CONV_DIM // P):
                    dve.wait_ge(s.scaled, c + 1)
                    for back in range(1, 4):
                        if back > 1:
                            dve.wait_ge(s.conv, n)
                        dve.scalar_tensor_tensor(conv[:, c % 2, back:T], bank(g, c % 4)[:, 0:T - back],
                                                 tapsT[:, 3 - back, c:c + 1], conv[:, c % 2, back:T],
                                                 ALU.mult, ALU.add).then_inc(s.conv, 1)
                        n += 1
                dve.wait_ge(s.dt_half, 1)
                link(dve.tensor_scalar(d.a[:, :], d.a[:, :], -1.0, None, ALU.mult))
                dve.wait_ge(s.dt_mm, 1)
                dve.wait_ge(s.small, 128)
                dve.tensor_tensor(d.dt[:, :, :], bank(g, 6)[:, 0:NT * SH].rearrange("p (t h) -> p t h", t=NT),
                                  d.dt_bias[:, :].unsqueeze(1).broadcast_to([P, NT, SH]), ALU.add).then_inc(s.dt_out, 1)


def phase_ssd_scan(g, d):
    nc = g.nc
    s = sems(g, "scan", "gain", "abs", "ln", "da", "cum", "cums", "ecs", "rows", "y", "seg", "exp", "mix", "state",
             "xdt", "ydone", "sq", "ms", "rstd", "chain", "skip")
    R = SH // SG
    W = R * SP
    with ExitStack() as local:
        sb = lambda n, sh, dt=F32: local.enter_context(nc.sbuf_tensor(f"scan_{n}", sh, dt))
        gain = sb("gain", [P, DIN])
        tmp = sb("tmp", [P, NT, SH])
        dA = sb("dA", [P, NT, SH])
        cs = sb("cs", [P, NT, SH])
        ecs = sb("ecs", [P, NT, SH])
        dte = sb("dte", [P, NT, SH])
        cdec = sb("cdec", [P, NT, SH])
        xdt = sb("xdt", [P, 2, W])
        xdte = sb("xdte", [P, 2, W])
        cbm = sb("cbm", [P, 2, P])
        seg = sb("seg", [P, 2, R * P])
        btok = sb("btok", [P, 2, P])
        state = sb("state", [P, SG, W])
        skip = sb("skip", [P, 2, W])
        yt = sb("yt", [P, 2, W])
        ss = sb("ss", [P, NT, SG])
        rs = sb("rs", [P, NT, SG])
        junk = sb("junk", [P, W])
        NCG = NT * SG
        heads = lambda ap: ap.rearrange("p (r c) -> p r c", r=R)
        spread = lambda ap, n: ap.unsqueeze(2).broadcast_to([P, R, n])
        with nc.Block() as block:
            @block.sync
            def _(sp):
                sp.dma_start(gain[:, :], g.dram["ssm_norm_g"].partition_broadcast(P)).then_inc(s.gain, 16)

            @block.tensor
            def _(pe):
                pe.wait_ge(s.da, 1)
                for c in range(NT):
                    pe.matmul(bank(g, 0)[:, c * SH:(c + 1) * SH], const(g, "upper"), dA[:, c, :], start=True, stop=True)
                    mm = pe.matmul(bank(g, 0)[:, 128 + c * SH:128 + (c + 1) * SH], const(g, "ones"), dA[:, c, :],
                                   start=True, stop=True)
                mm.then_inc(s.cum, 1)

                def decays(n):
                    c, q, b = n // SG, n % SG, n % 2
                    at = slice(c * P, (c + 1) * P)
                    if n == 0:
                        pe.wait_ge(s.cums, 1)
                    if n >= 2:
                        pe.wait_ge(s.mix, n - 1)
                    pe.matmul(bank(g, b)[:, 0:P], d.BT[:, q, at], d.CT[:, q, at], start=True, stop=True)
                    pe.transpose(bank(g, b)[:, P:2 * P], d.BT[:, q, at], const(g, "ident"))
                    for r in range(R):
                        mm = pe.matmul(bank(g, 2 + b)[:, r * P:(r + 1) * P],
                                       dA[:, c, q * R + r:q * R + r + 1].broadcast_to([P, P]), const(g, "upper"),
                                       start=True, stop=True)
                    mm.then_inc(s.rows, 1)

                decays(0)
                for n in range(NCG):
                    c, q, b = n // SG, n % SG, n % 2
                    at = slice(c * P, (c + 1) * P)
                    if n + 1 < NCG:
                        decays(n + 1)
                    pe.wait_ge(s.mix, n + 1)
                    pe.wait_ge(s.xdt, 2 * n + 2)
                    if n >= 2:
                        pe.wait_ge(s.ydone, n - 1)
                    if c:
                        pe.wait_ge(s.state, n - SG + 1)
                    for r in range(R):
                        pe.matmul(bank(g, 4 + b)[:, r * SP:(r + 1) * SP], seg[:, b, r * P:(r + 1) * P],
                                  xdt[:, b, r * SP:(r + 1) * SP], start=True, stop=True)
                    if c:
                        pe.matmul(bank(g, 4 + b)[:, W:2 * W], d.CT[:, q, at], state[:, q, :], start=True, stop=True)
                    if c < NT - 1:
                        mm = pe.matmul(bank(g, 6 + b)[:, 0:W], btok[:, b, :], xdte[:, b, :], start=True, stop=True)
                    else:
                        mm = pe.matmul(bank(g, 6 + b)[:, 0:1], const(g, "ident"), const(g, "ones")[:, 0:1], start=True, stop=True)
                    mm.then_inc(s.y, 1)

            @block.gpsimd
            def _(pool):
                for n in range(NCG):
                    c, q, b = n // SG, n % SG, n % 2
                    if n >= 2:
                        pool.wait_ge(s.ydone, n - 1)
                    xg = heads(d.x[:, c, q * W:(q + 1) * W])
                    pool.tensor_tensor(heads(skip[:, b, :]), xg, spread(d.skip[:, q * R:(q + 1) * R], SP), ALU.mult).then_inc(s.skip, 1)

            @block.scalar
            def _(act):
                act.activation(tmp[:, :, :], d.dt[:, :, :], ACT.Abs).then_inc(s.abs, 1)
                act.wait_ge(s.abs, 1)
                act.activation(tmp[:, :, :], tmp[:, :, :], ACT.Exp, scale=-1.0).then_inc(s.abs, 1)
                act.wait_ge(s.abs, 2)
                act.activation(tmp[:, :, :], tmp[:, :, :], ACT.Ln, bias=1.0).then_inc(s.ln, 1)
                act.wait_ge(s.ecs, 1)
                act.activation(ecs[:, :, :], cs[:, :, :], ACT.Exp).then_inc(s.cums, 1)
                act.activation(dte[:, :, :], dte[:, :, :], ACT.Exp).then_inc(s.cums, 1)
                act.activation(cdec[:, :, :], cdec[:, :, :], ACT.Exp).then_inc(s.cums, 1)
                for n in range(NCG):
                    b = n % 2
                    act.wait_ge(s.seg, n + 1)
                    act.activation(seg[:, b, :], seg[:, b, :], ACT.Exp).then_inc(s.exp, 1)
                for n in range(NCG):
                    c, q = n // SG, n % SG
                    act.wait_ge(s.ydone, NCG)
                    if n:
                        act.wait_ge(s.sq, n)
                    act.activation(junk[:, :], d.z[:, c, q * W:(q + 1) * W], ACT.Square, accum_out=ss[:, c, q:q + 1]).then_inc(s.sq, 1)
                act.wait_ge(s.ms, 1)
                act.activation(rs[:, :, :], ss[:, :, :], ACT.Sqrt).then_inc(s.rstd, 1)

            @block.vector
            def _(dve):
                link = Chain(dve, s.chain)
                dve.wait_ge(s.ln, 1)
                link(dve.scalar_tensor_tensor(d.dt[:, :, :], d.dt[:, :, :], 0.0, tmp[:, :, :], ALU.max, ALU.add))
                dve.tensor_tensor(dA[:, :, :], d.dt[:, :, :], d.a[:, :].unsqueeze(1).broadcast_to([P, NT, SH]), ALU.mult).then_inc(s.da, 1)
                dve.wait_ge(s.cum, 1)
                v = lambda a: a[:, :, :].rearrange("p c h -> p (c h)")
                link(dve.tensor_copy(v(cs), bank(g, 0)[:, 0:128]))
                link(dve.tensor_copy(v(cdec), bank(g, 0)[:, 128:256]))
                dve.tensor_tensor(v(dte), v(cdec), v(cs), ALU.subtract).then_inc(s.ecs, 1)
                dve.wait_ge(s.cums, 3)
                for n in range(NCG + 1):
                    if n < NCG:
                        c, q, b = n // SG, n % SG, n % 2
                        hs = slice(q * R, (q + 1) * R)
                        if n >= 2:
                            dve.wait_ge(s.y, n - 1)
                        dve.tensor_tensor(heads(xdt[:, b, :]), heads(d.x[:, c, q * W:(q + 1) * W]),
                                          spread(d.dt[:, c, hs], SP), ALU.mult).then_inc(s.xdt, 1)
                        dve.wait_ge(s.xdt, 2 * n + 1)
                        dve.tensor_tensor(heads(xdte[:, b, :]), heads(xdt[:, b, :]), spread(dte[:, c, hs], SP),
                                          ALU.mult).then_inc(s.xdt, 1)
                        dve.wait_ge(s.rows, n + 1)
                        link(dve.tensor_tensor(heads(seg[:, b, :]), heads(bank(g, 2 + b)), spread(cs[:, c, hs], P), ALU.subtract))
                        dve.tensor_scalar(seg[:, b, :], seg[:, b, :], 0.0, None, ALU.min).then_inc(s.seg, 1)
                        link(dve.tensor_copy(btok[:, b, :], bank(g, b)[:, P:2 * P]))
                        link(dve.tensor_tensor(cbm[:, b, :], bank(g, b)[:, 0:P], const(g, "upper"), ALU.mult))
                        dve.wait_ge(s.exp, n + 1)
                        dve.tensor_tensor(heads(seg[:, b, :]), heads(seg[:, b, :]),
                                          cbm[:, b, :].unsqueeze(1).broadcast_to([P, R, P]), ALU.mult).then_inc(s.mix, 1)
                    if n >= 1:
                        k = n - 1
                        c, q, b = k // SG, k % SG, k % 2
                        hs = slice(q * R, (q + 1) * R)
                        dve.wait_ge(s.y, k + 1)
                        if c < NT - 1:
                            if c:
                                dve.wait_ge(s.state, k - SG + 1)
                                link(dve.tensor_tensor(heads(state[:, q, :]), heads(state[:, q, :]), spread(cdec[:, c, hs], SP), ALU.mult))
                                dve.tensor_tensor(state[:, q, :], state[:, q, :], bank(g, 6 + b)[:, 0:W], ALU.add).then_inc(s.state, 1)
                            else:
                                dve.tensor_copy(state[:, q, :], bank(g, 6 + b)[:, 0:W]).then_inc(s.state, 1)
                        y, yb = yt[:, b, :], bank(g, 4 + b)
                        dve.wait_ge(s.skip, k + 1)
                        link(dve.tensor_tensor(y, skip[:, b, :], yb[:, 0:W], ALU.add))
                        if c:
                            link(dve.tensor_tensor(heads(skip[:, b, :]), heads(yb[:, W:2 * W]), spread(ecs[:, c, hs], SP), ALU.mult))
                            link(dve.tensor_tensor(y, y, skip[:, b, :], ALU.add))
                        z = d.z[:, c, q * W:(q + 1) * W]
                        dve.tensor_tensor(z, z, y, ALU.mult).then_inc(s.ydone, 1)
                dve.wait_ge(s.sq, NCG)
                link(dve.tensor_scalar(ss[:, :, :], ss[:, :, :], 1.0 / W, EPS, ALU.mult, ALU.add))
                dve.reciprocal(ss[:, :, :], ss[:, :, :]).then_inc(s.ms, 1)
                dve.wait_ge(s.rstd, 1)
                dve.wait_ge(s.gain, 16)
                for c in range(NT):
                    zg = d.z[:, c, :].rearrange("p (q w) -> p q w", q=SG)
                    link(dve.tensor_tensor(zg, zg, rs[:, c, :].unsqueeze(2).broadcast_to([P, SG, W]), ALU.mult))
                    link(dve.tensor_tensor(d.z[:, c, :], d.z[:, c, :], gain[:, :], ALU.mult))


def phase_ssd_turn(g, d, yT):
    nc = g.nc
    s = sems(g, "ssd_turn", "tr", "ev_a", "ev_v")
    with nc.Block() as block:
        @block.tensor
        def _(pe):
            for k in range(DIN // P):
                if k >= 8:
                    pe.wait_ge(s.ev_a if k % 2 == 0 else s.ev_v, (k - 8) // 2 + 1)
                for t in range(NT):
                    tr = pe.transpose(bank(g, k % 8)[:, t * P:(t + 1) * P], d.z[:, t, k * P:(k + 1) * P], const(g, "ident"))
                tr.then_inc(s.tr, 1)

        def evacuate(eng, copy, odd, sem):
            for k in range(odd, DIN // P, 2):
                eng.wait_ge(s.tr, k + 1)
                copy(yT[:, k, :], bank(g, k % 8)).then_inc(sem, 1)

        @block.scalar
        def _(act):
            evacuate(act, act.copy, 0, s.ev_a)

        @block.vector
        def _(dve):
            evacuate(dve, dve.tensor_copy, 1, s.ev_v)


def ssd_layer(g):
    nc = g.nc
    with ExitStack() as mixer:
        mb = lambda n, sh, dt=F32: mixer.enter_context(nc.sbuf_tensor(n, sh, dt))
        d = Stage()
        d.z = mb("z", [P, NT, DIN])
        d.dt_bias = mb("dt_bias", [P, SH])
        d.a = mb("a", [P, SH])
        d.skip = mb("skip_w", [P, SH])
        d.dt = mb("dt", [P, NT, SH])
        with ExitStack() as scan:
            cb = lambda n, sh: scan.enter_context(nc.sbuf_tensor(n, sh, F32))
            d.x, d.BT, d.CT = cb("xs", [P, NT, DIN]), cb("BT", [P, SG, T]), cb("CT", [P, SG, T])
            with ExitStack() as inp:
                hT = inp.enter_context(nc.sbuf_tensor("hT1", [P, KD, T], F32))
                phase_norm(g, "mix1", 1, g.dram["x2"], 0, hT)
                phase_ssd_in(g, hT, d)
            phase_ssd_scan(g, d)
        yT = mb("yT1", [P, DIN // P, T])
        phase_ssd_turn(g, d, yT)
        phase_out(g, "mix1", yT, g.dram["ssm_w_out"].rearrange("(j p) n -> p j n", p=P), DIN // P, g.dram["x2"], g.dram["x3"])


def ffn(g, tag, layer, x_dram, out_dram):
    nc = g.nc
    with ExitStack() as local:
        fb = lambda n, sh, dt=F32: local.enter_context(nc.sbuf_tensor(f"{n}_{tag}", sh, dt))
        hT = fb("hT_ffn", [P, KD, T])
        r = Stage()
        rb = lambda n, sh, dt=F32: local.enter_context(nc.sbuf_tensor(f"{n}_{tag}", sh, dt))
        r.gates, r.sel, r.pos = rb("gates", [P, NT, E]), rb("sel", [P, NT, E]), rb("pos", [P, NT, E])
        r.table = rb("table", [P, NT, E, 6], BF16)
        r.index, r.slot_gate = rb("index", [P, E], U32), rb("slot_gate", [P, E])
        r.extra_blocks, r.extra_expert, r.extra_base = rb("extra_blocks", [P, 1], I32), rb("extra_expert", [P, 32], I32), rb("extra_base", [P, 32])
        phase_norm(g, tag, layer, x_dram, 1, hT, g.dram["rows"])
        phase_router(g, tag, layer, hT, r)
        phase_shared(g, tag, layer, hT, r, x_dram, out_dram)
        phase_routed_experts(g, tag, layer, r, out_dram)
        recycle(g)
        blocks = nc.values_load(r.extra_blocks[0:1, 0:1], min_val=0, max_val=31)
        with nc.If(blocks > 0):
            phase_extra_blocks(g, tag, layer, r, out_dram, blocks)
        recycle(g)


def build(nc, a, where):
    with ExitStack() as ctx:
        g = Stage()
        g.nc, g.ctx, g.where, g.live, g.dram = nc, ctx, where, [], a
        sb = lambda n, sh, dt=F32: ctx.enter_context(nc.sbuf_tensor(n, sh, dt))
        g.ps = ctx.enter_context(nc.psum_tensor("ps", [P, 8 * BANK], F32))
        NC_ = max(b for _, b in where.values())
        g.consts = sb("consts", [P, NC_])
        ring = sb("ring", [P, NSLOT, SLOT])
        g.ring = Ring(ring, [ctx.enter_context(nc.semaphore(f"slot{i}_full")) for i in range(NSLOT)])
        g.gate_b = sb("gate_b", [P, 2, D])
        g.scale = sb("scale", [P, 2, KD])
        g.shift = sb("shift", [P, 2, KD])
        g.cond = sb("cond", [P, KD])
        phase_ada_head(g)
        with ExitStack() as mixer:
            mb = lambda n, sh, dt=F32: mixer.enter_context(nc.sbuf_tensor(n, sh, dt))
            yT = mb("yT0", [P, KD, T])
            proj = mb("proj", [P, NT, EVEN_IN])
            with ExitStack() as inp:
                hT = inp.enter_context(nc.sbuf_tensor("hT0", [P, KD, T], F32))
                phase_norm(g, "mix0", 0, g.dram["x"], 0, hT)
                phase_even_in(g, hT, proj)
            m = Stage()
            m.ret_gain = mb("ret_gain", [P, RH * P])
            m.q_gain = mb("q_gain", [P, 1])
            m.k_gain = mb("k_gain", [P, 1])
            m.pos_row_i = mb("pos_row_i", [P, T], I32)
            m.pos_row = mb("pos_row", [P, T])
            m.pos_quad_i = mb("pos_quad_i", [4, P], I32)
            m.pos_edge = mb("pos_edge", [P, P])
            m.rel = mb("rel", [P, 2, AH])
            m.delta3 = mb("delta3", [P, 3, 4 * AH], BF16)
            m.expand = mb("expand", [P, P * AH], BF16)
            m.mask = mb("mask", [P, NT, T], BF16)
            m.wi = mb("wi", [P, NT, IH])
            m.kaT = mb("kaT", [DH, T])
            m.qaT = mb("qaT", [DH, T, AH])
            with ExitStack() as head:
                hb = lambda n, sh, dt=F32: head.enter_context(nc.sbuf_tensor(n, sh, dt))
                m.qiT, m.kiT, m.ki4 = hb("qiT", [P, 2, T]), hb("kiT", [P, T]), hb("ki4", [P, NT, P])
                m.kz = hb("kz", [P, NT, RH * P])
                phase_even_prep(g, proj, m)
                m.qT, m.kT, m.qxT = hb("qT", [P, RH, T]), hb("kT", [P, RH, T]), hb("qxT", [P, RH, T])
                phase_even_turn(g, proj, m)
                phase_retention(g, proj, m, yT)
                phase_index(g, m)
            phase_attention(g, proj, m, yT)
            phase_out(g, "mix0", yT, g.dram["even_w_out"].rearrange("(j p) n -> p j n", p=P), KD, g.dram["x"], g.dram["x1"])
        recycle(g)
        ffn(g, "ffn0", 0, g.dram["x1"], g.dram["x2"])
        ssd_layer(g)
        recycle(g)
        ffn(g, "ffn1", 1, g.dram["x3"], g.dram["out"])


_INS = ["x", "c", "positions", "ada_w", "ada_b", "norm_mix_g", "norm_ffn_g", "rel_bias", "even_w_in", "ret_norm_g",
        "dsa_q_g", "dsa_k_g", "even_w_out", "ssm_w_in", "ssm_conv_w", "ssm_conv_b", "ssm_dt_bias", "ssm_a_log",
        "ssm_d", "ssm_norm_g", "ssm_w_out", "router_w", "router_b", "exp_w1", "exp_w3", "exp_w2", "sh_w1", "sh_w3",
        "sh_w2"]
_FLAT = {"x", "positions", "even_w_in", "ret_norm_g", "dsa_q_g", "dsa_k_g", "even_w_out", "ssm_w_in", "ssm_conv_w",
         "ssm_conv_b", "ssm_dt_bias", "ssm_a_log", "ssm_d", "ssm_norm_g", "ssm_w_out"}


def kernel(**inputs):
    import concourse.bacc as bacc
    from concourse.bass_utils import run_bass_kernel_spmd

    nc = bacc.Bacc("TRN2", target_bir_lowering=False, num_devices=1)
    table, where = constants()
    arrays, aps = {"consts_dram": table}, {}
    for name in _INS:
        v = np.ascontiguousarray(inputs[name])
        arrays[f"{name}_dram"] = v.reshape(v.shape[1:]) if name in _FLAT else v
    for name, v in arrays.items():
        ap = nc.dram_tensor(name, v.shape, mybir.dt.from_np(v.dtype), kind="ExternalInput").ap()
        aps["consts_in" if name == "consts_dram" else name[:-5]] = ap
    aps["out"] = nc.dram_tensor("out_dram", (T + P, D), F32, kind="ExternalOutput").ap()
    for name, rows in (("x1", T), ("x2", T + P), ("x3", T), ("rows", T + P)):
        aps[name] = nc.dram_tensor(f"{name}_scratch", (rows, D), F32).ap()
    aps["mod"] = nc.dram_tensor("mod_scratch", (2, 6 * D), F32).ap()
    with nc.allow_non_contiguous_dma(reason="positions and gains, a few KiB, turned while they are loaded"):
        build(nc, aps, where)
    r = run_bass_kernel_spmd(nc, [arrays], core_ids=[0])
    return r.results[0]["out_dram"][:T].reshape(1, T, D)
```

```python
import math
from collections import namedtuple
from contextlib import ExitStack

import numpy as np

import concourse.bass as bass
from concourse import mybir

F32 = mybir.dt.float32
BF16 = mybir.dt.bfloat16
I32 = mybir.dt.int32
U32 = mybir.dt.uint32
ALU = mybir.AluOpType
ACT = mybir.ActivationFunctionType
AX = mybir.AxisListType

P = 128
D = 1024
T = 512
NT = T // P
KD = D // P
EPS = 1e-6
BANK = 512
SLOT = 2048
NSLOT = 6
NEG = -1e30

RH, RDK = 4, 128
AH, DH, IH, IDH = 8, 64, 8, 32
TOPK_KEYS = min(256, T // 4)
EVEN_IN = 2984
QA, KA, VA, QI, KI, WI = 2048, 2560, 2624, 2688, 2944, 2976
BUCKETS, MAX_DIST = 32, 128
DIN, SH, SG, SN, SP = 2048, 32, 8, 128, 64
CONV_DIM = DIN + 2 * SG * SN
SSM_IN = DIN + CONV_DIM + SH
E, TOPK, FE = 64, 8, 256
MORE = T * TOPK // P
MANY = 9
GROUP = 8
ROUTED_SCALE = 2.5
PI2_A = 6.28125
PI2_B = float(np.float32(2 * math.pi - 6.28125) // np.float32(2.0 ** -21) * 2.0 ** -21)
PI2_C = 2 * math.pi - PI2_A - PI2_B
ROUND = 1.5 * 2.0 ** 23


def bucket_thresholds():
    exact = BUCKETS // 2
    n = np.arange(1, 4 * MAX_DIST)
    large = exact + (np.log(n.astype(np.float32) / exact) / math.log(MAX_DIST / exact)
                     * (BUCKETS - exact)).astype(np.int32)
    bucket = np.where(n < exact, n, np.minimum(large, BUCKETS - 1))
    return np.array([-1e9] + [n[bucket >= b][0] for b in range(1, BUCKETS)], np.float32)


def constants():
    i = np.arange(P, dtype=np.float64)
    log_g = np.log(1.0 - 2.0 ** (-5.0 - np.arange(RH)))
    rel = i[None, :] - i[:, None]
    decay = [np.where(rel >= 0, np.exp(g * np.maximum(rel, 0)), 0) for g in log_g]
    parts = {
        "ident": np.eye(P),
        "upper": (rel >= 0) * 1.0,
        "ones": np.ones((P, P)),
        "causal": np.where(rel > 0, NEG, 0.0),
        "decayT": np.concatenate(decay, 1),
        "xi": np.tile(np.concatenate([np.exp(g * (i + 1)) for g in log_g])[None], (P, 1)),
        "zeta": np.stack([np.exp(g * (P - 1 - i)) for g in log_g], 1),
        "inv": np.tile((np.float32(10000.0) ** (-np.arange(64, dtype=np.float32) / np.float32(64)))[None], (P, 1)),
        "thr": np.tile(bucket_thresholds(), 4)[:, None],
        "count": np.tile(i[None] + 1, (P, 1)),
        "row": i[:, None],
        "count_col": i[:, None] + 1,
        "minus_row": -i[:, None],
        "spare_row": T + i[:, None],
        "block_expert": np.tile(np.arange(3 * E) % E, (P, 1)),
        "block_base": np.tile(P * (1 + np.arange(3 * E) // E), (P, 1)),
        "quad": (np.arange(P)[:, None] // 32 == np.arange(4)[None]) * 1.0,
    }
    at, where = 0, {}
    for name, a in parts.items():
        where[name] = (at, at + a.shape[1])
        at += a.shape[1]
    return np.ascontiguousarray(np.concatenate(list(parts.values()), 1).astype(np.float32)), where


class Stage:
    pass


class Chain:

    def __init__(self, eng, sem, base=0):
        self.eng, self.sem, self.n = eng, sem, base

    def __call__(self, ins):
        self.n = self.n + 1
        ins.then_inc(self.sem, 1)
        self.eng.wait_ge(self.sem, self.n)


class Marks:

    def __init__(self, eng, sem):
        self.eng, self.sem, self.n = eng, sem, 0

    def mark(self, ins):
        self.n += 1
        ins.then_inc(self.sem, 1)
        return self.n

    def after(self, n):
        self.eng.wait_ge(self.sem, n)


Item = namedtuple("Item", "s buf free full filled")


class Ring:

    def __init__(self, slots):
        self.slots, self.n = slots, 0

    def renew(self, full):
        self.full, self.fills, self.release = full, [0] * NSLOT, [None] * NSLOT

    def take(self, release):
        s = self.n % NSLOT
        self.n += 1
        self.fills[s] += 16
        free, self.release[s] = self.release[s], release
        return Item(s, self.slots[:, s, :], free, self.full[s], self.fills[s])


def load_slot(eng, item, dst, src):
    if item.free:
        eng.wait_ge(*item.free)
    eng.dma_start(dst, src).then_inc(item.full, 16)


def take_all(g, early, releases):
    for it, release in zip(early, releases):
        g.ring.release[it.s] = release
    return early + [g.ring.take(release) for release in releases[len(early):]]


def load_half_block(g, sp, w, n, it):
    nb, half = n // 2, n % 2
    width = min(BANK, w.shape[1] - nb * BANK)
    load_slot(sp, it, it.buf.rearrange("p (j n) -> p j n", j=4)[:, :, 0:width],
              w.rearrange("(p j) n -> p j n", j=KD)[:, 4 * half:4 * half + 4, nb * BANK:nb * BANK + width])


def load_out_block(sp, w_view, kc, n, it):
    nb, q = n // (kc // 4), n % (kc // 4)
    load_slot(sp, it, it.buf.rearrange("p (j n) -> p j n", j=4), w_view[:, 4 * q:4 * q + 4, nb * BANK:(nb + 1) * BANK])


def bank(g, b):
    return g.ps[:, b * BANK:(b + 1) * BANK]


def const(g, name):
    a, b = g.where[name]
    return g.consts[:, a:b]


def sems(g, stage, *names):
    new = [g.nc.alloc_semaphore(f"{stage}_{n}") for n in names]
    g.live += new
    return namedtuple("Semaphores", names)(*new)


def slot_sems(g):
    g.parts += 1
    return sems(g, f"slots{g.parts}", *[f"full{i}" for i in range(NSLOT)])


def recycle(g):
    g.nc.clear_and_free_semaphores(g.live)
    g.nc.all_engine_barrier()
    g.live = []
    g.ring.renew(slot_sems(g))


def phase_ada_head(g):
    nc = g.nc
    s = sems(g, "ada", "table", "c", "bias", "cond", "mm", "added", "stored")
    with ExitStack() as local:
        sb = lambda n, sh, dt=F32: local.enter_context(nc.sbuf_tensor(f"ada_{n}", sh, dt))
        brow = sb("brow", [1, 2 * D])
        modrow = sb("modrow", [1, 2 * D])
        ccol = sb("ccol", [P, KD])
        NB = 2 * D // BANK
        items = [g.ring.take((s.mm, n // 2 + 1)) for n in range(2 * NB)]
        w = g.dram["ada_w"][0].rearrange("(p j) n -> p j n", j=KD)
        with nc.Block() as block:
            @block.sync
            def _(sp):
                sp.dma_start(ccol[:, :], g.dram["c"][0].rearrange("(p j) -> p j", j=KD)).then_inc(s.c, 16)
                for n, it in enumerate(items):
                    nb, half = n // 2, n % 2
                    load_slot(sp, it, it.buf.rearrange("p (j n) -> p j n", j=4),
                              w[:, 4 * half:4 * half + 4, nb * BANK:(nb + 1) * BANK])
                    if n == 1:
                        sp.dma_start(brow[:, :], g.dram["ada_b"][0:1, 0:2 * D]).then_inc(s.bias, 16)
                        sp.dma_start(g.consts[:, :], g.dram["consts_in"]).then_inc(s.table, 16)
                sp.wait_ge(s.added, NB)
                sp.dma_start(g.dram["mod"][0:1, 0:2 * D], modrow[:, :]).then_inc(s.stored, 16)
                sp.wait_ge(s.table, 16)
                sp.wait_ge(s.stored, 16)

            @block.scalar
            def _(act):
                act.wait_ge(s.c, 16)
                act.activation(g.cond[:, :], ccol[:, :], ACT.Silu).then_inc(s.cond, 1)

            @block.tensor
            def _(pe):
                pe.wait_ge(s.cond, 1)
                for nb in range(NB):
                    for half in range(2):
                        it = items[2 * nb + half]
                        pe.wait_ge(it.full, it.filled)
                        for j in range(4):
                            mm = pe.matmul(bank(g, nb)[0:1, :], g.cond[:, 4 * half + j:4 * half + j + 1],
                                           it.buf[:, j * BANK:(j + 1) * BANK], start=(half == 0 and j == 0),
                                           stop=(half == 1 and j == 3))
                    mm.then_inc(s.mm, 1)

            @block.vector
            def _(dve):
                dve.wait_ge(s.bias, 16)
                for nb in range(NB):
                    dve.wait_ge(s.mm, nb + 1)
                    at = slice(nb * BANK, (nb + 1) * BANK)
                    dve.tensor_tensor(modrow[:, at], bank(g, nb)[0:1, :], brow[:, at], ALU.add).then_inc(s.added, 1)


def phase_norm(g, tag, layer, x_dram, which, hT, rows_dram=None, router=None, ahead=()):
    nc = g.nc
    s = sems(g, f"norm_{tag}", "x0", "x1", "x2", "x3", "mod", "gate", "sq", "ms", "rstd", "xn", "tr", "scaled", "ev_a",
             "ev_v", "chain", "stored", "router")
    with ExitStack() as local:
        sb = lambda n, sh, dt=F32: local.enter_context(nc.sbuf_tensor(f"norm_{tag}_{n}", sh, dt))
        x = sb("x", [P, NT, D])
        junk = sb("junk", [P, D])
        ss = sb("ss", [P, NT])
        ms = sb("ms", [P, NT])
        rstd = sb("rstd", [P, NT])
        gain = sb("gain", [P, KD])
        one_more = sb("one_more", [P, KD])
        scale, shift = g.scale[:, which, :], g.shift[:, which, :]
        ident = const(g, "ident")
        x_loaded = [s.x0, s.x1, s.x2, s.x3]
        with nc.Block() as block:
            @block.sync
            def _(sp):
                for t in range(NT):
                    sp.dma_start(x[:, t, :], x_dram[t * P:(t + 1) * P, :]).then_inc(x_loaded[t], 16)
                if router is not None:
                    sp.dma_start(router[:, :, :], g.dram["router_w"][layer].rearrange("(p j) n -> p j n", j=KD)).then_inc(s.router, 16)
                mod = lambda k: g.dram["mod"][layer, (3 * which + k) * D:(3 * which + k + 1) * D]
                norm_gain = g.dram["norm_ffn_g" if which else "norm_mix_g"][layer]
                for dst, src in ((shift, mod(0)), (one_more[:, :], mod(1)), (gain[:, :], norm_gain)):
                    sp.dma_start(dst, src.rearrange("(p j) -> p j", j=KD)).then_inc(s.mod, 16)
                if tag != "mix0":
                    sp.dma_start(g.gate_b[:, which, :], mod(2).partition_broadcast(P)).then_inc(s.gate, 16)
                for n, it in enumerate(ahead):
                    load_half_block(g, sp, g.dram["even_w_in" if layer == 0 else "ssm_w_in"], n, it)
                if rows_dram is not None:
                    for t in range(NT):
                        sp.wait_ge(s.xn, t + 1)
                        sp.dma_start(rows_dram[t * P:(t + 1) * P, :], x[:, t, :]).then_inc(s.stored, 16)
                    sp.wait_ge(s.stored, 16 * NT)
                if tag != "mix0":
                    sp.wait_ge(s.gate, 16)

            @block.scalar
            def _(act):
                for t in range(NT):
                    act.wait_ge(x_loaded[t], 16)
                    if t:
                        act.wait_ge(s.sq, t)
                    act.activation(junk[:, :], x[:, t, :], ACT.Square, accum_out=ss[:, t:t + 1]).then_inc(s.sq, 1)
                act.wait_ge(s.ms, 1)
                act.activation(rstd[:, :], ms[:, :], ACT.Sqrt).then_inc(s.rstd, 1)
                act.wait_ge(s.scaled, 1)
                for t in range(NT):
                    act.wait_ge(s.tr, 2 * t + 2)
                    for j in range(4, KD):
                        act.activation(hT[:, j, t * P:(t + 1) * P], bank(g, 1 + 2 * (t % 2))[:, (j - 4) * P:(j - 3) * P],
                                       ACT.Identity, scale=scale[:, j:j + 1], bias=shift[:, j:j + 1]).then_inc(s.ev_a, 1)

            @block.vector
            def _(dve):
                link = Chain(dve, s.chain)
                dve.wait_ge(s.mod, 48)
                dve.scalar_tensor_tensor(scale, one_more[:, :], 1.0, gain[:, :], ALU.add, ALU.mult).then_inc(s.scaled, 1)
                dve.wait_ge(s.scaled, 1)
                dve.wait_ge(s.sq, NT)
                link(dve.tensor_scalar(ms[:, :], ss[:, :], 1.0 / D, EPS, ALU.mult, ALU.add))
                dve.reciprocal(ms[:, :], ms[:, :]).then_inc(s.ms, 1)
                dve.wait_ge(s.rstd, 1)

                def normalise(t):
                    dve.tensor_scalar(x[:, t, :], x[:, t, :], rstd[:, t:t + 1], None, ALU.mult).then_inc(s.xn, 1)

                normalise(0)
                normalise(1)
                for t in range(NT):
                    if t + 2 < NT:
                        normalise(t + 2)
                    dve.wait_ge(s.tr, 2 * t + 1)
                    for j in range(4):
                        dve.tensor_scalar(hT[:, j, t * P:(t + 1) * P], bank(g, 2 * (t % 2))[:, j * P:(j + 1) * P],
                                          scale[:, j:j + 1], shift[:, j:j + 1], ALU.mult, ALU.add).then_inc(s.ev_v, 1)

            @block.tensor
            def _(pe):
                def logits(t):
                    pe.wait_ge(s.ev_v, 4 * (t + 1))
                    pe.wait_ge(s.ev_a, 4 * (t + 1))
                    for j in range(KD):
                        pe.matmul(bank(g, 7)[:, t * E:(t + 1) * E], hT[:, j, t * P:(t + 1) * P], router[:, j, :],
                                  start=(j == 0), stop=(j == KD - 1))

                if router is not None:
                    pe.wait_ge(s.router, 16)
                for t in range(NT):
                    if router is not None and t >= 2:
                        logits(t - 2)
                    pe.wait_ge(s.xn, t + 1)
                    if t >= 2:
                        pe.wait_ge(s.ev_v, 4 * (t - 1))
                        pe.wait_ge(s.ev_a, 4 * (t - 1))
                    for j in range(KD):
                        tr = pe.transpose(bank(g, j // 4 + 2 * (t % 2))[:, (j % 4) * P:(j % 4 + 1) * P],
                                          x[:, t, j:D:KD], ident)
                        if j % 4 == 3:
                            tr.then_inc(s.tr, 1)
                if router is not None:
                    logits(NT - 2)
                    logits(NT - 1)


def phase_even_in(g, hT, proj, early, m):
    nc = g.nc
    s = sems(g, "even_in", "half", "mm", "ev_a", "ev_v", "sum", "total", "added", "bias_even", "bias_odd", "mod_even",
             "mod_odd", "ada0", "ada1", "ada2", "gate", "pos", "angle", "trig", "chain")
    NB = -(-EVEN_IN // BANK)
    width = [min(BANK, EVEN_IN - nb * BANK) for nb in range(NB)]
    items = take_all(g, early, [(s.half, nb + 1) if h == 0 else (s.mm, 4 * nb + 4) for nb in range(NB) for h in range(2)])
    blocks = [(0, k) for k in range(2, 6)] + [(1, k) for k in range(6)]
    PIECES, HELD = 4 * len(blocks), 3
    s_piece = (s.ada0, s.ada1, s.ada2)
    s_bias, s_mod = (s.bias_even, s.bias_odd), (s.mod_even, s.mod_odd)
    ADDS = KD * len(blocks)
    share = [ADDS * (nb + 1) // NB for nb in range(NB)]
    piece_at = lambda n: HELD + (2 * n - 1) * share[0] // 4

    def total_step(b):
        last = KD * b + KD - 1
        nb = min(i for i in range(NB) if share[i] > last)
        return 8 * nb + 2 + (last - (share[nb - 1] if nb else 0)) * 4 // share[0]

    total_at = [total_step(b) for b in range(len(blocks))]
    with ExitStack() as local:
        sb = lambda n, sh: local.enter_context(nc.sbuf_tensor(f"ada_{n}", sh, F32))
        piece = sb("piece", [P, HELD, 2 * D])
        acc = sb("acc", [P, 2, D])
        brow = sb("brow2", [1, 2, D])
        modrow = sb("modrow2", [1, 2, D])
        pos_i = local.enter_context(nc.sbuf_tensor("pos_i", [P, NT], I32))
        pos_f = sb("pos_f", [P, NT])
        ang = sb("ang", [P, NT, 64])
        turns = sb("turns", [P, NT, 64])
        arg = sb("arg", [P, 2, NT, 64])
        with nc.Block() as block:
            @block.sync
            def _(sp):
                def load_w(n):
                    load_half_block(g, sp, g.dram["even_w_in"], n, items[n])

                def load_ada(n):
                    b, q = n // 4, n % 4
                    layer, k = blocks[b]
                    if q == 3:
                        if b >= 2:
                            store(b - 2)
                        sp.dma_start(brow[:, b % 2, :], g.dram["ada_b"][layer:layer + 1, k * D:(k + 1) * D]).then_inc(s_bias[b % 2], 16)
                    if n >= HELD:
                        sp.wait_ge(s.sum, 2 * (n - HELD) + 2)
                    src = g.dram["ada_w"][layer].rearrange("(p j) n -> p j n", j=KD)
                    sp.dma_start(piece[:, n % HELD, :].rearrange("p (j n) -> p j n", j=2),
                                 src[:, 2 * q:2 * q + 2, k * D:(k + 1) * D]).then_inc(s_piece[n % HELD], 16)

                def store(b):
                    layer, k = blocks[b]
                    sp.wait_ge(s.added, b + 1)
                    sp.dma_start(g.dram["mod"][layer:layer + 1, k * D:(k + 1) * D], modrow[:, b % 2, :]).then_inc(s_mod[b % 2], 16)

                sp.dma_start(pos_i[:, :], g.dram["positions"].rearrange("(t p) -> p t", p=P)).then_inc(s.pos, 16)
                for n in range(HELD):
                    load_ada(n)
                for n in range(len(early), NSLOT):
                    load_w(n)
                late = NSLOT
                for n in range(HELD, PIECES):
                    load_ada(n)
                    while late < len(items) and n >= piece_at(late - NSLOT + 1):
                        load_w(late)
                        late += 1
                store(len(blocks) - 2)
                store(len(blocks) - 1)
                for par in range(2):
                    sp.wait_ge(s_mod[par], 16 * (len(blocks) // 2))
                sp.dma_start(g.gate_b[:, 0, :], g.dram["mod"][0, 2 * D:3 * D].partition_broadcast(P)).then_inc(s.gate, 16)
                sp.wait_ge(s.gate, 16)

            @block.tensor
            def _(pe):
                def total(b):
                    pe.wait_ge(s.sum, 8 * b + 8)
                    if b >= 2:
                        pe.wait_ge(s.added, b - 1)
                    for half in range(2):
                        mm = pe.matmul(bank(g, 4 + 2 * (b % 2) + half)[0:1, :], const(g, "ones")[:, 0:1],
                                       acc[:, b % 2, half * BANK:(half + 1) * BANK], start=True, stop=True)
                    mm.then_inc(s.total, 1)

                for nb in range(NB):
                    for half in range(2):
                        it = items[2 * nb + half]
                        pe.wait_ge(it.full, it.filled)
                        for t in range(NT):
                            if nb and half == 0:
                                pe.wait_ge(s.ev_a if t % 2 == 0 else s.ev_v, 2 * (nb - 1) + t // 2 + 1)
                            for j in range(4):
                                k = 4 * half + j
                                mm = pe.matmul(bank(g, t)[:, 0:width[nb]], hT[:, k, t * P:(t + 1) * P],
                                               it.buf[:, j * BANK:j * BANK + width[nb]], start=(k == 0), stop=(k == 7))
                            if half == 1:
                                mm.then_inc(s.mm, 1)
                            elif t == NT - 1:
                                mm.then_inc(s.half, 1)
                            for b in range(len(blocks)):
                                if total_at[b] == 8 * nb + 4 * half + t:
                                    total(b)

            @block.scalar
            def _(act):
                act.wait_ge(s.angle, 1)
                act.activation(m.trig[:, :, :, :], arg[:, :, :, :], ACT.Sin).then_inc(s.trig, 1)
                for nb in range(NB):
                    for t in range(0, NT, 2):
                        act.wait_ge(s.mm, 4 * nb + t + 1)
                        act.copy(proj[:, t, nb * BANK:nb * BANK + width[nb]], bank(g, t)[:, 0:width[nb]]).then_inc(s.ev_a, 1)

            @block.vector
            def _(dve):
                def accumulate(b, j):
                    n = 4 * b + j // 2
                    if j == 0 and b >= 2:
                        add_bias(b - 2)
                    if j % 2 == 0:
                        dve.wait_ge(s_piece[n % HELD], 16 * (n // HELD + 1))
                    w_j, c_j, a = piece[:, n % HELD, (j % 2) * D:(j % 2 + 1) * D], g.cond[:, j:j + 1], acc[:, b % 2, :]
                    if j == 0:
                        dve.tensor_scalar(a, w_j, c_j, None, ALU.mult).then_inc(s.sum, 1)
                    else:
                        dve.wait_ge(s.sum, KD * b + j)
                        dve.scalar_tensor_tensor(a, w_j, c_j, a, ALU.mult, ALU.add).then_inc(s.sum, 1)

                def add_bias(b):
                    dve.wait_ge(s_bias[b % 2], 16 * (b // 2 + 1))
                    dve.wait_ge(s.total, b + 1)
                    if b >= 2:
                        dve.wait_ge(s_mod[b % 2], 16 * (b // 2))
                    totals = g.ps[0:1, (4 + 2 * (b % 2)) * BANK:(6 + 2 * (b % 2)) * BANK]
                    dve.tensor_tensor(modrow[:, b % 2, :], totals, brow[:, b % 2, :], ALU.add).then_inc(s.added, 1)

                link = Chain(dve, s.chain)
                dve.wait_ge(s.pos, 16)
                link(dve.tensor_copy(pos_f[:, :], pos_i[:, :]))
                for t in range(NT):
                    last = dve.tensor_scalar(ang[:, t, :], const(g, "inv"), pos_f[:, t:t + 1], None, ALU.mult)
                link(last)
                link(dve.tensor_scalar(turns[:, :, :], ang[:, :, :], 0.5 / math.pi, ROUND, ALU.mult, ALU.add))
                link(dve.tensor_scalar(turns[:, :, :], turns[:, :, :], -ROUND, None, ALU.add))
                for c in (PI2_A, PI2_B, PI2_C):
                    link(dve.scalar_tensor_tensor(ang[:, :, :], turns[:, :, :], -c, ang[:, :, :], ALU.mult, ALU.add))
                link(dve.tensor_scalar(arg[:, 0, :, :], ang[:, :, :], 3.1415925, -3.1415925, ALU.min, ALU.max))
                link(dve.tensor_scalar(ang[:, :, :], ang[:, :, :], 0.5 * math.pi, None, ALU.add))
                link(dve.tensor_scalar(turns[:, :, :], ang[:, :, :], math.pi, -2.0 * math.pi, ALU.is_gt, ALU.mult))
                link(dve.tensor_tensor(ang[:, :, :], ang[:, :, :], turns[:, :, :], ALU.add))
                dve.tensor_scalar(arg[:, 1, :, :], ang[:, :, :], 3.1415925, -3.1415925, ALU.min, ALU.max).then_inc(s.angle, 1)
                dve.wait_ge(s.trig, 1)
                dve.tensor_scalar(m.trig_k[:, :, :, :], m.trig[:, :, :, :], RDK ** -0.5, None, ALU.mult).then_inc(s.trig, 1)
                for nb in range(NB):
                    for q in range(share[nb - 1] if nb else 0, share[nb]):
                        accumulate(q // KD, q % KD)
                    for t in range(1, NT, 2):
                        dve.wait_ge(s.mm, 4 * nb + t + 1)
                        dve.tensor_copy(proj[:, t, nb * BANK:nb * BANK + width[nb]], bank(g, t)[:, 0:width[nb]]).then_inc(s.ev_v, 1)
                add_bias(len(blocks) - 2)
                add_bias(len(blocks) - 1)


def phase_even_prep(g, proj, m):
    nc = g.nc
    s = sems(g, "prep", "pos", "ms", "rstd", "gate", "chain", "done", "rep", "repd")
    with ExitStack() as local:
        sb = lambda n, sh, dt=F32: local.enter_context(nc.sbuf_tensor(f"prep_{n}", sh, dt))
        part = sb("part", [P, 4, NT, 256])
        ss = sb("ss", [P, NT, 9])
        rs = sb("rs", [P, NT, 9])
        q_gain = sb("q_gain", [P, 1])
        with nc.Block() as block:
            @block.sync
            def _(sp):
                sp.dma_start(m.ret_gain[:, :], g.dram["ret_norm_g"].rearrange("h d -> (h d)").partition_broadcast(P)).then_inc(s.pos, 16)
                for half in range(2):
                    at = slice(64 * half, 64 * half + 64)
                    sp.dma_start(q_gain[at, :], g.dram["dsa_q_g"].rearrange("(d a) -> d a", a=1)).then_inc(s.pos, 16)
                    sp.dma_start(m.k_gain[at, :], g.dram["dsa_k_g"].rearrange("(d a) -> d a", a=1)).then_inc(s.pos, 16)
                sp.dma_start(m.pos_row_i[:, :], g.dram["positions"].partition_broadcast(P)).then_inc(s.pos, 16)
                sp.dma_start(m.pos_quad_i[:, :], g.dram["positions"].rearrange("(g q) -> q g", q=4)).then_inc(s.pos, 16)
                for r in range(4):
                    sp.dma_start(m.rel[32 * r:32 * r + 32, 0, :], g.dram["rel_bias"]).then_inc(s.rep, 16)
                sp.wait_ge(s.repd, 1)
                for r in range(4):
                    sp.dma_start(m.rel[32 * r + 1:32 * r + 32, 1, :], g.dram["rel_bias"][0:BUCKETS - 1, :]).then_inc(s.rep, 16)
                sp.wait_ge(s.rep, 128)

            @block.scalar
            def _(act):
                act.activation(proj[:, :, 1536:2048], proj[:, :, 1536:2048], ACT.Silu).then_inc(s.gate, 1)
                act.wait_ge(s.ms, 1)
                act.activation(rs[:, :, :], ss[:, :, :], ACT.Sqrt).then_inc(s.rstd, 1)

            @block.vector
            def _(dve):
                link = Chain(dve, s.chain)
                dve.memset(m.rel[:, 1, :], 0.0).then_inc(s.repd, 1)
                sq = part[:, 0:2, :, :].rearrange("p a t c -> p (a t c)").rearrange("p (t c) -> p t c", t=NT)
                link(dve.tensor_tensor(sq, proj[:, :, QA:KA], proj[:, :, QA:KA], ALU.mult))
                sqk = part[:, 2, :, 0:64]
                link(dve.tensor_tensor(sqk, proj[:, :, KA:VA], proj[:, :, KA:VA], ALU.mult))
                link(dve.tensor_reduce(ss[:, :, 0:8], sq.rearrange("p t (h d) -> p t h d", d=DH), AX.X, ALU.add))
                link(dve.tensor_reduce(ss[:, :, 8:9], sqk.unsqueeze(2), AX.X, ALU.add))
                link(dve.tensor_scalar(ss[:, :, :], ss[:, :, :], 1.0 / DH, EPS, ALU.mult, ALU.add))
                dve.reciprocal(ss[:, :, :], ss[:, :, :]).then_inc(s.ms, 1)
                dve.wait_ge(s.pos, 112)
                dve.tensor_scalar(m.q_gain[:, :], q_gain[:, :], DH ** -0.5, None, ALU.mult).then_inc(s.done, 1)
                dve.tensor_scalar(m.wi[:, :, :], proj[:, :, WI:EVEN_IN], IH ** -0.5 * IDH ** -0.5, None, ALU.mult).then_inc(s.done, 1)
                for base, tr in ((0, m.trig), (512, m.trig_k)):
                    v = proj[:, :, base:base + 512].rearrange("p t (h two d) -> p t h two d", two=2, d=64)
                    x1, x2 = v[:, :, :, 0, :], v[:, :, :, 1, :]
                    sn = tr[:, 0, :, :].unsqueeze(2).broadcast_to([P, NT, RH, 64])
                    cs = tr[:, 1, :, :].unsqueeze(2).broadcast_to([P, NT, RH, 64])
                    pt = [part[:, i, :, :].rearrange("p t (h d) -> p t h d", d=64) for i in range(4)]
                    for i, (x, f) in enumerate(((x1, cs), (x2, sn), (x1, sn), (x2, cs))):
                        link(dve.tensor_tensor(pt[i], x, f, ALU.mult))
                    link(dve.tensor_tensor(x1, pt[0], pt[1], ALU.subtract))
                    link(dve.tensor_tensor(x2, pt[2], pt[3], ALU.add))
                for t in range(NT):
                    k = proj[:, t, 512:1024].rearrange("p (h d) -> p h d", d=RDK)
                    dve.tensor_tensor(m.kz[:, t, :].rearrange("p (h d) -> p h d", d=RDK), k,
                                      const(g, "zeta").unsqueeze(2).broadcast_to([P, RH, RDK]), ALU.mult).then_inc(s.done, 1)
                dve.wait_ge(s.rstd, 1)
                qa = proj[:, :, QA:KA].rearrange("p t (h d) -> p t h d", d=DH)
                dve.tensor_tensor(qa, qa, rs[:, :, 0:8].unsqueeze(3).broadcast_to([P, NT, AH, DH]), ALU.mult).then_inc(s.done, 1)
                ka = proj[:, :, KA:VA]
                dve.tensor_tensor(ka, ka, rs[:, :, 8:9].broadcast_to([P, NT, DH]), ALU.mult).then_inc(s.done, 1)


def phase_even_turn(g, proj, m):
    nc = g.nc
    s = sems(g, "turn", "ki4", "tr", "ev_a", "ev_v")
    ident = const(g, "ident")
    groups = []
    for h in range(RH):
        groups.append(("q", h, [proj[:, t, h * 128:(h + 1) * 128] for t in range(NT)], P))
    for h in range(RH):
        groups.append(("k", h, [proj[:, t, 512 + h * 128:512 + (h + 1) * 128] for t in range(NT)], P))
    for r in range(AH // 2):
        groups.append(("qa", r, [proj[:, t, QA + r * 128:QA + (r + 1) * 128] for t in range(NT)], P))
    groups.append(("ka", 0, [proj[:, t, KA:VA] for t in range(NT)], DH))
    for r in range(2):
        groups.append(("qi", r, [proj[:, t, QI + r * 128:QI + (r + 1) * 128] for t in range(NT)], P))
    groups.append(("ki", 0, [m.ki4[:, t, :] for t in range(NT)], P))
    copies_a = {"q": 1, "qa": 2}
    copies_v = {"q": 1, "k": 1, "ka": 1, "qi": 1, "ki": 1}
    done_a, done_v, na, nv = [], [], 0, 0
    for kind, *_ in groups:
        na += copies_a.get(kind, 0)
        nv += copies_v.get(kind, 0)
        done_a.append(na)
        done_v.append(nv)
    with nc.Block() as block:
        @block.gpsimd
        def _(pool):
            ki = proj[:, :, KI:WI]
            for r in range(4):
                pool.tensor_copy(m.ki4[:, :, r * IDH:(r + 1) * IDH], ki).then_inc(s.ki4, 1)

        @block.tensor
        def _(pe):
            for n, (kind, r, srcs, rows) in enumerate(groups):
                if n >= 8:
                    if done_a[n - 8]:
                        pe.wait_ge(s.ev_a, done_a[n - 8])
                    pe.wait_ge(s.ev_v, done_v[n - 8])
                if kind == "ki":
                    pe.wait_ge(s.ki4, 4)
                for t in range(NT):
                    tr = pe.transpose(bank(g, n % 8)[0:rows, t * P:(t + 1) * P], srcs[t], ident)
                tr.then_inc(s.tr, 1)

        @block.scalar
        def _(act):
            for n, (kind, r, _, rows) in enumerate(groups):
                b = bank(g, n % 8)
                if kind in copies_a:
                    act.wait_ge(s.tr, n + 1)
                if kind == "q":
                    act.copy(m.qT[:, r, :], b).then_inc(s.ev_a, 1)
                if kind == "qa":
                    for odd in range(2):
                        at = slice(64 * odd, 64 * odd + 64)
                        act.activation(m.qaT[:, :, 2 * r + odd], b[at, :], ACT.Copy,
                                       scale=m.q_gain[at, :]).then_inc(s.ev_a, 1)

        @block.vector
        def _(dve):
            for n, (kind, r, _, rows) in enumerate(groups):
                b = bank(g, n % 8)
                if kind == "q":
                    dve.wait_ge(s.ev_a, n + 1)
                    xi = const(g, "xi")[:, r * P:(r + 1) * P].unsqueeze(1).broadcast_to([P, NT, P])
                    dve.tensor_tensor(m.qxT[:, r, :].rearrange("p (t n) -> p t n", t=NT),
                                      m.qT[:, r, :].rearrange("p (t n) -> p t n", t=NT), xi, ALU.mult).then_inc(s.ev_v, 1)
                elif kind in copies_v:
                    dve.wait_ge(s.tr, n + 1)
                if kind == "k":
                    dve.tensor_copy(m.kT[:, r, :], b).then_inc(s.ev_v, 1)
                if kind == "ka":
                    dve.tensor_scalar(m.kaT[:, :], b[0:DH, :], m.k_gain[0:DH, :], None, ALU.mult).then_inc(s.ev_v, 1)
                if kind == "qi":
                    dve.tensor_copy(m.qiT[:, r, :], b).then_inc(s.ev_v, 1)
                if kind == "ki":
                    dve.tensor_copy(m.kiT[:, :], b).then_inc(s.ev_v, 1)


def phase_retention(g, proj, m, yT):
    nc = g.nc
    s = sems(g, "ret", "gate", "inner", "decayed", "y", "u", "state", "y_out", "chain", "ms", "rstd", "yn", "tr", "ev")
    log_g = np.log(1.0 - 2.0 ** (-5.0 - np.arange(RH)))
    with ExitStack() as local:
        sb = lambda n, sh, dt=F32: local.enter_context(nc.sbuf_tensor(f"ret_{n}", sh, dt))
        inner = sb("inner", [P, 2, RH * P])
        state = sb("state", [P, RH, P])
        y, sq = proj[:, :, 0:512], proj[:, :, 512:1024]
        ss = sb("ss", [P, NT, RH])
        rs = sb("rs", [P, NT, RH])
        with nc.Block() as block:
            @block.tensor
            def _(pe):
                def scores(c):
                    if c >= 2:
                        pe.wait_ge(s.decayed, c - 1)
                    for h in range(RH):
                        mm = pe.matmul(bank(g, c % 2)[:, h * P:(h + 1) * P], m.kT[:, h, c * P:(c + 1) * P],
                                       m.qT[:, h, c * P:(c + 1) * P], start=True, stop=True)
                    mm.then_inc(s.inner, 1)
                    for h in range(RH):
                        mm = pe.matmul(bank(g, 4 + c % 2)[:, h * P:(h + 1) * P], m.kz[:, c, h * P:(h + 1) * P],
                                       proj[:, c, 1024 + h * P:1024 + (h + 1) * P], start=True, stop=True)
                    mm.then_inc(s.u, 1)

                scores(0)
                for c in range(NT):
                    pe.wait_ge(s.decayed, c + 1)
                    if c >= 2:
                        pe.wait_ge(s.y_out, c - 1)
                    if c:
                        pe.wait_ge(s.state, RH * c)
                    for h in range(RH):
                        yb = bank(g, 2 + c % 2)[:, h * P:(h + 1) * P]
                        mm = pe.matmul(yb, inner[:, c % 2, h * P:(h + 1) * P],
                                       proj[:, c, 1024 + h * P:1024 + (h + 1) * P], start=True, stop=(c == 0))
                        if c:
                            mm = pe.matmul(yb, m.qxT[:, h, c * P:(c + 1) * P], state[:, h, :], start=False, stop=True)
                    mm.then_inc(s.y, 1)
                    if c + 1 < NT:
                        scores(c + 1)
                for h in range(RH):
                    pe.wait_ge(s.yn, NT)
                    for t in range(NT):
                        tr = pe.transpose(bank(g, h)[:, t * P:(t + 1) * P], y[:, t, h * P:(h + 1) * P], const(g, "ident"))
                    tr.then_inc(s.tr, 1)

            @block.scalar
            def _(act):
                for c in range(NT):
                    act.wait_ge(s.y, c + 1)
                    act.copy(y[:, c, :], bank(g, 2 + c % 2)).then_inc(s.y_out, 1)
                act.wait_ge(s.ms, 1)
                act.activation(rs[:, :, :], ss[:, :, :], ACT.Sqrt).then_inc(s.rstd, 1)
                for h in range(RH):
                    act.wait_ge(s.tr, h + 1)
                    act.copy(yT[:, h, :], bank(g, h)).then_inc(s.ev, 1)

            @block.vector
            def _(dve):
                link = Chain(dve, s.chain)

                def squares(c):
                    dve.wait_ge(s.y_out, c + 1)
                    link(dve.tensor_tensor(sq[:, c, :], y[:, c, :], y[:, c, :], ALU.mult))
                    link(dve.tensor_reduce(ss[:, c, :], sq[:, c, :].rearrange("p (h d) -> p h d", d=P), AX.X, ALU.add))

                for c in range(NT):
                    dve.wait_ge(s.inner, c + 1)
                    dve.tensor_tensor(inner[:, c % 2, :], bank(g, c % 2), const(g, "decayT"), ALU.mult).then_inc(s.decayed, 1)
                    gate = proj[:, c, 1536:2048]
                    dve.tensor_tensor(gate, gate, m.ret_gain[:, :], ALU.mult).then_inc(s.gate, 1)
                    if c:
                        squares(c - 1)
                    if c == NT - 1:
                        break
                    dve.wait_ge(s.u, c + 1)
                    dve.wait_ge(s.y, c + 1)
                    if c:
                        dve.wait_ge(s.state, RH * c)
                    for h in range(RH):
                        u = bank(g, 4 + c % 2)[:, h * P:(h + 1) * P]
                        if c == 0:
                            dve.tensor_copy(state[:, h, :], u).then_inc(s.state, 1)
                        else:
                            dve.scalar_tensor_tensor(state[:, h, :], state[:, h, :], float(np.exp(log_g[h] * P)), u,
                                                     ALU.mult, ALU.add).then_inc(s.state, 1)
                squares(NT - 1)
                link(dve.tensor_scalar(ss[:, :, :], ss[:, :, :], 1.0 / P, EPS, ALU.mult, ALU.add))
                dve.reciprocal(ss[:, :, :], ss[:, :, :]).then_inc(s.ms, 1)
                dve.wait_ge(s.gate, NT)
                dve.wait_ge(s.rstd, 1)
                yv = y.rearrange("p t (h d) -> p t h d", d=P)
                link(dve.tensor_tensor(yv, yv, rs[:, :, :].unsqueeze(3).broadcast_to([P, NT, RH, P]), ALU.mult))
                for t in range(NT):
                    dve.tensor_tensor(y[:, t, :], y[:, t, :], proj[:, t, 1536:2048], ALU.mult).then_inc(s.yn, 1)


def phase_index(g, m):
    nc = g.nc
    s = sems(g, "index", "mm", "relu", "added", "chain", "quad", "quadT", "pos", "posT", "scored", "own")
    with ExitStack() as local:
        sb = lambda n, sh, dt=F32: local.enter_context(nc.sbuf_tensor(f"index_{n}", sh, dt))
        relu = g.ring.slots[:, 0, 0:2 * T].rearrange("p (b n) -> p b n", b=2)
        score_at = [P * sum(range(2, k + 2)) for k in range(NT)]
        score = sb("score", [P, score_at[-1]])
        best = sb("best", [P, NT - 1, 8])
        quadT = sb("quadT", [4, P])
        pos_quad = sb("pos_quad", [4, P])
        delta = sb("delta", [P, AH])
        rest = sb("rest", [P, 4, AH])
        with nc.Block() as block:
            @block.tensor
            def _(pe):
                pe.transpose(bank(g, 7)[0:4, 0:P], const(g, "quad"), const(g, "ident")).then_inc(s.quad, 1)
                n = 0
                for qb in range(1, NT):
                    w = P * (qb + 1)
                    for h in range(IH):
                        if n >= 4:
                            pe.wait_ge(s.relu, n - 3)
                        at = slice(32 * (h % 4), 32 * (h % 4) + 32)
                        pe.matmul(bank(g, n % 4)[:, 0:w], m.qiT[at, h // 4, qb * P:(qb + 1) * P], m.kiT[at, 0:w],
                                  start=True, stop=True).then_inc(s.mm, 1)
                        n += 1
                    if qb == 1:
                        pe.wait_ge(s.quadT, 1)
                        pe.matmul(bank(g, 7)[:, P:2 * P], quadT[:, :], pos_quad[:, :], start=True, stop=True).then_inc(s.pos, 1)

            @block.scalar
            def _(act):
                for n in range(IH * (NT - 1)):
                    w = P * (n // IH + 2)
                    act.wait_ge(s.mm, n + 1)
                    if n >= 2:
                        act.wait_ge(s.added, n - 1)
                    act.activation(relu[:, n % 2, 0:w], bank(g, n % 4)[:, 0:w], ACT.Relu).then_inc(s.relu, 1)

            @block.vector
            def _(dve):
                link = Chain(dve, s.chain)
                link(dve.tensor_copy(pos_quad[:, :], m.pos_quad_i[:, :]))
                link(dve.tensor_copy(m.pos_row[:, :], m.pos_row_i[:, :]))
                dve.wait_ge(s.quad, 1)
                dve.tensor_copy(quadT[:, :], bank(g, 7)[0:4, 0:P]).then_inc(s.quadT, 1)
                link(dve.tensor_tensor(delta[:, :], m.rel[:, 0, :], m.rel[:, 1, :], ALU.subtract))
                link(dve.tensor_tensor(rest[:, :, :], delta[:, :].unsqueeze(1).broadcast_to([P, 4, AH]),
                                       const(g, "quad").unsqueeze(2).broadcast_to([P, 4, AH]), ALU.mult))
                for i in range(3):
                    d = m.delta3[:, i, :].rearrange("p (q h) -> p q h", q=4)
                    link(dve.tensor_copy(d, rest[:, :, :]))
                    if i < 2:
                        link(dve.tensor_tensor(rest[:, :, :], rest[:, :, :], d, ALU.subtract))
                link(dve.tensor_copy(m.expand[:, :].rearrange("p (q h) -> p q h", h=AH),
                                     const(g, "ident").unsqueeze(2).broadcast_to([P, P, AH])))
                link(dve.tensor_copy(m.mask[:, 0, 0:P], const(g, "causal")))
                own = Marks(dve, s.own)
                views = [score[:, score_at[k]:score_at[k + 1]] for k in range(NT - 1)]
                assert TOPK_KEYS // 8 == IH * (NT - 2)
                rounds, taken, found = ([0] * len(views) for _ in range(3))

                def take(*blocks):
                    for k in blocks:
                        if rounds[k]:
                            own.after(taken[k])
                        found[k] = own.mark(dve.max(best[:, k, :], views[k]))
                        rounds[k] += 1
                    for k in blocks:
                        own.after(found[k])
                        taken[k] = own.mark(dve.match_replace(views[k], best[:, k, :], views[k], -3e38))

                n = 0
                for qb in range(1, NT):
                    w = P * (qb + 1)
                    sc = score[:, score_at[qb - 1]:score_at[qb]]
                    for h in range(IH):
                        dve.wait_ge(s.relu, n + 1)
                        if h:
                            dve.wait_ge(s.added, n)
                            dve.scalar_tensor_tensor(sc, relu[:, n % 2, 0:w], m.wi[:, qb, h:h + 1], sc,
                                                     ALU.mult, ALU.add).then_inc(s.added, 1)
                        else:
                            dve.tensor_scalar(sc, relu[:, n % 2, 0:w], m.wi[:, qb, 0:1], None, ALU.mult).then_inc(s.added, 1)
                        n += 1
                        if qb > 1:
                            if rounds[0] == 0:
                                dve.wait_ge(s.scored, 1)
                            take(0)
                    if qb == 1:
                        dve.wait_ge(s.pos, 1)
                        link(dve.tensor_scalar(m.pos_edge[:, :], bank(g, 7)[:, P:2 * P], const(g, "thr"), None, ALU.subtract))
                    dve.wait_ge(s.added, n)
                    dve.tensor_tensor(sc[:, w - P:w], sc[:, w - P:w], const(g, "causal"), ALU.add).then_inc(s.scored, 1)
                dve.wait_ge(s.scored, NT - 1)
                while rounds[1] < TOPK_KEYS // 8:
                    take(*range(1, len(views)))
                for k, sc in enumerate(views):
                    own.after(taken[k])
                    link(dve.tensor_scalar(m.mask[:, k + 1, 0:P * (k + 2)], sc, -2e38, NEG, ALU.is_gt, ALU.mult))


def phase_attention(g, proj, m, yT, early, w_out):
    nc = g.nc
    s = sems(g, "att", "steps", "logits", "max", "exp", "prob", "turn", "turned", "out", "stored", "chain")
    NTILE = T // 16
    with ExitStack() as local:
        sb = lambda n, sh, dt=F32: local.enter_context(nc.sbuf_tensor(f"att_{n}", sh, dt))
        steps = sb("steps", [P, 2, 4, T], BF16)
        prob = sb("prob", [P, 2, T])
        probT = sb("probT", [P, 2, T])
        nmax = sb("nmax", [P, 2])
        total = sb("total", [P, 2])
        inv = sb("inv", [P, 2])
        with nc.Block() as block:
            @block.sync
            def _(sp):
                for n, it in enumerate(early):
                    load_out_block(sp, w_out, KD, n, it)

            @block.tensor
            def _(pe):
                def logits(i):
                    w, b = P * (i // 8 + 1), bank(g, i % 2)
                    if i >= 2:
                        pe.wait_ge(s.exp, i - 1)
                    pe.matmul(b[:, 0:w], m.qaT[:, 16 * i:16 * i + 16, :].rearrange("p q h -> p (q h)"), m.kaT[:, 0:w],
                              start=True, stop=False)
                    pe.matmul(b[:, 0:w], m.expand[:, (i % 8) * P:(i % 8 + 1) * P], m.mask[:, i // 8, 0:w],
                              start=False, stop=False)
                    pe.wait_ge(s.steps, i + 1)
                    for j in range(4):
                        for part in range(3):
                            mm = pe.matmul(b[32 * j:32 * j + 32, 0:w], m.delta3[:, part, :], steps[:, i % 2, j, 0:w],
                                           start=False, stop=(part == 2))
                    mm.then_inc(s.logits, 1)

                def turn(i):
                    w, b = P * (i // 8 + 1), bank(g, 2 + i % 2)
                    pe.wait_ge(s.prob, i + 1)
                    if i >= 2:
                        pe.wait_ge(s.turned, i - 1)
                    for k in range(w // P):
                        tr = pe.transpose(b[:, k * P:(k + 1) * P], prob[:, i % 2, k * P:(k + 1) * P], const(g, "ident"))
                    tr.then_inc(s.turn, 1)

                def values(i):
                    nk, b = i // 8 + 1, bank(g, 4 + i % 2)
                    pe.wait_ge(s.turned, i + 1)
                    if i >= 2:
                        pe.wait_ge(s.stored, 2 * (i - 1))
                    for k in range(nk):
                        mm = pe.matmul(b[0:DH, 0:P], proj[:, k, VA:QI], probT[:, i % 2, k * P:(k + 1) * P],
                                       start=(k == 0), stop=(k == nk - 1))
                    mm.then_inc(s.out, 1)

                for i in range(NTILE + 2):
                    if i < NTILE:
                        logits(i)
                    if 1 <= i <= NTILE:
                        turn(i - 1)
                    if i >= 2:
                        values(i - 2)

            @block.scalar
            def _(act):
                def exp(i):
                    w = P * (i // 8 + 1)
                    act.wait_ge(s.max, i + 1)
                    if i >= 2:
                        act.wait_ge(s.turn, i - 1)
                    act.activation(prob[:, i % 2, 0:w], bank(g, i % 2)[:, 0:w], ACT.Exp, bias=nmax[:, i % 2:i % 2 + 1],
                                   accum_out=total[:, i % 2:i % 2 + 1]).then_inc(s.exp, 1)

                def turned(i):
                    w = P * (i // 8 + 1)
                    act.wait_ge(s.turn, i + 1)
                    if i >= 2:
                        act.wait_ge(s.out, i - 1)
                    act.copy(probT[:, i % 2, 0:w], bank(g, 2 + i % 2)[:, 0:w]).then_inc(s.turned, 1)

                def store(i):
                    act.wait_ge(s.out, i + 1)
                    o = bank(g, 4 + i % 2)[0:DH, 0:P].rearrange("p (q h two) -> p h two q", h=4, two=2)
                    for odd in range(2):
                        act.copy(yT[64 * odd:64 * odd + 64, 4:8, 16 * i:16 * i + 16], o[:, :, odd, :]).then_inc(s.stored, 1)

                for i in range(NTILE + 3):
                    if i < NTILE:
                        exp(i)
                    if 1 <= i <= NTILE:
                        turned(i - 1)
                    if 3 <= i:
                        store(i - 3)

            @block.vector
            def _(dve):
                link = Chain(dve, s.chain)

                def make_steps(i):
                    w = P * (i // 8 + 1)
                    if i >= 2:
                        dve.wait_ge(s.logits, i - 1)
                    for j in range(4):
                        last = dve.tensor_scalar(steps[:, i % 2, j, 0:w], m.pos_row[:, 0:w],
                                                 m.pos_edge[:, 4 * i + j:4 * i + j + 1], None, ALU.is_le)
                    last.then_inc(s.steps, 1)

                make_steps(0)
                for i in range(NTILE):
                    w = P * (i // 8 + 1)
                    if i + 1 < NTILE:
                        make_steps(i + 1)
                    dve.wait_ge(s.logits, i + 1)
                    link(dve.reduce_max(nmax[:, i % 2:i % 2 + 1], bank(g, i % 2)[:, 0:w], AX.X))
                    dve.tensor_scalar(nmax[:, i % 2:i % 2 + 1], nmax[:, i % 2:i % 2 + 1], -1.0, None, ALU.mult).then_inc(s.max, 1)
                    dve.wait_ge(s.exp, i + 1)
                    link(dve.reciprocal(inv[:, i % 2:i % 2 + 1], total[:, i % 2:i % 2 + 1]))
                    dve.tensor_scalar(prob[:, i % 2, 0:w], prob[:, i % 2, 0:w], inv[:, i % 2:i % 2 + 1], None,
                                      ALU.mult).then_inc(s.prob, 1)


def phase_out(g, tag, yT, w_view, kc, x_dram, out_dram, early):
    nc = g.nc
    s = sems(g, f"out_{tag}", "x", "half", "mm", "gated", "added", "store")
    nslots = kc // 4
    last_of = lambda nb: (s.mm, 4 * nb + 4)
    items = take_all(g, early, [(s.half, nb * (nslots - 1) + q + 1) if q < nslots - 1 else last_of(nb)
                                for nb in range(2) for q in range(nslots)])
    with ExitStack() as local:
        x = local.enter_context(nc.sbuf_tensor(f"out_{tag}_x", [P, NT, D], F32))
        with nc.Block() as block:
            @block.sync
            def _(sp):
                sp.dma_start(x[:, :, :], x_dram[0:T, :].rearrange("(t p) n -> p t n", p=P)).then_inc(s.x, 16)
                for n, it in enumerate(items):
                    if n >= len(early):
                        load_out_block(sp, w_view, kc, n, it)
                for t in range(NT):
                    sp.wait_ge(s.added, NT + t + 1)
                    sp.dma_start(out_dram[t * P:(t + 1) * P, :], x[:, t, :]).then_inc(s.store, 16)
                sp.wait_ge(s.store, 16 * NT)

            @block.tensor
            def _(pe):
                for nb in range(2):
                    for q in range(nslots):
                        it = items[nb * nslots + q]
                        pe.wait_ge(it.full, it.filled)
                        for t in range(NT):
                            for j in range(4):
                                k = 4 * q + j
                                mm = pe.matmul(bank(g, 4 * nb + t), yT[:, k, t * P:(t + 1) * P],
                                               it.buf[:, j * BANK:(j + 1) * BANK], start=(k == 0), stop=(k == kc - 1))
                            if q == nslots - 1:
                                mm.then_inc(s.mm, 1)
                            elif t == NT - 1:
                                mm.then_inc(s.half, 1)

            @block.vector
            def _(dve):
                dve.wait_ge(s.x, 16)
                for nb in range(2):
                    at = slice(nb * BANK, (nb + 1) * BANK)
                    for t in range(NT):
                        n = 4 * nb + t
                        dve.wait_ge(s.mm, n + 1)
                        dve.tensor_tensor(bank(g, n), bank(g, n), g.gate_b[:, 0, at], ALU.mult).then_inc(s.gated, 1)
                        dve.wait_ge(s.gated, n + 1)
                        dve.tensor_tensor(x[:, t, at], bank(g, n), x[:, t, at], ALU.add).then_inc(s.added, 1)


def phase_shared(g, tag, layer, hT, r, x_dram, out_dram):
    nc = g.nc
    s = sems(g, f"shared_{tag}", "router", "exp", "chain", "sel", "counted", "listed", "spread", "table", "up",
             "silu", "hidden", "down", "x", "gated", "added", "store", "zero", "onehot", "known", "pairs")
    with ExitStack() as local:
        sb = lambda n, sh, dt=F32: local.enter_context(nc.sbuf_tensor(f"shared_{tag}_{n}", sh, dt))
        bias = sb("bias", [P, E])
        score = sb("score", [P, NT, E])
        biased = sb("biased", [P, NT, E])
        left = sb("left", [P, NT, E])
        best = sb("best", [P, NT, 8])
        total = sb("total", [P, NT])
        rest = sb("rest", [P, NT, E])
        gates, sel, pos = sb("gates", [P, NT, E]), sb("sel", [P, NT, E]), sb("pos", [P, NT, E])
        table = sb("table", [P, NT, E, 6], BF16)
        more = sb("more", [P, 3 * E])
        rank = sb("rank", [P, 3 * E])
        nothing = sb("nothing", [P, 3 * E])
        junk = sb("junk", [P, 3 * E])
        which = sb("which", [P, 3])
        spreadx = sb("spreadx", [P, 3, MORE])
        missing = sb("missing", [P, MORE])
        more_base = sb("more_base", [P, MORE])
        pairs_f = sb("pairs_f", [P, 1])
        silu = sb("silu", [P, 2, T])
        hidden = sb("hidden", [P, 2, T])
        x = sb("x", [P, NT, D])
        zeros = sb("zeros", [P, D])
        count = sb("count", [P, P], BF16)
        count_g = sb("count_g", [P, P, GROUP], BF16)
        pos_b = sb("pos_b", [P, NT, E], BF16)
        onehot_flat = sb("onehot", [P, E * NT * P], BF16)
        onehot = onehot_flat[:, :].rearrange("p (e t n) -> p e t n", t=NT, n=P)
        onehot_g = onehot_flat[:, :].rearrange("p (g t n e) -> p g t n e", t=NT, n=P, e=GROUP)
        facts = sb("facts", [P, E + MORE, 6])
        part = sb("part", [P, E + MORE])
        while g.ring.n % 3:
            g.ring.n += 1
        w1, w3, w2 = g.ring.take((s.up, 2)), g.ring.take((s.up, 4)), g.ring.take((s.down, 8))
        r.items = [g.ring.take(None) for _ in range(3 * E)]
        down_bank = lambda q: bank(g, (4, 5, 6, 0, 1, 2)[q % 6])
        with nc.Block() as block:
            @block.sync
            def _(sp):
                load_slot(sp, w1, w1.buf.rearrange("p (j n) -> p j n", j=KD), g.dram["sh_w1"][layer].rearrange("(p j) n -> p j n", j=KD))
                sp.dma_start(bias[:, :], g.dram["router_b"][layer].partition_broadcast(P)).then_inc(s.router, 16)
                load_slot(sp, w3, w3.buf.rearrange("p (j n) -> p j n", j=KD), g.dram["sh_w3"][layer].rearrange("(p j) n -> p j n", j=KD))
                load_slot(sp, w2, w2.buf.rearrange("p (j n) -> p j n", j=2), g.dram["sh_w2"][layer].rearrange("(j p) n -> p j n", p=P))
                sp.dma_start(x[:, :, :], x_dram[0:T, :].rearrange("(t p) n -> p t n", p=P)).then_inc(s.x, 16)
                sp.wait_ge(s.zero, 1)
                sp.dma_start(out_dram[T:T + P, :], zeros[:, :]).then_inc(s.store, 16)
                sp.dma_start(g.dram["rows"][T:T + P, :], zeros[:, :]).then_inc(s.store, 16)
                for k, name in enumerate(("exp_w1", "exp_w3", "exp_w2")):
                    load_expert(g, sp, r.items[k], name, layer, 0)
                for t in range(NT):
                    sp.wait_ge(s.added, 2 * t + 2)
                    sp.dma_start(out_dram[t * P:(t + 1) * P, :], x[:, t, :]).then_inc(s.store, 16)
                sp.wait_ge(s.store, 16 * (NT + 2))

            @block.gpsimd
            def _(pool):
                pool.memset(zeros[:, :], 0.0).then_inc(s.zero, 1)
                pool.memset(table[:, :, :, 2], 1.0).then_inc(s.table, 1)
                for t in range(NT):
                    pool.memset(table[:, t, :, 1], float(P * t - T)).then_inc(s.table, 1)
                pool.tensor_copy(table[:, :, :, 0], const(g, "row").unsqueeze(2).broadcast_to([P, NT, E])).then_inc(s.table, 1)

            @block.tensor
            def _(pe):
                def up(m):
                    it = w1 if m < 2 else w3
                    if m % 2 == 0:
                        pe.wait_ge(it.full, it.filled)
                    for j in range(KD):
                        mm = pe.matmul(bank(g, m), it.buf[:, j * FE + (m % 2) * P:j * FE + (m % 2 + 1) * P],
                                       hT[:, j, :], start=(j == 0), stop=(j == KD - 1))
                    mm.then_inc(s.up, 1)

                up(0)
                pe.wait_ge(s.sel, 1)
                for t in range(NT):
                    for u in range(t + 1):
                        pe.matmul(bank(g, 4)[:, t * E:(t + 1) * E], const(g, "ones" if u < t else "upper"), sel[:, u, :],
                                  start=(u == 0), stop=(u == t))
                for u in range(NT):
                    mm = pe.matmul(bank(g, 4)[:, NT * E:(NT + 1) * E], const(g, "ones"), sel[:, u, :],
                                   start=(u == 0), stop=(u == NT - 1))
                mm.then_inc(s.counted, 1)
                up(1)
                up(2)
                up(3)
                pe.wait_ge(s.listed, 1)
                pe.matmul(bank(g, 7)[:, 0:3 * MORE], const(g, "ones"), spreadx[:, :, :].rearrange("p w x -> p (w x)"),
                          start=True, stop=True).then_inc(s.spread, 1)

                def down(q):
                    if q >= 6:
                        pe.wait_ge(s.added, q - 5)
                    for k in range(2):
                        mm = pe.matmul(down_bank(q), hidden[:, k, (q // 2) * P:(q // 2 + 1) * P],
                                       w2.buf[:, k * D + (q % 2) * BANK:k * D + (q % 2 + 1) * BANK],
                                       start=(k == 0), stop=(k == 1))
                    mm.then_inc(s.down, 1)

                pe.wait_ge(w2.full, w2.filled)
                pe.wait_ge(s.hidden, 2)
                for q in range(8):
                    down(q)
                pe.wait_ge(s.table, NT + 2)
                pe.wait_ge(s.pairs, 1)
                for e in range(E):
                    if e % GROUP == 0:
                        pe.wait_ge(s.onehot, e // GROUP + 1)
                    for t in range(NT):
                        mm = pe.matmul(bank(g, 7)[:, 6 * e:6 * e + 6], onehot_g[:, e // GROUP, t, :, e % GROUP], table[:, t, e, :],
                                       start=(t == 0), stop=(t == NT - 1))
                mm.then_inc(s.known, 1)
                pairs = pe.value_load(r.pairs[0:1, 0:1], min_val=0, max_val=MORE // 2)
                with pe.Fori(0, pairs * 2) as i:
                    e = pe.value_load(r.order[0:1, bass.ds(E + i, 1)], min_val=0, max_val=E - 1)
                    pe.wait_ge(s.onehot, i + E // GROUP + 1)
                    for t in range(NT):
                        mm = pe.matmul(bank(g, 3)[:, bass.ds(6 * i, 6)], onehot[:, bass.ds(i, 1), t, :].rearrange("p e n -> p (e n)"),
                                       table[:, t, bass.ds(e, 1), :].rearrange("p e n -> p (e n)"),
                                       start=(t == 0), stop=(t == NT - 1))
                    mm.then_inc(s.known, 1)

            @block.scalar
            def _(act):
                act.activation(score[:, :, :].rearrange("p t e -> p (t e)"), bank(g, 7)[:, 0:NT * E], ACT.Exp,
                               scale=-1.0).then_inc(s.exp, 1)
                for c in range(2):
                    act.wait_ge(s.up, 1 + c)
                    act.activation(silu[:, c, :], bank(g, c), ACT.Silu).then_inc(s.silu, 1)

            @block.vector
            def _(dve):
                link = Chain(dve, s.chain)
                link(dve.tensor_copy(count[:, :], const(g, "count")))
                link(dve.tensor_copy(count_g[:, :, :], const(g, "count").unsqueeze(2).broadcast_to([P, P, GROUP])))
                link(dve.memset(nothing[:, :], 0.0))
                dve.wait_ge(s.router, 16)
                dve.wait_ge(s.exp, 1)
                link(dve.tensor_scalar(score[:, :, :], score[:, :, :], 1.0, None, ALU.add))
                link(dve.reciprocal(score[:, :, :], score[:, :, :]))
                link(dve.tensor_tensor(biased[:, :, :], score[:, :, :], bias[:, :].unsqueeze(1).broadcast_to([P, NT, E]), ALU.add))
                for t in range(NT):
                    last = dve.max(best[:, t, :], biased[:, t, :])
                link(last)
                for t in range(NT):
                    last = dve.match_replace(left[:, t, :], best[:, t, :], biased[:, t, :], NEG)
                link(last)
                dve.tensor_scalar(sel[:, :, :], left[:, :, :], NEG / 2, None, ALU.is_lt).then_inc(s.sel, 1)
                dve.wait_ge(s.sel, 1)
                link(dve.tensor_tensor(gates[:, :, :], sel[:, :, :], score[:, :, :], ALU.mult))
                link(dve.tensor_reduce(total[:, :], gates[:, :, :], AX.X, ALU.add))
                link(dve.reciprocal(total[:, :], total[:, :]))
                link(dve.tensor_scalar(total[:, :], total[:, :], ROUTED_SCALE, None, ALU.mult))
                link(dve.tensor_tensor(gates[:, :, :], gates[:, :, :], total[:, :].unsqueeze(2).broadcast_to([P, NT, E]), ALU.mult))
                link(dve.tensor_copy(rest[:, :, :], gates[:, :, :]))
                for i in range(3):
                    link(dve.tensor_copy(table[:, :, :, 3 + i], rest[:, :, :]))
                    if i < 2:
                        link(dve.tensor_tensor(rest[:, :, :], rest[:, :, :], table[:, :, :, 3 + i], ALU.subtract))
                dve.wait_ge(s.counted, 1)
                link(dve.tensor_tensor(pos[:, :, :], bank(g, 4)[:, 0:NT * E].rearrange("p (t e) -> p t e", t=NT),
                                       sel[:, :, :], ALU.mult))
                view = lambda a: a.rearrange("p (k e) -> p k e", k=3)
                link(dve.tensor_tensor(view(more[:, :]), bank(g, 4)[:, NT * E:(NT + 1) * E].unsqueeze(1).broadcast_to([P, 3, E]),
                                       view(const(g, "block_base")), ALU.is_gt))
                link(dve.tensor_tensor_scan(rank[:, :], more[:, :], nothing[:, :], 0.0, ALU.add, ALU.add))
                link(dve.tensor_tensor(rank[:, :], rank[:, :], more[:, :], ALU.mult))
                link(dve.tensor_scalar(rank[:, :], rank[:, :], const(g, "count_col"), None, ALU.is_equal))
                for i, name in enumerate(("block_expert", "block_base")):
                    link(dve.tensor_tensor(junk[:, :], rank[:, :], const(g, name), ALU.mult))
                    link(dve.reduce_sum(which[:, i:i + 1], junk[:, :], AX.X))
                link(dve.reduce_sum(which[:, 2:3], rank[:, :], AX.X))
                for i in range(3):
                    last = dve.tensor_scalar(spreadx[:, i, :], const(g, "ident")[:, 0:MORE], which[:, i:i + 1], None, ALU.mult)
                last.then_inc(s.listed, 1)
                link(dve.tensor_copy(pos_b[:, :, :], pos[:, :, :]))

                def mark_group(n):
                    for t in range(NT):
                        at = pos_b[:, t, n * GROUP:(n + 1) * GROUP].unsqueeze(1).broadcast_to([P, P, GROUP])
                        last = dve.tensor_tensor(onehot_g[:, n, t, :, :], count_g[:, :, :], at, ALU.is_equal)
                    last.then_inc(s.onehot, 1)

                for n in range(3):
                    mark_group(n)
                for c in range(2):
                    dve.wait_ge(s.silu, c + 1)
                    dve.wait_ge(s.up, 3 + c)
                    dve.tensor_tensor(hidden[:, c, :], silu[:, c, :], bank(g, 2 + c), ALU.mult).then_inc(s.hidden, 1)
                    if c == 0:
                        mark_group(3)
                        mark_group(4)
                dve.wait_ge(s.hidden, 2)
                link(dve.memset(bank(g, 3)[:, 0:6 * MORE], 0.0))
                dve.wait_ge(s.spread, 1)
                exists = bank(g, 7)[:, 2 * MORE:3 * MORE]
                link(dve.tensor_copy(r.order[:, 0:E], const(g, "block_expert")[:, 0:E]))
                link(dve.tensor_copy(r.order[:, E:E + MORE], bank(g, 7)[:, 0:MORE]))
                link(dve.tensor_scalar(missing[:, :], exists, -float(2 * T), float(2 * T), ALU.mult, ALU.add))
                link(dve.tensor_tensor(more_base[:, :], bank(g, 7)[:, MORE:2 * MORE], missing[:, :], ALU.add))
                link(dve.reduce_sum(pairs_f[:, :], exists[:, 0:MORE:2], AX.X))
                dve.tensor_copy(r.pairs[:, :], pairs_f[:, :]).then_inc(s.pairs, 1)

                dve.wait_ge(s.x, 16)
                for q in range(8):
                    t, at = q // 2, slice((q % 2) * BANK, (q % 2 + 1) * BANK)
                    dve.wait_ge(s.down, q + 1)
                    dve.tensor_tensor(down_bank(q), down_bank(q), g.gate_b[:, 1, at], ALU.mult).then_inc(s.gated, 1)
                    dve.wait_ge(s.gated, q + 1)
                    dve.tensor_tensor(x[:, t, at], down_bank(q), x[:, t, at], ALU.add).then_inc(s.added, 1)
                for n in range(5, E // GROUP):
                    mark_group(n)
                dve.wait_ge(s.pairs, 1)
                pairs = dve.value_load(r.pairs[0:1, 0:1], min_val=0, max_val=MORE // 2)
                dve.wait_ge(s.known, 1)
                with dve.Fori(0, pairs * 2) as i:
                    e = dve.value_load(r.order[0:1, bass.ds(E + i, 1)], min_val=0, max_val=E - 1)
                    for t in range(NT):
                        last = dve.tensor_scalar(onehot[:, bass.ds(i, 1), t, :].rearrange("p e n -> p (e n)"), count[:, :],
                                                 more_base[:, bass.ds(i, 1)], pos[:, t, bass.ds(e, 1)], ALU.add, ALU.is_equal)
                    last.then_inc(s.onehot, 1)
                link(dve.tensor_copy(facts[:, 0:E, :].rearrange("p e n -> p (e n)"), bank(g, 7)[:, 0:6 * E]))
                dve.wait_ge(s.known, pairs * 2 + 1)
                link(dve.tensor_copy(facts[:, E:E + MORE, :].rearrange("p e n -> p (e n)"), bank(g, 3)[:, 0:6 * MORE]))
                link(dve.scalar_tensor_tensor(part[:, :], facts[:, :, 2], const(g, "minus_row"), facts[:, :, 0], ALU.mult, ALU.add))
                link(dve.tensor_tensor(part[:, :], part[:, :], facts[:, :, 1], ALU.add))
                link(dve.tensor_scalar(r.index[:, :], part[:, :], const(g, "spare_row"), None, ALU.add))
                link(dve.tensor_tensor(part[:, :], facts[:, :, 3], facts[:, :, 4], ALU.add))
                link(dve.tensor_tensor(r.slot_gate[:, :], part[:, :], facts[:, :, 5], ALU.add))


def load_expert(g, eng, item, name, layer, e):
    src = g.dram[name][layer, bass.ds(e, 1)]
    j = 2 if name == "exp_w2" else KD
    view = src.rearrange("e (j p) n -> p e j n", p=P) if name == "exp_w2" else src.rearrange("e (p j) n -> p e j n", j=j)
    eng.dma_start(item.buf.rearrange("p (e j n) -> p e j n", e=1, j=j), view).then_inc(item.full, 16)


def phase_routed_experts(g, tag, layer, r, out_dram):
    nc = g.nc
    s = sems(g, f"routed_{tag}", "copied", "gathered_even", "gathered_odd", "turned", "ev_a", "ev_v", "up", "silu", "hidden",
             "hturn", "hturned", "down", "weighted", "added_even", "added_odd", "passed", "passed_dve")
    s_gathered = (s.gathered_even, s.gathered_odd)
    with ExitStack() as local:
        sb = lambda n, sh, dt=F32: local.enter_context(nc.sbuf_tensor(f"routed_{tag}_{n}", sh, dt))
        idx = sb("idx", [P, 4], U32)
        rows = sb("rows", [P, 2, D])
        rowsT = sb("rowsT", [P, 2, KD, P])
        silu = sb("silu", [P, 2, FE])
        hidden = sb("hidden", [P, 2, FE])
        hiddenT = sb("hiddenT", [P, 2, FE])
        y = sb("y", [P, 2, D])
        scale, shift = g.scale[:, 1, :], g.shift[:, 1, :]
        items = r.items
        flip = items[0].s // 3
        both = [g.ring.slots[:, 3 * (par ^ flip):3 * (par ^ flip) + 2, :].rearrange("p w (j n) -> p w j n", j=KD) for par in range(2)]

        def slot(n, par, which):
            it = items[3 * par + which]
            return it, it.filled + (n - par) * 8

        def steps(eng, body):
            pairs = eng.value_load(r.pairs[0:1, 0:1], min_val=0, max_val=MORE // 2)
            for n in range(3):
                body(n, n % 2, MANY)
            with eng.Fori(0, pairs + (E - 6) // 2) as i:
                body(2 * i + 3, 1, MANY)
                body(2 * i + 4, 0, MANY)
            last = 2 * pairs + E - 1
            for k in (2, 1, 0):
                body(last - k, (k + 1) % 2, k)
            return last

        early = lambda n: isinstance(n, int) and n < 2
        first = lambda n: isinstance(n, int) and n == 0
        with nc.Block() as block:
            @block.sync
            def _(sp):
                def loads(n, par, left):
                    if first(n):
                        return
                    e = n if early(n) else sp.value_load(r.order[0:1, bass.ds(n, 1)], min_val=0, max_val=E - 1)
                    for which, name in enumerate(("exp_w1", "exp_w3", "exp_w2")):
                        it = slot(n, par, which)[0]
                        if not early(n) and which == 0:
                            sp.wait_ge(s.up, n - 1)
                        if not early(n) and which == 2:
                            sp.wait_ge(s.down, 2 * (n - 1))
                        load_expert(g, sp, it, name, layer, e)

                steps(sp, loads)

            @block.gpsimd
            def _(pool):
                def add(n, par):
                    done, before = (s.added_even, s.added_odd) if par == 0 else (s.added_odd, s.added_even)
                    if not first(n):
                        pool.wait_ge(before, (n + par) * 8)
                    pool.wait_ge(s.weighted, 2 * n + 2)
                    pool.sem_inc(s.passed)
                    pool.indirect_dma_start(out_dram, bass.IndirectOffsetOnAxis(idx[:, 2 + par:3 + par], 0), y[:, par, :],
                                            None, compute_op=ALU.add).then_inc(done, 16)

                def gather(n, par):
                    pool.wait_ge(s.copied, n + 1)
                    if not early(n):
                        pool.wait_ge(s.turned, 2 * (n - 1))
                    pool.sem_inc(s.passed)
                    pool.indirect_dma_start(rows[:, par, :], None, g.dram["rows"],
                                            bass.IndirectOffsetOnAxis(idx[:, par:par + 1], 0)).then_inc(s_gathered[par], 16)

                def step(n, par, left):
                    if left >= 2:
                        gather(n + 2, par)
                    if not first(n):
                        add(n - 1, 1 - par)

                gather(0, 0)
                gather(1, 1)
                last = steps(pool, step)
                add(last, 1)
                pool.wait_ge(s.added_even, 8 * last + 8)
                pool.wait_ge(s.added_odd, 8 * last + 8)

            @block.tensor
            def _(pe):
                def turn(n, par):
                    pe.wait_ge(s_gathered[par], (n - par) * 8 + 16)
                    if not first(n):
                        pe.wait_ge(s.ev_v, 4 * n)
                        pe.wait_ge(s.ev_a, 4 * n)
                    for j in range(KD):
                        tr = pe.transpose(bank(g, j // 4)[:, (j % 4) * P:(j % 4 + 1) * P], rows[:, par, j:D:KD], const(g, "ident"))
                        if j % 4 == 3:
                            tr.then_inc(s.turned, 1)

                def up(n, par):
                    for which in range(2):
                        it, filled = slot(n, par, which)
                        pe.wait_ge(it.full, filled)
                    pe.wait_ge(s.ev_v, 4 * n + 4)
                    pe.wait_ge(s.ev_a, 4 * n + 4)
                    if not early(n):
                        pe.wait_ge(s.hidden, n - 1)
                    for j in range(KD):
                        mm = pe.matmul(bank(g, 2 + par).rearrange("p (w n) -> p w n", w=2), rowsT[:, par, j, :],
                                       both[par][:, :, j, :], start=(j == 0), stop=(j == KD - 1))
                    mm.then_inc(s.up, 1)

                def hidden_turn(n, par):
                    pe.wait_ge(s.hidden, n + 1)
                    if not first(n):
                        pe.wait_ge(s.hturned, n)
                    for k in range(2):
                        tr = pe.transpose(bank(g, 4)[:, k * P:(k + 1) * P], hidden[:, par, k * P:(k + 1) * P], const(g, "ident"))
                    tr.then_inc(s.hturn, 1)

                def down(n, par):
                    it, filled = slot(n, par, 2)
                    pe.wait_ge(it.full, filled)
                    pe.wait_ge(s.hturned, n + 1)
                    for half in range(2):
                        if not first(n):
                            pe.wait_ge(s.weighted, 2 * n - 1 + half)
                        for k in range(2):
                            mm = pe.matmul(bank(g, 5 + half), hiddenT[:, par, k * P:(k + 1) * P],
                                           it.buf[:, k * D + half * BANK:k * D + (half + 1) * BANK], start=(k == 0), stop=(k == 1))
                        mm.then_inc(s.down, 1)

                def step(n, par, left):
                    if not first(n):
                        hidden_turn(n - 1, 1 - par)
                    up(n, par)
                    if left >= 1:
                        turn(n + 1, 1 - par)
                    if not first(n):
                        down(n - 1, 1 - par)

                turn(0, 0)
                last = steps(pe, step)
                hidden_turn(last, 1)
                down(last, 1)

            @block.scalar
            def _(act):
                def turned(n, par):
                    act.wait_ge(s.turned, 2 * n + 2)
                    if not early(n):
                        act.wait_ge(s.up, n - 1)
                    for j in range(4, KD):
                        act.activation(rowsT[:, par, j, :], bank(g, 1)[:, (j - 4) * P:(j - 3) * P], ACT.Identity,
                                       scale=scale[:, j:j + 1], bias=shift[:, j:j + 1]).then_inc(s.ev_a, 1)

                def gate(n, par):
                    act.wait_ge(s.up, n + 1)
                    if not early(n):
                        act.wait_ge(s.hidden, n - 1)
                    act.activation(silu[:, par, :], bank(g, 2 + par)[:, 0:FE], ACT.Silu).then_inc(s.silu, 1)

                def step(n, par, left):
                    gate(n, par)
                    if left >= 1:
                        turned(n + 1, 1 - par)

                turned(0, 0)
                steps(act, step)

            @block.vector
            def _(dve):
                def copy_index(n, par):
                    if not early(n):
                        dve.wait_ge(s_gathered[par], (n - par) * 8)
                        dve.sem_inc(s.passed_dve)
                    dve.tensor_copy(idx[:, par:par + 1], r.index[:, bass.ds(n, 1)]).then_inc(s.copied, 1)

                def turned(n, par):
                    dve.wait_ge(s.turned, 2 * n + 1)
                    if not early(n):
                        dve.wait_ge(s.up, n - 1)
                    for j in range(4):
                        dve.tensor_scalar(rowsT[:, par, j, :], bank(g, 0)[:, j * P:(j + 1) * P], scale[:, j:j + 1],
                                          shift[:, j:j + 1], ALU.mult, ALU.add).then_inc(s.ev_v, 1)

                def multiply(n, par):
                    dve.wait_ge(s.silu, n + 1)
                    if not early(n):
                        dve.wait_ge(s.hturn, n - 1)
                    dve.tensor_tensor(hidden[:, par, :], silu[:, par, :], bank(g, 2 + par)[:, FE:2 * FE], ALU.mult).then_inc(s.hidden, 1)

                def hidden_turned(n, par):
                    dve.wait_ge(s.hturn, n + 1)
                    if not early(n):
                        dve.wait_ge(s.down, 2 * (n - 1))
                    dve.tensor_copy(hiddenT[:, par, :], bank(g, 4)[:, 0:FE]).then_inc(s.hturned, 1)

                def weigh(n, par):
                    if not early(n):
                        dve.wait_ge(s.added_odd if par else s.added_even, (n - par) * 8)
                        dve.sem_inc(s.passed_dve)
                    dve.tensor_copy(idx[:, 2 + par:3 + par], r.index[:, bass.ds(n, 1)])
                    for half in range(2):
                        dve.wait_ge(s.down, 2 * n + half + 1)
                        at = slice(half * BANK, (half + 1) * BANK)
                        dve.scalar_tensor_tensor(y[:, par, at], bank(g, 5 + half), r.slot_gate[:, bass.ds(n, 1)],
                                                 g.gate_b[:, 1, at], ALU.mult, ALU.mult).then_inc(s.weighted, 1)

                def step(n, par, left):
                    if left >= 2:
                        copy_index(n + 2, par)
                    if not first(n):
                        hidden_turned(n - 1, 1 - par)
                    multiply(n, par)
                    if left >= 1:
                        turned(n + 1, 1 - par)
                    if not first(n):
                        weigh(n - 1, 1 - par)

                copy_index(0, 0)
                copy_index(1, 1)
                turned(0, 0)
                last = steps(dve, step)
                hidden_turned(last, 1)
                weigh(last, 1)


def phase_ssd_in(g, hT, d, early):
    nc = g.nc
    s = sems(g, "ssd_in", "small", "dt_half", "dt_mm", "dt_out", "turned", "turn_out", "half", "mm", "ev_a", "ev_v",
             "scaled", "conv", "act", "tr", "x_out", "chain")
    NZ = DIN // BANK
    NC = CONV_DIM // BANK
    w = g.dram["ssm_w_in"].rearrange("(p j) n -> p j n", j=KD)
    with ExitStack() as local:
        sb = lambda n, sh, dt=F32: local.enter_context(nc.sbuf_tensor(f"ssd_in_{n}", sh, dt))
        taps = sb("taps", [32, 5, P])
        tapsT = sb("tapsT", [P, 5, 32])
        conv = sb("conv", [P, 2, T])
        silu = sb("silu", [P, 2, T])
        NB = NZ + NC
        items = take_all(g, early, [(s.half, nb + 1) if h == 0 else (s.mm, 4 * nb + 4) for nb in range(NB) for h in range(2)])
        items.append(g.ring.take(None))
        with nc.Block() as block:
            @block.sync
            def _(sp):
                for k in range(4):
                    sp.dma_start(taps[:, k, :], g.dram["ssm_conv_w"][k].rearrange("(c p) -> c p", p=P)).then_inc(s.small, 16)
                sp.dma_start(taps[:, 4, :], g.dram["ssm_conv_b"].rearrange("(c p) -> c p", p=P)).then_inc(s.small, 16)
                sp.dma_start(d.dt_bias[:, :], g.dram["ssm_dt_bias"].partition_broadcast(P)).then_inc(s.small, 16)
                sp.dma_start(d.a[:, :], g.dram["ssm_a_log"].partition_broadcast(P)).then_inc(s.small, 16)
                sp.dma_start(d.skip[:, :], g.dram["ssm_d"].partition_broadcast(P)).then_inc(s.small, 16)
                for n, it in enumerate(items[:-1]):
                    if n >= len(early):
                        load_half_block(g, sp, g.dram["ssm_w_in"], n, it)
                it = items[-1]
                load_slot(sp, it, it.buf[:, 0:KD * SH].rearrange("p (j n) -> p j n", j=KD), w[:, :, NB * BANK:SSM_IN])

            @block.tensor
            def _(pe):
                pe.wait_ge(s.small, 128)
                for k in range(5):
                    tr = pe.transpose(bank(g, 7)[:, k * 32:(k + 1) * 32], taps[:, k, :], const(g, "ident")[0:32, 0:32])
                tr.then_inc(s.turned, 1)

                def turn_x(c):
                    pe.wait_ge(s.act, c + 1)
                    if c >= 2:
                        pe.wait_ge(s.x_out, c - 1)
                    for t in range(NT):
                        tr = pe.transpose(bank(g, 4 + c % 2)[:, t * P:(t + 1) * P], silu[:, c % 2, t * P:(t + 1) * P],
                                          const(g, "ident"))
                    tr.then_inc(s.tr, 1)

                for nb in range(NB):
                    for half in range(2):
                        it = items[2 * nb + half]
                        pe.wait_ge(it.full, it.filled)
                        for t in range(4):
                            if nb and half == 0:
                                if nb <= NZ:
                                    pe.wait_ge(s.ev_a, 4 * (nb - 1) + t + 1)
                                else:
                                    pe.wait_ge(s.conv, 3 * (4 * (nb - 1 - NZ) + t + 1))
                            for j in range(4):
                                k = 4 * half + j
                                if nb < NZ:
                                    lhsT, rhs = hT[:, k, t * P:(t + 1) * P], it.buf[:, j * BANK:(j + 1) * BANK]
                                else:
                                    lhsT, rhs = it.buf[:, j * BANK + t * P:j * BANK + (t + 1) * P], hT[:, k, :]
                                mm = pe.matmul(bank(g, t), lhsT, rhs, start=(k == 0), stop=(k == 7))
                            if half == 1:
                                mm.then_inc(s.mm, 1)
                            elif t == 3:
                                mm.then_inc(s.half, 1)
                            c = 4 * (nb - NZ) + t - 2
                            if half == 1 and 0 <= c < DIN // P:
                                turn_x(c)
                it = items[-1]
                pe.wait_ge(it.full, it.filled)
                for t in range(NT):
                    for k in range(KD):
                        mm = pe.matmul(bank(g, 6)[:, t * SH:(t + 1) * SH], hT[:, k, t * P:(t + 1) * P],
                                       it.buf[:, k * SH:(k + 1) * SH], start=(k == 0), stop=(k == KD - 1))
                mm.then_inc(s.dt_mm, 1)

            def place(c):
                if c < DIN // P:
                    return silu[:, c % 2, :]
                c -= DIN // P
                return d.BT[:, c, :] if c < SG else d.CT[:, c - SG, :]

            @block.scalar
            def _(act):
                act.wait_ge(s.small, 128)
                act.activation(d.a[:, :], d.a[:, :], ACT.Exp).then_inc(s.dt_half, 1)
                for n in range(4 * NZ):
                    act.wait_ge(s.mm, n + 1)
                    act.activation(d.z[:, n % 4, (n // 4) * BANK:(n // 4 + 1) * BANK], bank(g, n % 4), ACT.Silu).then_inc(s.ev_a, 1)
                act.wait_ge(s.turn_out, 1)

                def scaled(c):
                    act.wait_ge(s.mm, 4 * NZ + c + 1)
                    if c >= 2:
                        act.wait_ge(s.act, c - 1)
                    act.activation(conv[:, c % 2, :], bank(g, c % 4), ACT.Identity, scale=tapsT[:, 3, c:c + 1],
                                   bias=tapsT[:, 4, c:c + 1]).then_inc(s.scaled, 1)

                def activate(c):
                    act.wait_ge(s.conv, 3 * (c + 1))
                    if c < DIN // P and c >= 2:
                        act.wait_ge(s.tr, c - 1)
                    act.activation(place(c), conv[:, c % 2, :], ACT.Silu).then_inc(s.act, 1)

                def copy_x(c):
                    act.wait_ge(s.tr, c + 1)
                    act.copy(d.x[:, :, c * P:(c + 1) * P], bank(g, 4 + c % 2).rearrange("p (t n) -> p t n", t=NT)).then_inc(s.x_out, 1)

                N = CONV_DIM // P
                for c in range(N + 1):
                    if c < N:
                        scaled(c)
                    if 3 <= c < DIN // P + 3:
                        copy_x(c - 3)
                    if c >= 1:
                        activate(c - 1)

            @block.vector
            def _(dve):
                link = Chain(dve, s.chain)
                dve.wait_ge(s.turned, 1)
                dve.tensor_copy(tapsT[:, :, :].rearrange("p k c -> p (k c)"), bank(g, 7)[:, 0:160]).then_inc(s.turn_out, 1)
                dve.wait_ge(s.turn_out, 1)
                n = 0
                for c in range(CONV_DIM // P):
                    dve.wait_ge(s.scaled, c + 1)
                    for back in range(1, 4):
                        if back > 1:
                            dve.wait_ge(s.conv, n)
                        dve.scalar_tensor_tensor(conv[:, c % 2, back:T], bank(g, c % 4)[:, 0:T - back],
                                                 tapsT[:, 3 - back, c:c + 1], conv[:, c % 2, back:T],
                                                 ALU.mult, ALU.add).then_inc(s.conv, 1)
                        n += 1
                dve.wait_ge(s.dt_half, 1)
                link(dve.tensor_scalar(d.a[:, :], d.a[:, :], -1.0, None, ALU.mult))
                dve.wait_ge(s.dt_mm, 1)
                dve.wait_ge(s.small, 128)
                dve.tensor_tensor(d.dt[:, :, :], bank(g, 6)[:, 0:NT * SH].rearrange("p (t h) -> p t h", t=NT),
                                  d.dt_bias[:, :].unsqueeze(1).broadcast_to([P, NT, SH]), ALU.add).then_inc(s.dt_out, 1)


def phase_ssd_scan(g, d, early, w_out):
    nc = g.nc
    s = sems(g, "scan", "gain", "abs", "ln", "da", "cum", "cums", "ecs", "rows", "y", "seg", "exp", "mix", "state",
             "xdt", "weight", "copied", "xdte", "masked", "own", "ydone", "sq", "ms", "rstd", "chain", "skip")
    R = SH // SG
    W = R * SP
    with ExitStack() as local:
        sb = lambda n, sh, dt=F32: local.enter_context(nc.sbuf_tensor(f"scan_{n}", sh, dt))
        gain = sb("gain", [P, DIN])
        tmp = sb("tmp", [P, NT, SH])
        dA = sb("dA", [P, NT, SH])
        cs = sb("cs", [P, NT, SH])
        ecs = sb("ecs", [P, NT, SH])
        dte = sb("dte", [P, NT, SH])
        cdec = sb("cdec", [P, NT, SH])
        xdt = sb("xdt", [P, 2, W])
        xdte = sb("xdte", [P, 2, W])
        cbm = sb("cbm", [P, 2, P])
        seg = sb("seg", [P, 2, R * P])
        both = sb("both", [P, 2, 2 * P])
        weight = sb("weight", [P, NT, SH])
        state = sb("state", [P, SG, W])
        skip = sb("skip", [P, 2, W])
        carried = sb("carried", [P, 2, W])
        yt = sb("yt", [P, 2, W])
        ss = sb("ss", [P, NT, SG])
        rs = sb("rs", [P, NT, SG])
        junk = sb("junk", [P, W])
        NCG = NT * SG
        heads = lambda ap: ap.rearrange("p (r c) -> p r c", r=R)
        spread = lambda ap, n: ap.unsqueeze(2).broadcast_to([P, R, n])
        with nc.Block() as block:
            @block.sync
            def _(sp):
                sp.dma_start(gain[:, :], g.dram["ssm_norm_g"].partition_broadcast(P)).then_inc(s.gain, 16)
                for n, it in enumerate(early):
                    load_out_block(sp, w_out, DIN // P, n, it)

            @block.tensor
            def _(pe):
                pe.wait_ge(s.da, 1)
                for c in range(NT):
                    pe.matmul(bank(g, 0)[:, c * SH:(c + 1) * SH], const(g, "upper"), dA[:, c, :], start=True, stop=True)
                    mm = pe.matmul(bank(g, 0)[:, 128 + c * SH:128 + (c + 1) * SH], const(g, "ones"), dA[:, c, :],
                                   start=True, stop=True)
                mm.then_inc(s.cum, 1)

                def decays(n):
                    c, q, b = n // SG, n % SG, n % 2
                    at = slice(c * P, (c + 1) * P)
                    if n == 0:
                        pe.wait_ge(s.cums, 1)
                    if n >= 2:
                        pe.wait_ge(s.copied, n - 1)
                        pe.wait_ge(s.seg, n - 1)
                    pe.matmul(bank(g, b)[:, 0:P], d.BT[:, q, at], d.CT[:, q, at], start=True, stop=True)
                    pe.transpose(bank(g, b)[:, P:2 * P], d.BT[:, q, at], const(g, "ident"))
                    for r in range(R):
                        mm = pe.matmul(bank(g, 2 + b)[:, r * P:(r + 1) * P],
                                       dA[:, c, q * R + r:q * R + r + 1].broadcast_to([P, P]), const(g, "upper"),
                                       start=True, stop=True)
                    mm.then_inc(s.rows, 1)

                decays(0)
                for n in range(NCG):
                    c, q, b = n // SG, n % SG, n % 2
                    at = slice(c * P, (c + 1) * P)
                    if n + 1 < NCG:
                        decays(n + 1)
                    pe.wait_ge(s.mix, n + 1)
                    pe.wait_ge(s.xdt, n + 1)
                    pe.wait_ge(s.xdte, n + 1)
                    pe.wait_ge(s.copied, n + 1)
                    if n >= 2:
                        pe.wait_ge(s.ydone, n - 1)
                    if c:
                        pe.wait_ge(s.state, n - SG + 1)
                    for r in range(R):
                        pe.matmul(bank(g, 4 + b)[:, r * SP:(r + 1) * SP], seg[:, b, r * P:(r + 1) * P],
                                  xdt[:, b, r * SP:(r + 1) * SP], start=True, stop=True)
                    if c:
                        pe.matmul(bank(g, 4 + b)[:, W:2 * W], d.CT[:, q, at], state[:, q, :], start=True, stop=True)
                    if c < NT - 1:
                        mm = pe.matmul(bank(g, 6 + b)[:, 0:W], both[:, b, P:2 * P], xdte[:, b, :], start=True, stop=True)
                    else:
                        mm = pe.matmul(bank(g, 6 + b)[:, 0:1], const(g, "ident"), const(g, "ones")[:, 0:1], start=True, stop=True)
                    mm.then_inc(s.y, 1)

            @block.gpsimd
            def _(pool):
                for n in range(NCG):
                    c, q, b = n // SG, n % SG, n % 2
                    pool.wait_ge(s.copied, n + 1)
                    if n >= 2:
                        pool.wait_ge(s.mix, n - 1)
                    pool.tensor_tensor(cbm[:, b, :], both[:, b, 0:P], const(g, "upper"), ALU.mult).then_inc(s.masked, 1)
                    if n >= 2:
                        pool.wait_ge(s.ydone, n - 1)
                    xg = heads(d.x[:, c, q * W:(q + 1) * W])
                    pool.tensor_tensor(heads(skip[:, b, :]), xg, spread(d.skip[:, q * R:(q + 1) * R], SP), ALU.mult).then_inc(s.skip, 1)

            @block.scalar
            def _(act):
                act.activation(tmp[:, :, :], d.dt[:, :, :], ACT.Abs).then_inc(s.abs, 1)
                act.wait_ge(s.abs, 1)
                act.activation(tmp[:, :, :], tmp[:, :, :], ACT.Exp, scale=-1.0).then_inc(s.abs, 1)
                act.wait_ge(s.abs, 2)
                act.activation(tmp[:, :, :], tmp[:, :, :], ACT.Ln, bias=1.0).then_inc(s.ln, 1)
                act.wait_ge(s.ecs, 1)
                act.activation(ecs[:, :, :], cs[:, :, :], ACT.Exp).then_inc(s.cums, 1)
                act.activation(dte[:, :, :], dte[:, :, :], ACT.Exp).then_inc(s.cums, 1)
                act.activation(cdec[:, :, :], cdec[:, :, :], ACT.Exp).then_inc(s.cums, 1)

                def square(n):
                    c, q = n // SG, n % SG
                    act.wait_ge(s.ydone, n + 1)
                    if n:
                        act.wait_ge(s.sq, n)
                    act.activation(junk[:, :], d.z[:, c, q * W:(q + 1) * W], ACT.Square, accum_out=ss[:, c, q:q + 1]).then_inc(s.sq, 1)

                for n in range(NCG):
                    c, q, b = n // SG, n % SG, n % 2
                    act.wait_ge(s.rows, n + 1)
                    if n >= 2:
                        act.wait_ge(s.y, n - 1)
                    act.copy(both[:, b, :], bank(g, b)[:, 0:2 * P]).then_inc(s.copied, 1)
                    for r in range(R):
                        last = act.activation(seg[:, b, r * P:(r + 1) * P], bank(g, 2 + b)[:, r * P:(r + 1) * P], ACT.Relu,
                                              scale=-1.0, bias=cs[:, c, q * R + r:q * R + r + 1])
                    last.then_inc(s.seg, 1)
                    act.wait_ge(s.seg, n + 1)
                    act.activation(seg[:, b, :], seg[:, b, :], ACT.Exp, scale=-1.0).then_inc(s.exp, 1)
                    if n == 0:
                        act.wait_ge(s.weight, 1)
                    for r in range(R):
                        h = q * R + r
                        last = act.activation(xdte[:, b, r * SP:(r + 1) * SP], d.x[:, c, h * SP:(h + 1) * SP], ACT.Identity,
                                              scale=weight[:, c, h:h + 1])
                    last.then_inc(s.xdte, 1)
                    if n >= 2:
                        square(n - 2)
                square(NCG - 2)
                square(NCG - 1)
                act.wait_ge(s.ms, 1)
                act.activation(rs[:, :, :], ss[:, :, :], ACT.Sqrt).then_inc(s.rstd, 1)

            @block.vector
            def _(dve):
                link = Chain(dve, s.chain)
                dve.wait_ge(s.ln, 1)
                link(dve.scalar_tensor_tensor(d.dt[:, :, :], d.dt[:, :, :], 0.0, tmp[:, :, :], ALU.max, ALU.add))
                dve.tensor_tensor(dA[:, :, :], d.dt[:, :, :], d.a[:, :].unsqueeze(1).broadcast_to([P, NT, SH]), ALU.mult).then_inc(s.da, 1)
                dve.wait_ge(s.cum, 1)
                v = lambda a: a[:, :, :].rearrange("p c h -> p (c h)")
                link(dve.tensor_copy(v(cs), bank(g, 0)[:, 0:128]))
                link(dve.tensor_copy(v(cdec), bank(g, 0)[:, 128:256]))
                dve.tensor_tensor(v(dte), v(cdec), v(cs), ALU.subtract).then_inc(s.ecs, 1)
                dve.wait_ge(s.cums, 3)
                dve.tensor_tensor(weight[:, :, :], d.dt[:, :, :], dte[:, :, :], ALU.mult).then_inc(s.weight, 1)
                own = Marks(dve, s.own)
                for n in range(NCG + 1):
                    if n < NCG:
                        c, q, b = n // SG, n % SG, n % 2
                        hs = slice(q * R, (q + 1) * R)
                        if n >= 2:
                            dve.wait_ge(s.y, n - 1)
                        dve.tensor_tensor(heads(xdt[:, b, :]), heads(d.x[:, c, q * W:(q + 1) * W]),
                                          spread(d.dt[:, c, hs], SP), ALU.mult).then_inc(s.xdt, 1)
                        dve.wait_ge(s.exp, n + 1)
                        dve.wait_ge(s.masked, n + 1)
                        dve.tensor_tensor(heads(seg[:, b, :]), heads(seg[:, b, :]),
                                          cbm[:, b, :].unsqueeze(1).broadcast_to([P, R, P]), ALU.mult).then_inc(s.mix, 1)
                    if n >= 1:
                        k = n - 1
                        c, q, b = k // SG, k % SG, k % 2
                        hs = slice(q * R, (q + 1) * R)
                        dve.wait_ge(s.y, k + 1)
                        going, first = c < NT - 1, c == 0
                        y, yb, z = yt[:, b, :], bank(g, 4 + b), d.z[:, c, q * W:(q + 1) * W]
                        if going and first:
                            dve.tensor_copy(state[:, q, :], bank(g, 6 + b)[:, 0:W]).then_inc(s.state, 1)
                        if going and not first:
                            dve.wait_ge(s.state, k - SG + 1)
                            decayed = own.mark(dve.tensor_tensor(heads(state[:, q, :]), heads(state[:, q, :]),
                                                                 spread(cdec[:, c, hs], SP), ALU.mult))
                        if not first:
                            past = own.mark(dve.tensor_tensor(heads(carried[:, b, :]), heads(yb[:, W:2 * W]),
                                                              spread(ecs[:, c, hs], SP), ALU.mult))
                        dve.wait_ge(s.skip, k + 1)
                        summed = own.mark(dve.tensor_tensor(y, skip[:, b, :], yb[:, 0:W], ALU.add))
                        if going and not first:
                            own.after(decayed)
                            dve.tensor_tensor(state[:, q, :], state[:, q, :], bank(g, 6 + b)[:, 0:W], ALU.add).then_inc(s.state, 1)
                        own.after(summed)
                        if not first:
                            own.after(past)
                            own.after(own.mark(dve.tensor_tensor(y, y, carried[:, b, :], ALU.add)))
                        dve.tensor_tensor(z, z, y, ALU.mult).then_inc(s.ydone, 1)
                dve.wait_ge(s.sq, NCG)
                link(dve.tensor_scalar(ss[:, :, :], ss[:, :, :], 1.0 / W, EPS, ALU.mult, ALU.add))
                dve.reciprocal(ss[:, :, :], ss[:, :, :]).then_inc(s.ms, 1)
                dve.wait_ge(s.rstd, 1)
                dve.wait_ge(s.gain, 16)
                for c in range(NT):
                    zg = d.z[:, c, :].rearrange("p (q w) -> p q w", q=SG)
                    link(dve.tensor_tensor(zg, zg, rs[:, c, :].unsqueeze(2).broadcast_to([P, SG, W]), ALU.mult))
                    link(dve.tensor_tensor(d.z[:, c, :], d.z[:, c, :], gain[:, :], ALU.mult))


def phase_ssd_turn(g, d, yT):
    nc = g.nc
    s = sems(g, "ssd_turn", "tr", "ev_a", "ev_v")
    with nc.Block() as block:
        @block.tensor
        def _(pe):
            for k in range(DIN // P):
                if k >= 8:
                    pe.wait_ge(s.ev_a if k % 2 == 0 else s.ev_v, (k - 8) // 2 + 1)
                for t in range(NT):
                    tr = pe.transpose(bank(g, k % 8)[:, t * P:(t + 1) * P], d.z[:, t, k * P:(k + 1) * P], const(g, "ident"))
                tr.then_inc(s.tr, 1)

        def evacuate(eng, copy, odd, sem):
            for k in range(odd, DIN // P, 2):
                eng.wait_ge(s.tr, k + 1)
                copy(yT[:, k, :], bank(g, k % 8)).then_inc(sem, 1)

        @block.scalar
        def _(act):
            evacuate(act, act.copy, 0, s.ev_a)

        @block.vector
        def _(dve):
            evacuate(dve, dve.tensor_copy, 1, s.ev_v)


def ssd_layer(g):
    nc = g.nc
    with ExitStack() as mixer:
        mb = lambda n, sh, dt=F32: mixer.enter_context(nc.sbuf_tensor(n, sh, dt))
        d = Stage()
        d.z = mb("z", [P, NT, DIN])
        d.dt_bias = mb("dt_bias", [P, SH])
        d.a = mb("a", [P, SH])
        d.skip = mb("skip_w", [P, SH])
        d.dt = mb("dt", [P, NT, SH])
        with ExitStack() as scan:
            cb = lambda n, sh: scan.enter_context(nc.sbuf_tensor(n, sh, F32))
            d.x, d.BT, d.CT = cb("xs", [P, NT, DIN]), cb("BT", [P, SG, T]), cb("CT", [P, SG, T])
            with ExitStack() as inp:
                hT = inp.enter_context(nc.sbuf_tensor("hT1", [P, KD, T], F32))
                early = [g.ring.take(None) for _ in range(4)]
                phase_norm(g, "mix1", 1, g.dram["x2"], 0, hT, ahead=early)
                phase_ssd_in(g, hT, d, early)
            early, w_out = [g.ring.take(None) for _ in range(4)], g.dram["ssm_w_out"].rearrange("(j p) n -> p j n", p=P)
            phase_ssd_scan(g, d, early, w_out)
        yT = mb("yT1", [P, DIN // P, T])
        phase_ssd_turn(g, d, yT)
        phase_out(g, "mix1", yT, w_out, DIN // P, g.dram["x2"], g.dram["x3"], early)


def ffn(g, tag, layer, x_dram, out_dram):
    nc = g.nc
    with ExitStack() as local:
        fb = lambda n, sh, dt=F32: local.enter_context(nc.sbuf_tensor(f"{n}_{tag}", sh, dt))
        hT = fb("hT_ffn", [P, KD, T])
        r = Stage()
        rb = lambda n, sh, dt=F32: local.enter_context(nc.sbuf_tensor(f"{n}_{tag}", sh, dt))
        r.index, r.slot_gate = rb("index", [P, E + MORE], U32), rb("slot_gate", [P, E + MORE])
        r.order, r.pairs = rb("order", [P, E + MORE], I32), rb("pairs", [P, 1], I32)
        with nc.sbuf_tensor(f"router_w_{tag}", [P, KD, E], F32) as router:
            phase_norm(g, tag, layer, x_dram, 1, hT, g.dram["rows"], router)
        phase_shared(g, tag, layer, hT, r, x_dram, out_dram)
        phase_routed_experts(g, tag, layer, r, out_dram)
        recycle(g)


def build(nc, a, where):
    with ExitStack() as ctx:
        g = Stage()
        g.nc, g.ctx, g.where, g.live, g.dram = nc, ctx, where, [], a
        sb = lambda n, sh, dt=F32: ctx.enter_context(nc.sbuf_tensor(n, sh, dt))
        g.ps = ctx.enter_context(nc.psum_tensor("ps", [P, 8 * BANK], F32))
        NC_ = max(b for _, b in where.values())
        g.consts = sb("consts", [P, NC_])
        ring = sb("ring", [P, NSLOT, SLOT])
        g.ring, g.parts = Ring(ring), 0
        g.ring.renew(slot_sems(g))
        g.gate_b = sb("gate_b", [P, 2, D])
        g.scale = sb("scale", [P, 2, KD])
        g.shift = sb("shift", [P, 2, KD])
        g.cond = sb("cond", [P, KD])
        phase_ada_head(g)
        with ExitStack() as mixer:
            mb = lambda n, sh, dt=F32: mixer.enter_context(nc.sbuf_tensor(n, sh, dt))
            yT = mb("yT0", [P, KD, T])
            proj = mb("proj", [P, NT, EVEN_IN])
            m = Stage()
            m.trig, m.trig_k = (yT[:, j, :].rearrange("p (a t d) -> p a t d", a=2, t=NT) for j in (KD - 2, KD - 1))
            with ExitStack() as inp:
                hT = inp.enter_context(nc.sbuf_tensor("hT0", [P, KD, T], F32))
                early = [g.ring.take(None) for _ in range(3)]
                phase_norm(g, "mix0", 0, g.dram["x"], 0, hT, ahead=early)
                phase_even_in(g, hT, proj, early, m)
            m.ret_gain = mb("ret_gain", [P, RH * P])
            m.q_gain = mb("q_gain", [P, 1])
            m.k_gain = mb("k_gain", [P, 1])
            m.pos_row_i = mb("pos_row_i", [P, T], I32)
            m.pos_row = mb("pos_row", [P, T])
            m.pos_quad_i = mb("pos_quad_i", [4, P], I32)
            m.pos_edge = mb("pos_edge", [P, P])
            m.rel = mb("rel", [P, 2, AH])
            m.delta3 = mb("delta3", [P, 3, 4 * AH], BF16)
            m.expand = mb("expand", [P, P * AH], BF16)
            m.mask = mb("mask", [P, NT, T], BF16)
            m.wi = mb("wi", [P, NT, IH])
            m.kaT = mb("kaT", [DH, T])
            m.qaT = mb("qaT", [DH, T, AH])
            with ExitStack() as head:
                hb = lambda n, sh, dt=F32: head.enter_context(nc.sbuf_tensor(n, sh, dt))
                m.qiT, m.kiT, m.ki4 = hb("qiT", [P, 2, T]), hb("kiT", [P, T]), hb("ki4", [P, NT, P])
                m.kz = hb("kz", [P, NT, RH * P])
                phase_even_prep(g, proj, m)
                m.qT, m.kT, m.qxT = hb("qT", [P, RH, T]), hb("kT", [P, RH, T]), hb("qxT", [P, RH, T])
                phase_even_turn(g, proj, m)
                phase_retention(g, proj, m, yT)
                phase_index(g, m)
            early, w_out = [g.ring.take(None) for _ in range(4)], g.dram["even_w_out"].rearrange("(j p) n -> p j n", p=P)
            phase_attention(g, proj, m, yT, early, w_out)
            phase_out(g, "mix0", yT, w_out, KD, g.dram["x"], g.dram["x1"], early)
        recycle(g)
        ffn(g, "ffn0", 0, g.dram["x1"], g.dram["x2"])
        ssd_layer(g)
        recycle(g)
        ffn(g, "ffn1", 1, g.dram["x3"], g.dram["out"])


_INS = ["x", "c", "positions", "ada_w", "ada_b", "norm_mix_g", "norm_ffn_g", "rel_bias", "even_w_in", "ret_norm_g",
        "dsa_q_g", "dsa_k_g", "even_w_out", "ssm_w_in", "ssm_conv_w", "ssm_conv_b", "ssm_dt_bias", "ssm_a_log",
        "ssm_d", "ssm_norm_g", "ssm_w_out", "router_w", "router_b", "exp_w1", "exp_w3", "exp_w2", "sh_w1", "sh_w3",
        "sh_w2"]
_FLAT = {"x", "positions", "even_w_in", "ret_norm_g", "dsa_q_g", "dsa_k_g", "even_w_out", "ssm_w_in", "ssm_conv_w",
         "ssm_conv_b", "ssm_dt_bias", "ssm_a_log", "ssm_d", "ssm_norm_g", "ssm_w_out"}


def kernel(**inputs):
    import concourse.bacc as bacc
    from concourse.bass_utils import run_bass_kernel_spmd

    nc = bacc.Bacc("TRN2", target_bir_lowering=False, num_devices=1)
    table, where = constants()
    arrays, aps = {"consts_dram": table}, {}
    for name in _INS:
        v = np.ascontiguousarray(inputs[name])
        arrays[f"{name}_dram"] = v.reshape(v.shape[1:]) if name in _FLAT else v
    for name, v in arrays.items():
        ap = nc.dram_tensor(name, v.shape, mybir.dt.from_np(v.dtype), kind="ExternalInput").ap()
        aps["consts_in" if name == "consts_dram" else name[:-5]] = ap
    aps["out"] = nc.dram_tensor("out_dram", (T + P, D), F32, kind="ExternalOutput").ap()
    for name, rows in (("x1", T), ("x2", T + P), ("x3", T), ("rows", T + P)):
        aps[name] = nc.dram_tensor(f"{name}_scratch", (rows, D), F32).ap()
    aps["mod"] = nc.dram_tensor("mod_scratch", (2, 6 * D), F32).ap()
    with nc.allow_non_contiguous_dma(reason="positions and gains, a few KiB, turned while they are loaded"):
        build(nc, aps, where)
    r = run_bass_kernel_spmd(nc, [arrays], core_ids=[0])
    return r.results[0]["out_dram"][:T].reshape(1, T, D)
```
